# Optimizing a Trainium2 kernel written in Bass

```python
import jax, jax.numpy as jnp
from jax import lax
import numpy as np

D_MODEL = 1024
BATCH = 1
SEQ = 256
DEPTH = 2

GRID_W = 64
CTX_LEN = 256
HEAD_DIM = 64
N_Q_HEADS = 8
N_KV_HEADS = 2
Q_PER_KV = N_Q_HEADS // N_KV_HEADS
ATT_WIDTH = N_Q_HEADS * HEAD_DIM
KV_WIDTH = N_KV_HEADS * HEAD_DIM
WINDOW = 128
BLOCK = 128
POOL_WINDOWS = (2, 4, 8, 16)
N_POOL_GROUPS = 4
POOL_WIDTH = D_MODEL // 2
POOL_GROUP = POOL_WIDTH // N_POOL_GROUPS
N_BRANCHES = 2
IN_WIDTH = ATT_WIDTH + 2 * KV_WIDTH + POOL_WIDTH + N_BRANCHES * D_MODEL
N_MOD = 6
D_FF = 2816
N_EXPERTS = 8
TOP_K = 2
D_FF_EXPERT = 3584
ROPE_BASE = 10000.0
EPS = 1e-6
N_DENSE = (DEPTH + 1) // 2
N_MOE = DEPTH // 2
NEG_INF = -1e30

kernel_name = "hybrid_gated_swa_pool_moe_dit"

def rms_norm(x, g):
    xf = x.astype(jnp.float32)
    y = xf * lax.rsqrt(jnp.mean(xf * xf, axis=-1, keepdims=True) + EPS)
    return (y * g.astype(jnp.float32)).astype(x.dtype)

def modulate(h, shift, scale):
    return h * (1 + scale) + shift

def rope_axis(x, pos):
    half = x.shape[-1] // 2
    freqs = ROPE_BASE ** (-jnp.arange(half, dtype=jnp.float32) / half)
    ang = pos.astype(jnp.float32)[:, None] * freqs[None, :]
    cos = jnp.cos(ang)[None, :, None, :].astype(x.dtype)
    sin = jnp.sin(ang)[None, :, None, :].astype(x.dtype)
    x1, x2 = x[..., :half], x[..., half:]
    return jnp.concatenate([x1 * cos - x2 * sin, x2 * cos + x1 * sin], axis=-1)

def rope_2d(x, row, col):
    r = HEAD_DIM // 2
    return jnp.concatenate([rope_axis(x[..., :r], row), rope_axis(x[..., r:], col)], axis=-1)

def sink_softmax(scores, sinks):
    sink = sinks.astype(jnp.float32).reshape(1, N_KV_HEADS, Q_PER_KV, 1, 1)
    lead = scores.ndim - 4
    sink = sink.reshape((1,) * (lead - 1) + sink.shape)
    sink = jnp.broadcast_to(sink, scores.shape[:-1] + (1,))
    p = jax.nn.softmax(jnp.concatenate([scores, sink], axis=-1), axis=-1)
    return p[..., :-1]

def split_proj(u):
    o1 = ATT_WIDTH
    o2 = o1 + KV_WIDTH
    o3 = o2 + KV_WIDTH
    o4 = o3 + POOL_WIDTH
    return u[..., :o1], u[..., o1:o2], u[..., o2:o3], u[..., o3:o4], u[..., o4:]

def context_attention(qc, kc, vc, sinks):
    scale = HEAD_DIM ** -0.5
    s = jnp.einsum('bqhgd,bkhd->bhgqk', qc, kc).astype(jnp.float32) * scale
    p = sink_softmax(s, sinks).astype(vc.dtype)
    o = jnp.einsum('bhgqk,bkhd->bqhgd', p, vc)
    return o.reshape(o.shape[0], o.shape[1], ATT_WIDTH)

def latent_attention(q, k, v, kc, vc, sinks):
    B, L = q.shape[0], q.shape[1]
    nb = L // BLOCK
    scale = HEAD_DIM ** -0.5
    qb = q.reshape(B, nb, BLOCK, N_KV_HEADS, Q_PER_KV, HEAD_DIM)
    pad = ((0, 0), (BLOCK, BLOCK), (0, 0), (0, 0))
    kp = jnp.pad(k, pad).reshape(B, nb + 2, BLOCK, N_KV_HEADS, HEAD_DIM)
    vp = jnp.pad(v, pad).reshape(B, nb + 2, BLOCK, N_KV_HEADS, HEAD_DIM)
    k_win = jnp.concatenate([kp[:, :-2], kp[:, 1:-1], kp[:, 2:]], axis=2)
    v_win = jnp.concatenate([vp[:, :-2], vp[:, 1:-1], vp[:, 2:]], axis=2)
    blk = jnp.arange(nb)
    qpos = blk[:, None] * BLOCK + jnp.arange(BLOCK)[None, :]
    kpos = blk[:, None] * BLOCK - BLOCK + jnp.arange(3 * BLOCK)[None, :]
    valid = ((jnp.abs(qpos[:, :, None] - kpos[:, None, :]) <= WINDOW)
             & (kpos >= 0)[:, None, :] & (kpos < L)[:, None, :])

    def block_fn(args):
        qi, ki, vi, mi = args
        s_loc = jnp.einsum('bqhgd,bkhd->bhgqk', qi, ki).astype(jnp.float32) * scale
        s_loc = jnp.where(mi[None, None, None], s_loc, NEG_INF)
        s_ctx = jnp.einsum('bqhgd,bkhd->bhgqk', qi, kc).astype(jnp.float32) * scale
        p = sink_softmax(jnp.concatenate([s_loc, s_ctx], axis=-1), sinks).astype(vi.dtype)
        return (jnp.einsum('bhgqk,bkhd->bqhgd', p[..., :3 * BLOCK], vi)
                + jnp.einsum('bhgqk,bkhd->bqhgd', p[..., 3 * BLOCK:], vc))

    o = lax.map(block_fn, (jnp.moveaxis(qb, 1, 0), jnp.moveaxis(k_win, 1, 0),
                           jnp.moveaxis(v_win, 1, 0), valid))
    return jnp.moveaxis(o, 0, 1).reshape(B, L, ATT_WIDTH)

def multiscale_pool(p, w_grp, pool_scale):
    B, L, _ = p.shape
    pf = p.astype(jnp.float32)
    cs = jnp.concatenate([jnp.zeros((B, 1, POOL_WIDTH), jnp.float32), jnp.cumsum(pf, axis=1)], axis=1)
    t = jnp.arange(L)
    means = []
    for gi, w in enumerate(POOL_WINDOWS):
        lo = jnp.clip(t - w // 2, 0, L)
        hi = jnp.clip(t + w // 2, 0, L)
        csg = cs[..., gi * POOL_GROUP:(gi + 1) * POOL_GROUP]
        sums = jnp.take(csg, hi, axis=1) - jnp.take(csg, lo, axis=1)
        means.append(sums / (hi - lo).astype(jnp.float32)[None, :, None])
    pooled = (jnp.concatenate(means, axis=-1) - pf).astype(p.dtype)
    pooled = pooled.reshape(B, L, N_POOL_GROUPS, POOL_GROUP)
    mixed = jnp.einsum('blgc,gcd->blgd', pooled, w_grp).reshape(B, L, POOL_WIDTH)
    return mixed * pool_scale

def merge_branches(att, pool, gate_logits, w_att_o, w_pool_o, w_out):
    g = jax.nn.sigmoid(gate_logits).reshape(gate_logits.shape[:-1] + (N_BRANCHES, D_MODEL))
    merged = g[..., 0, :] * (att @ w_att_o) + g[..., 1, :] * (pool @ w_pool_o)
    return merged @ w_out

def swiglu(h, wg, wu, wd):
    return (jax.nn.silu(h @ wg) * (h @ wu)) @ wd

def moe_ffn(h, w_router, b_router, wg, wu, wd):
    logits = (h @ w_router).astype(jnp.float32) + b_router.astype(jnp.float32)
    top_val, top_idx = lax.top_k(logits, TOP_K)
    top_w = jax.nn.softmax(top_val, axis=-1)
    combine = jnp.sum(jax.nn.one_hot(top_idx, N_EXPERTS, dtype=jnp.float32) * top_w[..., None], axis=-2)
    combine = combine.astype(h.dtype)
    out = jnp.zeros_like(h)
    for e in range(N_EXPERTS):
        out = out + combine[..., e:e + 1] * swiglu(h, wg[e], wu[e], wd[e])
    return out

def setup_inputs(seed: int = 0) -> dict:
    key = jax.random.key(seed)
    ks = jax.random.split(key, 24)
    f32 = jnp.float32
    n = lambda k, shape, s: jax.random.normal(k, shape, f32) * s
    D = D_MODEL
    return {
        "x": n(ks[0], (BATCH, SEQ, D), 1.0),
        "c": n(ks[1], (BATCH, D), 1.0),
        "ctx": n(ks[2], (BATCH, CTX_LEN, D), 1.0),
        "c_ctx": n(ks[3], (D,), 1.0),
        "w_mod": n(ks[4], (DEPTH, D, N_MOD * D), 0.5 * D ** -0.5),
        "b_mod": n(ks[5], (DEPTH, N_MOD * D), 0.02),
        "norm_g": 1.0 + n(ks[6], (DEPTH, 4, D), 0.02),
        "w_in": n(ks[7], (DEPTH, D, IN_WIDTH), D ** -0.5),
        "sinks": n(ks[8], (DEPTH, N_Q_HEADS), 0.5),
        "w_att_o": n(ks[9], (DEPTH, ATT_WIDTH, D), ATT_WIDTH ** -0.5),
        "pool_w": n(ks[10], (DEPTH, N_POOL_GROUPS, POOL_GROUP, POOL_GROUP), POOL_GROUP ** -0.5),
        "pool_scale": 1.0 + n(ks[11], (DEPTH, POOL_WIDTH), 0.1),
        "w_pool_o": n(ks[12], (DEPTH, POOL_WIDTH, D), POOL_WIDTH ** -0.5),
        "w_out": n(ks[13], (DEPTH, D, D), D ** -0.5),
        "w_ffn_gate": n(ks[14], (N_DENSE, D, D_FF), D ** -0.5),
        "w_ffn_up": n(ks[15], (N_DENSE, D, D_FF), D ** -0.5),
        "w_ffn_down": n(ks[16], (N_DENSE, D_FF, D), D_FF ** -0.5),
        "w_router": n(ks[17], (N_MOE, D, N_EXPERTS), D ** -0.5),
        "b_router": n(ks[18], (N_MOE, N_EXPERTS), 0.01),
        "w_exp_gate": n(ks[19], (N_MOE, N_EXPERTS, D, D_FF_EXPERT), D ** -0.5),
        "w_exp_up": n(ks[20], (N_MOE, N_EXPERTS, D, D_FF_EXPERT), D ** -0.5),
        "w_exp_down": n(ks[21], (N_MOE, N_EXPERTS, D_FF_EXPERT, D), D_FF_EXPERT ** -0.5),
    }

def reference(x, c, ctx, c_ctx, w_mod, b_mod, norm_g, w_in, sinks, w_att_o, pool_w, pool_scale,
              w_pool_o, w_out, w_ffn_gate, w_ffn_up, w_ffn_down, w_router, b_router,
              w_exp_gate, w_exp_up, w_exp_down):
    B, L, _ = x.shape
    C = ctx.shape[1]
    rows = L // GRID_W
    row = jnp.repeat(jnp.arange(rows), GRID_W)
    col = jnp.tile(jnp.arange(GRID_W), rows)
    sc = jax.nn.silu(c)
    sc_ctx = jax.nn.silu(c_ctx)

    def ffn(h, l):
        if l % 2 == 0:
            i = l // 2
            return swiglu(h, w_ffn_gate[i], w_ffn_up[i], w_ffn_down[i])
        i = l // 2
        return moe_ffn(h, w_router[i], b_router[i], w_exp_gate[i], w_exp_up[i], w_exp_down[i])

    for l in range(DEPTH):
        last = l == DEPTH - 1
        mod_lat = (sc @ w_mod[l] + b_mod[l])[:, None, :]
        mod_ctx = sc_ctx @ w_mod[l] + b_mod[l]
        sa, ca, ga, sf, cf, gf = jnp.split(mod_lat, N_MOD, axis=-1)
        sa_c, ca_c, ga_c, sf_c, cf_c, gf_c = jnp.split(mod_ctx, N_MOD, axis=-1)

        h = modulate(rms_norm(x, norm_g[l, 0]), sa, ca)
        hc = modulate(rms_norm(ctx, norm_g[l, 0]), sa_c, ca_c)
        q, k, v, p, gl = split_proj(h @ w_in[l])
        qc, kc, vc, pc, glc = split_proj(hc @ w_in[l])
        q = rope_2d(q.reshape(B, L, N_Q_HEADS, HEAD_DIM), row, col)
        k = rope_2d(k.reshape(B, L, N_KV_HEADS, HEAD_DIM), row, col)
        q = q.reshape(B, L, N_KV_HEADS, Q_PER_KV, HEAD_DIM)
        v = v.reshape(B, L, N_KV_HEADS, HEAD_DIM)
        kc = kc.reshape(B, C, N_KV_HEADS, HEAD_DIM)
        vc = vc.reshape(B, C, N_KV_HEADS, HEAD_DIM)
        att = latent_attention(q, k, v, kc, vc, sinks[l])
        pool = multiscale_pool(p, pool_w[l], pool_scale[l])
        y = merge_branches(att, pool, gl, w_att_o[l], w_pool_o[l], w_out[l])
        x = x + ga * rms_norm(y, norm_g[l, 1])

        hf = modulate(rms_norm(x, norm_g[l, 2]), sf, cf)
        x = x + gf * rms_norm(ffn(hf, l), norm_g[l, 3])

        if not last:
            qc = qc.reshape(B, C, N_KV_HEADS, Q_PER_KV, HEAD_DIM)
            att_c = context_attention(qc, kc, vc, sinks[l])
            pool_c = multiscale_pool(pc, pool_w[l], pool_scale[l])
            yc = merge_branches(att_c, pool_c, glc, w_att_o[l], w_pool_o[l], w_out[l])
            ctx = ctx + ga_c * rms_norm(yc, norm_g[l, 1])
            hfc = modulate(rms_norm(ctx, norm_g[l, 2]), sf_c, cf_c)
            ctx = ctx + gf_c * rms_norm(ffn(hfc, l), norm_g[l, 3])
    return x


_drawn_inputs = setup_inputs


def setup_inputs(seed=0):
    import zlib

    import numpy as np

    out = dict(_drawn_inputs(seed))
    spreads = {}
    factors = {'sinks': 8.0, 'b_router': 2.994}
    for name, (base, spread) in spreads.items():
        noise = np.random.default_rng([zlib.crc32(name.encode()), seed]).standard_normal(out[name].shape)
        drawn = base * np.exp(spread * noise) if base else spread * noise
        out[name] = __import__('jax').numpy.asarray(drawn.astype(out[name].dtype))
    for name, factor in factors.items():
        out[name] = (out[name] * factor).astype(out[name].dtype)
    return out
```

```python
from contextlib import ExitStack

import numpy as np
import concourse.bass as bass
from concourse import mybir

F32 = mybir.dt.float32
F32R = mybir.dt.float32r
I32 = mybir.dt.int32
BF16 = mybir.dt.bfloat16
ALU = mybir.AluOpType
ACT = mybir.ActivationFunctionType
AX_X = mybir.AxisListType.X

P = 128
D = 1024
KT = D // P
L = 256
LB = L // P
DEPTH = 2
HD, NH, NKV = 64, 8, 2
QC = NH // NKV
ATT = NH * HD
GRID_W, ROPE_BASE, WINDOW = 64, 10000.0, 128
POOL_WINDOWS = (2, 4, 8, 16)
NG = len(POOL_WINDOWS)
N_MOD = 6
MCH = N_MOD * D // 512
MT = N_MOD * KT
D_FF, D_EXP, NE = 2816, 3584, 8
EPS, NEG = 1e-6, -1e30
FFULL = D_FF // 512
FREM = D_FF - FFULL * 512
XS = D_EXP // 512
XU = 6 * XS
KVC, PC, GC = ATT, ATT + 2 * NKV * HD, ATT + 2 * NKV * HD + 512
(LG, T1, T2, RK, RK2, F1, F2, SEL, M8, DIF, EXD, DNR, W1, W2, CW, POS, POSM, CNT, FLAG, CURG, CURS, CURW) = np.cumsum(
    [0, 16, 128, 128, 16, 16, 16, 16, 16, 16, 2, 2, 2, 2, 2, 16, 16, 16, 8, 2, 2, 2]).tolist()

V_G, V_PS, V_BM = 2 * KT, 2 * KT + DEPTH * 4 * KT, 2 * KT + DEPTH * 4 * KT + DEPTH * NG
V_ALL = V_BM + DEPTH * MT
K_ID, K_TRI, K_IO, K_JLT, K_COS, K_SIN, K_MASK = 0, 128, 256, 384, 448, 576, 704
K_ALL = K_MASK + LB * L


def constants():
    k = np.zeros((P, K_ALL), np.float32)
    k[:, K_ID:K_ID + P] = np.eye(P)
    k[:, K_TRI:K_TRI + P] = np.triu(np.ones((P, P)), 1)
    k[:, K_IO:K_IO + P] = np.arange(P)[None]
    k[:, K_JLT:K_JLT + NE * NE] = (np.arange(NE)[None, :] < np.arange(NE)[:, None]).astype(np.float32).reshape(1, -1)
    half = HD // 4
    freqs = (ROPE_BASE ** (-np.arange(half, dtype=np.float32) / half)).astype(np.float32)
    t = np.arange(L)
    for b in range(LB):
        pos = t[b * P:(b + 1) * P]
        for axis, at in enumerate((pos // GRID_W, pos % GRID_W)):
            ang = at.astype(np.float32)[:, None] * freqs[None]
            c0 = K_COS + b * HD + axis * 2 * half
            s0 = K_SIN + b * HD + axis * 2 * half
            k[:, c0:c0 + 2 * half] = np.tile(np.cos(ang), 2)
            k[:, s0:s0 + 2 * half] = np.concatenate([-np.sin(ang), np.sin(ang)], 1)
        far = np.abs(pos[:, None] - t[None, :]) > WINDOW
        k[:, K_MASK + b * L:K_MASK + (b + 1) * L] = np.where(far, NEG, 0.0)
    pool = np.zeros((P, LB, NG, L), np.float32)
    for g, w in enumerate(POOL_WINDOWS):
        lo, hi = np.clip(t - w // 2, 0, L), np.clip(t + w // 2, 0, L)
        m = ((t[:, None] >= lo[None]) & (t[:, None] < hi[None])) / (hi - lo)[None] - np.eye(L)
        pool[:, :, g, :] = m.reshape(LB, P, L).transpose(1, 0, 2)
    return k, pool.reshape(P, -1)


def weight_plan(w):
    plan = []

    def piece(name, src, rows, width, groups):
        plan.append((name, src.rearrange("(j p) n -> p j n", p=P), rows, width, groups))

    def pair(name, m, c, groups):
        for k0 in (0, 4):
            piece(name, m[k0 * P:(k0 + 4) * P, c:c + 512], 4, 512, groups)

    for l in range(DEPTH):
        nb = 2 * LB if l + 1 < DEPTH else LB
        wi = w["w_in"][l]

        def mod(m):
            pair(f"m{m}.{l}", w["w_mod"][l], m * 512, 1)

        for m in range(4):
            mod(m)
        pair(f"q.{l}", wi, 0, nb)
        mod(4)
        piece(f"kv.{l}", wi[:, KVC:PC], 8, 256, 2 * LB)
        mod(5)
        pair(f"p.{l}", wi, PC, nb)
        pair(f"g0n0.{l}", wi, GC, nb)
        pair(f"g0n1.{l}", wi, GC + 512, nb)
        for n in range(2):
            piece(f"ao{n}.{l}", w["w_att_o"][l][:, n * 512:(n + 1) * 512], 4, 512, nb)
        mod(6)
        mod(7)
        for n in range(2):
            pair(f"g1n{n}.{l}", wi, GC + D + n * 512, nb)
            mod(8 + n)
            piece(f"po{n}.{l}", w["w_pool_o"][l][:, n * 512:(n + 1) * 512], 4, 512, nb)
        mod(10)
        mod(11)
        for n in range(2):
            pair(f"o{n}.{l}", w["w_out"][l], n * 512, nb)
        if l == 0:
            for f in range(FFULL):
                c = f * 512
                pair(f"fg{f}", w["w_ffn_gate"][0], c, nb)
                pair(f"fu{f}", w["w_ffn_up"][0], c, nb)
                for n in range(2):
                    piece(f"fd{f}.{n}", w["w_ffn_down"][0][c:c + 512, n * 512:(n + 1) * 512], 4, 512, nb)
            c = FFULL * 512
            piece("fgr", w["w_ffn_gate"][0][:, c:], 8, FREM, nb)
            piece("fur", w["w_ffn_up"][0][:, c:], 8, FREM, nb)
            piece("fdr", w["w_ffn_down"][0][c:, :], 2, D, 2 * nb)
    return plan


def backbone(nc, x, c, ctx, c_ctx, w_mod, b_mod, norm_g, w_in, sinks, w_att_o, pool_w, pool_scale,
             w_pool_o, w_out, w_ffn_gate, w_ffn_up, w_ffn_down, w_router, b_router,
             w_exp_gate, w_exp_up, w_exp_down, k_const, k_pool, out):
    plan = weight_plan(dict(w_mod=w_mod, w_in=w_in, w_att_o=w_att_o, w_pool_o=w_pool_o, w_out=w_out,
                            w_ffn_gate=w_ffn_gate, w_ffn_up=w_ffn_up, w_ffn_down=w_ffn_down))
    NU = len(plan)
    assert NU % 3 == 0
    first = {}
    before = [0]
    for n, (name, _, _, _, groups) in enumerate(plan):
        first.setdefault(name, n)
        before.append(before[-1] + groups)
    GM = before[NU]
    FN = first["fg0"]

    es = ExitStack()
    with es:
        def sb(name, shape, dt=F32):
            return es.enter_context(nc.sbuf_tensor(name, shape, dt))

        raw = [sb(f"raw{i}", [P, 2048]) for i in range(3)]
        whi = [sb(f"whi{i}", [P, 2048], F32R) for i in range(3)]
        wlo = [sb(f"wlo{i}", [P, 2048], F32R) for i in range(3)]
        X = sb("X", [P, 2 * LB, D])
        K = sb("K", [P, K_ALL])
        ones = sb("ones", [P, P])
        VT = sb("VT", [P, V_ALL])
        csil = sb("csil", [P, 2 * KT])
        cst = sb("cst", [P, KT, 4], F32R)
        csz = sb("csz", [P, KT, 4], F32R)
        modT = sb("modT", [P, MT, 2])
        sel4 = sb("sel4", [4, 2])
        SC = [sb(f"SC{i}", [P, KT, 2]) for i in range(2)]
        GG = [sb(f"GG{i}", [P, KT, 2]) for i in range(2)]
        ssq = sb("ssq", [P, 4])
        sdev = sb("sdev", [P, 4])
        rstd = sb("rstd", [P, 4])
        epst = sb("epst", [P, 1])
        identb = sb("identb", [P, P], BF16)
        maskb = sb("maskb", [P, LB * L], BF16)
        sinkB = sb("sinkB", [P, DEPTH * NH])
        nsink = sb("nsink", [P, DEPTH * NH])
        brB = sb("brB", [P, NE])
        negmax0 = sb("negmax0", [P, 2])
        negmax = sb("negmax", [P, 2])
        psumP = sb("psumP", [P, 2])
        esink = sb("esink", [P, 2])
        den = sb("den", [P, 2])
        rden = sb("rden", [P, 2])

        arena_kb = 106
        base = -(-nc.sbuf_base // 32) * 32
        arena = sb("arena", [P, arena_kb * 256])

        def at(name, kb, shape, dt=F32):
            return nc.alloc_sbuf_tensor_at(name, shape, dt, offset=base + int(kb * 1024))

        hTh = at("hTh", 0, [P, KT, 512], F32R)
        hTl = at("hTl", 16, [P, KT, 512], F32R)
        A = at("A", 32, [P, 2 * LB, D])
        rope1 = at("rope1", 32, [P, 512])
        rope2 = at("rope2", 34, [P, 512])
        qrot = at("qrot", 36, [P, 2 * LB, 512])
        krot = at("krot", 44, [P, 2 * LB, P])
        r1 = 48
        pin = at("pin", r1, [P, 2 * LB, 512])
        qT = at("qT", r1 + 8, [P, QC, 512])
        diag = at("diag", r1 + 8, [P, 2, KT, P])
        brh = at("brh", r1 + 16, [P, 4, 512], F32R)
        brl = at("brl", r1 + 24, [P, 4, 512], F32R)
        poolM = at("poolM", r1 + 32, [P, LB, NG, L])
        kT = at("kT", r1 + 40, [P, 512])
        V = at("V", r1 + 42, [P, 2 * LB, P])
        Pb = at("Pb", r1 + 45, [P, 2, 512])
        modrow = at("modrow", r1 + 45, [4, 2, 512])
        hmod = at("hmod", r1 + 45, [P, 2, 512])
        PT = at("PT", r1 + 49, [P, 2, 4, P])
        junk = at("junk", r1 + 49, [P, D])
        pooledT = at("pooledT", r1 + 53, [P, 512])
        att = at("att", r1 + 53, [P, ATT])
        poolW = at("poolW", r1 + 55, [P, NG, P])
        vst = at("vst", r1 + 16, [P, 2, P])
        sg = at("sg", r1, [P, 2 * LB, 512])
        h2h = at("h2h", r1 + 16, [P, 2 * LB, 4, P], F32R)
        h2l = at("h2l", r1 + 24, [P, 2 * LB, 4, P], F32R)
        rawm = raw + [at(f"raw{3 + i}", r1 + 16 + 8 * i, [P, 2048]) for i in range(3)]
        wr = at("wr", r1 + 57, [P, KT, NE])
        wrh = at("wrh", r1 + 44, [P, KT, NE], F32R)
        wrl = at("wrl", r1 + 44.25, [P, KT, NE], F32R)
        xn = A[:, 0:LB, :]
        yacc = A[:, LB:2 * LB, :]
        xgm = at("xgm", 0, [P, KT, P])
        xgh = at("xgh", r1, [P, KT, P], F32R)
        xgl = at("xgl", r1 + 4, [P, KT, P], F32R)
        yslot = at("yslot", r1 + 40, [P, D])
        sgm = at("sgm", 4, [P, 512])
        h2hm = at("h2hm", 8, [P, 4, P], F32R)
        h2lm = at("h2lm", 10, [P, 4, P], F32R)
        Gat = at("Gat", 12, [P, LB, P])
        Gsc = at("Gsc", 13, [P, LB, P])
        Sct = at("Sct", 14, [P, LB * P])
        route = at("route", r1 + 53, [P, 1024])

        bank = [es.enter_context(nc.psum_tensor(f"bank{i}", [P, 512], F32)) for i in range(8)]

        def sem(name):
            return es.enter_context(nc.semaphore(name))

        s_small = sem("small_in")
        s_const = sem("const_in")
        s_x = sem("x_in")
        s_poolw = sem("poolw_in")
        s_route_in = sem("router_in")
        s_raw = [sem(f"raw_full{i}") for i in range(6)]
        s_hi = sem("hi_done")
        s_lo = sem("lo_done")
        s_mm = sem("mm_done")
        s_ini = sem("ini")
        s_vt = sem("vt")
        s_vtc = sem("vt_copied")
        s_csil = sem("csil")
        s_csh = sem("csh")
        s_cs = sem("cs_ready")
        s_mrow = sem("modrow_ready")
        s_mt = sem("modT_psum")
        s_md = sem("modT_ready")
        s_col = sem("columns_ready")
        s_sq = sem("squares")
        s_sd = sem("sdev_ready")
        s_rs = sem("rstd_ready")
        s_xn = sem("xn_ready")
        s_tr = sem("xn_transposed")
        s_hm = sem("hmod_ready")
        s_hh = sem("h_high")
        s_h = sem("h_ready")
        s_r = sem("rope_steps")
        s_qr = sem("q_rotated")
        s_qt = sem("q_transposed")
        s_qk = sem("qT_copied")
        s_kr = sem("k_rotated")
        s_kt = sem("k_transposed")
        s_v = sem("v_copied")
        s_pin = sem("pool_in_copied")
        s_g0 = sem("gate0_copied")
        s_g0s = sem("gate0_sigmoid")
        s_s = sem("scores_ready")
        s_nm0 = sem("rowmax")
        s_nm = sem("negmax_ready")
        s_e = sem("exp_ready")
        s_es = sem("sink_exp")
        s_dn = sem("den_steps")
        s_pt = sem("probs_transposed")
        s_ptc = sem("probsT_copied")
        s_pv = sem("att_ready")
        s_oc = sem("att_scaled")
        s_at = sem("att_transposed")
        s_ah = sem("att_high")
        s_al = sem("att_low")
        s_ao = sem("att_gated")
        s_pl = sem("pooled")
        s_plc = sem("pooled_copied")
        s_mx = sem("pool_mixed")
        s_mxh = sem("pool_high")
        s_mxl = sem("pool_low")
        s_g1 = sem("gate1_sigmoid")
        s_po = sem("pool_gated")
        s_mg = sem("merged")
        s_mgt = sem("merged_transposed")
        s_mgh = sem("merged_high")
        s_mgl = sem("merged_low")
        s_y = sem("y_copied")
        s_dg = sem("diag_ready")
        s_gb = sem("gain_rows")
        s_ys = sem("y_scaled")
        s_xu = sem("x_updated")
        s_si = sem("silu_ready")
        s_hid = sem("hidden_ready")
        s_ht = sem("hidden_transposed")
        s_h2h = sem("hidden_high")
        s_h2l = sem("hidden_low")
        s_da = sem("down_added")
        s_wr = sem("router_high")
        s_wrl = sem("router_low")
        s_lg = sem("logits_psum")
        s_rt = sem("router_steps")
        s_rx = sem("router_exp")
        s_cnt = sem("counts_psum")
        s_flag = sem("flag_ready")
        s_gat = sem("gather_matrix")
        s_gsc = sem("scatter_weights")
        s_gst = sem("scatter_transposed")
        s_gsc2 = sem("scatter_copied")
        s_cur = sem("expert_columns")
        s_xg = sem("gathered")
        s_xgm = sem("gathered_modulated")
        s_xgh = sem("gathered_high")
        s_xgl = sem("gathered_low")
        s_ysl = sem("yslot_copied")
        s_sc = sem("scattered")
        s_sca = sem("scatter_added")
        s_moe = sem("experts_done")
        s_out = sem("out_stored")

        block = es.enter_context(nc.Block())

        ident = K[:, K_ID:K_ID + P]

        hm_at = [0, 16, 32, 48]
        col_of = [1, 3, 5, 7]
        gb_at = {1: 0, 3: 2, 5: 4, 7: 5}
        R_SEL = 17
        R_DIF = 4
        H0 = 4 * (FFULL + 1)

        def blocks(l):
            return 2 * LB if l + 1 < DEPTH else LB

        def units_of(l):
            return [(s, b, h) for s in range(blocks(l) // LB) for b in range(LB) for h in range(NH)]

        att0 = [0, len(units_of(0))]
        qb0 = [0, 2 * LB]
        norm_nb = [4, 4, 4, 4, 4, 2, 2, 2]
        norm_at = [sum(norm_nb[:i]) for i in range(9)]
        xu_at = [0, 0, 4, 4, 8, 8, 10, 10]
        xn_at = [0, 0, 4, 4, 8, 8, 12, 12]

        @block.sync
        def _(sp):
            sp.dma_start(X[:, 0:LB, :], x[0].rearrange("(b p) d -> p b d", p=P)).then_inc(s_x, 16)
            sp.dma_start(X[:, LB:2 * LB, :], ctx[0].rearrange("(b p) d -> p b d", p=P)).then_inc(s_x, 16)
            n = 0
            while n < NU:
                if n == FN:
                    with sp.Fori(0, FFULL) as f:
                        for j in range(6):
                            m = w_ffn_gate[0] if j < 2 else w_ffn_up[0] if j < 4 else w_ffn_down[0]
                            if j < 4:
                                src = m[(j % 2) * 512:(j % 2) * 512 + 512, bass.ds(f * 512, 512)]
                            else:
                                src = m[bass.ds(f * 512, 512), (j % 2) * 512:(j % 2) * 512 + 512]
                            sp.wait_ge(s_lo, FN + j - 2 + f * 6)
                            sp.dma_start(raw[(FN + j) % 3][:, :].rearrange("p (j n) -> p j n", j=4),
                                         src.rearrange("(j p) n -> p j n", p=P)).then_inc(s_raw[(FN + j) % 3], 16)
                    n += 6 * FFULL
                    continue
                _, src, rows, width, _ = plan[n]
                if n >= 3:
                    sp.wait_ge(s_lo, n - 2)
                sp.dma_start(raw[n % 3][:, 0:rows * width].rearrange("p (j n) -> p j n", j=rows),
                             src).then_inc(s_raw[n % 3], 16)
                n += 1

            def expert_loads(b, e):
                i0 = XU * NE * b + XU * e

                def go(i, slot, kind, src, cold):
                    if not cold:
                        sp.wait_ge(s_lo, NU - 5 + i)
                    sp.dma_start(rawm[slot][:, :].rearrange("p (j n) -> p j n", j=4),
                                 src.rearrange("(j p) n -> p j n", p=P)).then_inc(s_raw[slot], 16)

                def up(kind, f):
                    m = (w_exp_gate if kind < 2 else w_exp_up)[0].rearrange("e d f -> (e d) f")
                    return m[bass.ds(e * D + (kind % 2) * 512, 512), bass.ds(f * 512, 512)]

                def down(h, f):
                    m = w_exp_down[0].rearrange("e f d -> (e f) d")
                    return m[bass.ds(e * D_EXP + f * 512, 512), h * 512:h * 512 + 512]

                for j in range(4):
                    if b == 0 and isinstance(e, int) and e == 0 and j < 3:
                        sp.wait_ge(s_lo, NU - 2 + j)
                        go(i0 + j, j, j, up(j, 0), True)
                    else:
                        go(i0 + j, j, j, up(j, 0), b == 0 and isinstance(e, int) and e == 0)
                with sp.Fori(1, XS) as f:
                    for j in range(6):
                        src = up(j, f) if j < 4 else down(j - 4, f - 1)
                        go(i0 + f * 6 + (j - 2), (4 + j) % 6, j, src, False)
                for j in range(2):
                    go(i0 + XU - 2 + j, 4 + j, 4 + j, down(j, XS - 1), False)

            sp.wait_ge(s_mm, before[first["po1.1"] + 1])
            expert_loads(0, 0)
            with sp.Fori(1, NE) as e:
                expert_loads(0, e)
            sp.wait_ge(s_flag, 1)
            with sp.If(sp.value_load(route[0:1, FLAG:FLAG + 1].bitcast(I32), min_val=0, max_val=1) > 0):
                with sp.Fori(0, NE) as e:
                    expert_loads(1, e)
            sp.wait_ge(s_xu, 2 * 2 * LB + LB + LB)
            sp.dma_start(out[0].rearrange("(b p) d -> p b d", p=P), X[:, 0:LB, :]).then_inc(s_out, 16)
            sp.wait_ge(s_out, 16)

        @block.gpsimd
        def _(pool):
            pool.dma_start(vst[0:KT, 0, :], c[0].rearrange("(k p) -> k p", p=P)).then_inc(s_small, 16)
            pool.dma_start(vst[KT:2 * KT, 0, :], c_ctx.rearrange("(k p) -> k p", p=P)).then_inc(s_small, 16)
            pool.dma_start(vst[V_G:V_PS, 0, :], norm_g.rearrange("l i (k p) -> (l i k) p", p=P)).then_inc(s_small, 16)
            pool.dma_start(vst[V_PS:V_BM, 0, :], pool_scale.rearrange("l (g p) -> (l g) p", p=P)).then_inc(s_small, 16)
            pool.dma_start(vst[0:V_ALL - V_BM, 1, :],
                           b_mod.rearrange("l (k p) -> (l k) p", p=P)).then_inc(s_small, 16)
            pool.dma_start(K[:, :], k_const).then_inc(s_const, 16)
            pool.dma_start(sinkB[:, :],
                           sinks.rearrange("(o l) h -> o (l h)", o=1).to_broadcast([P, DEPTH * NH])).then_inc(s_const, 16)
            pool.dma_start(brB[:, :], b_router.to_broadcast([P, NE])).then_inc(s_const, 16)
            pool.dma_start(poolM[:, :, :, :].rearrange("p b g t -> p (b g t)"), k_pool).then_inc(s_const, 16)
            pool.dma_start(wr[:, :, :], w_router[0].rearrange("(k p) e -> p k e", p=P)).then_inc(s_route_in, 16)
            for l in range(DEPTH):
                if l:
                    pool.wait_ge(s_mx, NG * l)
                pool.dma_start(poolW[:, :, :], pool_w[l].rearrange("g c d -> c g d")).then_inc(s_poolw, 16)

        @block.scalar
        def _(act):
            def split(n):
                act.wait_ge(s_raw[n % 3], 16 * (n // 3 + 1))
                if n >= 3:
                    act.wait_ge(s_mm, before[n - 2])
                w = plan[n][2] * plan[n][3]
                act.activation(whi[n % 3][:, 0:w], raw[n % 3][:, 0:w], ACT.Copy).then_inc(s_hi, 1)

            def ahead(n):
                if n + 2 < NU:
                    split(n + 2)

            def mod(l, m):
                n, M = first[f"m{m}.{l}"], MCH * l + m
                ahead(n)
                ahead(n + 1)
                act.wait_ge(s_mm, before[n + 2])
                if M >= 2:
                    act.wait_ge(s_mt, M - 1)
                act.activation(modrow[:, M % 2, :], bank[6][0:4, :], ACT.Copy).then_inc(s_mrow, 1)

            def squares(i, src):
                nb = norm_nb[i]
                for t in range(nb):
                    if i + t:
                        act.wait_ge(s_sq, norm_at[i] + t)
                    act.activation(junk[:, :], src(t), ACT.Square, accum_out=ssq[:, t:t + 1]).then_inc(s_sq, 1)
                act.wait_ge(s_sq, norm_at[i] + nb)
                if i:
                    act.wait_ge(s_rs, i)
                act.activation(sdev[:, 0:nb], ssq[:, 0:nb], ACT.Sqrt, bias=epst[:, 0:1], scale=1.0 / D).then_inc(s_sd, 1)

            def build(i, bi, streams):
                if i == 0:
                    act.wait_ge(s_x, 32)
                else:
                    act.wait_ge(s_xu, xu_at[i])
                squares(i, lambda t: X[:, t, :])
                for k in range(KT):
                    act.wait_ge(s_hm, hm_at[bi] + streams * (k + 1))
                    w = streams * L
                    act.activation(hTh[:, k, 0:w], hmod[:, k % 2, 0:w], ACT.Copy).then_inc(s_hh, 1)

            act.wait_ge(s_vtc, 1)
            act.activation(csil[:, :], VT[:, 0:2 * KT], ACT.Silu).then_inc(s_csil, 1)
            act.wait_ge(s_csil, 1)
            act.activation(cst[:, :, 0:2].rearrange("p k s -> p s k"),
                           csil[:, :].rearrange("p (s k) -> p s k", s=2), ACT.Copy).then_inc(s_csh, 1)
            act.wait_ge(s_ini, 3)
            split(0)
            split(1)
            for l in range(DEPTH):
                nb, streams = blocks(l), blocks(l) // LB
                for m in range(4):
                    mod(l, m)
                build(4 * l, 2 * l, 2)
                n = first[f"q.{l}"]
                ahead(n)
                ahead(n + 1)
                mod(l, 4)
                ahead(first[f"kv.{l}"])
                for t in range(nb):
                    act.wait_ge(s_qt, qb0[l] + t + 1)
                    act.activation(qT[:, :, t * P:(t + 1) * P],
                                   bank[4 + t % 2][:, :].rearrange("p (c t) -> p c t", c=QC), ACT.Copy).then_inc(s_qk, 1)
                mod(l, 5)
                act.wait_ge(s_kt, l + 1)
                act.activation(kT[:, :], bank[4][:, :], ACT.Copy).then_inc(s_qk, 1)
                n = first[f"p.{l}"]
                ahead(n)
                ahead(n + 1)
                for t in range(nb):
                    act.wait_ge(s_mm, before[n + 1] + t + 1)
                    act.activation(pin[:, t, :], bank[t][:, :], ACT.Copy).then_inc(s_pin, 1)

                units, a0 = units_of(l), att0[l]
                n0 = first[f"g0n0.{l}"]

                def probs_t(a):
                    act.wait_ge(s_pt, a0 + a + 1)
                    if a0 + a >= 2:
                        act.wait_ge(s_pv, a0 + a - 1)
                    act.activation(PT[:, a % 2, :, :].rearrange("p k t -> p (k t)"), bank[6][:, :],
                                   ACT.Copy).then_inc(s_ptc, 1)

                def att_high(j):
                    T = qb0[l] + j
                    act.wait_ge(s_at, T + 1)
                    act.activation(brh[:, :, j * P:(j + 1) * P], bank[7][:, :].rearrange("p (c t) -> p c t", c=QC),
                                   ACT.Copy).then_inc(s_ah, 1)

                for a in range(len(units) + 1):
                    g = a // 2
                    if a % (2 * nb) == 0 and a < len(units):
                        ahead(n0 + g // nb)
                    if a:
                        probs_t(a - 1)
                    if a < len(units):
                        h, u = units[a][2], a0 + a
                        act.wait_ge(s_nm, u + 1)
                        if u >= 2:
                            act.wait_ge(s_dn, 2 * u - 3)
                            act.wait_ge(s_pt, u - 1)
                        kw = 2 * L if units[a][0] == 0 else L
                        act.activation(Pb[:, u % 2, 0:kw], bank[4 + u % 2][:, 0:kw], ACT.Exp,
                                       bias=negmax[:, u % 2:u % 2 + 1], scale=HD ** -0.5,
                                       accum_out=psumP[:, u % 2:u % 2 + 1]).then_inc(s_e, 1)
                        act.activation(esink[:, u % 2:u % 2 + 1], negmax[:, u % 2:u % 2 + 1], ACT.Exp,
                                       bias=sinkB[:, l * NH + h:l * NH + h + 1]).then_inc(s_es, 1)
                    if a % NH == 1 and a > NH:
                        att_high(a // NH - 1)
                    if a % 2 == 1 and (g // nb) % 2 == 1:
                        t, half = g % nb, g // (2 * nb)
                        act.wait_ge(s_mm, before[n0] + g + 1)
                        act.activation(A[:, t, half * 512:(half + 1) * 512], bank[t][:, :], ACT.Copy).then_inc(s_g0, 1)
                att_high(nb - 1)
                for t in range(nb):
                    act.wait_ge(s_g0, (0 if l == 0 else 8) + nb + t + 1)
                    act.activation(A[:, t, :], A[:, t, :], ACT.Sigmoid).then_inc(s_g0s, 1)
                ahead(first[f"ao0.{l}"])
                ahead(first[f"ao1.{l}"])
                mod(l, 6)
                mod(l, 7)
                for g in range(NG):
                    act.wait_ge(s_mx, NG * l + g + 1)
                    act.activation(brh[:, g, 0:nb * P], bank[6 + g % 2][:, 0:nb * P], ACT.Copy,
                                   scale=VT[:, V_PS + l * NG + g:V_PS + l * NG + g + 1]).then_inc(s_mxh, 1)
                for half in range(2):
                    n = first[f"g1n{half}.{l}"]
                    ahead(n)
                    ahead(n + 1)
                    for t in range(nb):
                        if half:
                            act.wait_ge(s_mg, (0 if l == 0 else 8) + t + 1)
                        act.wait_ge(s_mm, before[n + 1] + t + 1)
                        act.activation(pin[:, t, :], bank[t][:, :], ACT.Sigmoid).then_inc(s_g1, 1)
                    mod(l, 8 + half)
                    ahead(first[f"po{half}.{l}"])
                mod(l, 10)
                mod(l, 11)
                for k in range(KT):
                    act.wait_ge(s_mgt, KT * l + k + 1)
                    act.activation(hTh[:, k, 0:nb * P], bank[4 + k % 2][:, 0:nb * P], ACT.Copy).then_inc(s_mgh, 1)
                for half in range(2):
                    n = first[f"o{half}.{l}"]
                    ahead(n)
                    ahead(n + 1)
                act.wait_ge(s_y, (0 if l == 0 else 8) + 2 * nb)
                squares(4 * l + 1, lambda t: A[:, t, :])
                build(4 * l + 2, 2 * l + 1, streams)
                if l == 0:
                    with act.Fori(0, FFULL) as f:
                        def split_f(j):
                            s = (FN + j) % 3
                            act.wait_ge(s_raw[s], 16 * ((FN + j) // 3 + 1) + f * 32)
                            act.wait_ge(s_mm, before[FN] + 4 * (j - 2) + f * 24)
                            act.activation(whi[s][:, :], raw[s][:, :], ACT.Copy).then_inc(s_hi, 1)

                        for j in range(6):
                            if j == 2:
                                for t in range(4):
                                    act.wait_ge(s_mm, before[FN] + 4 + t + 1 + f * 24)
                                    act.activation(sg[:, t, :], bank[t][:, :], ACT.Silu).then_inc(s_si, 1)
                            if j == 4:
                                for t in range(2):
                                    act.wait_ge(s_ht, t + 1 + f * 4)
                                    act.activation(h2h[:, t, :, :].rearrange("p j t -> p (j t)"), bank[4 + t][:, :],
                                                   ACT.Copy).then_inc(s_h2h, 1)
                            if j < 4:
                                split_f(j + 2)
                            else:
                                split_f(j + 2)
                            if j == 4:
                                for t in range(2, 4):
                                    act.wait_ge(s_ht, t + 1 + f * 4)
                                    act.activation(h2h[:, t, :, :].rearrange("p j t -> p (j t)"), bank[2 + t][:, :],
                                                   ACT.Copy).then_inc(s_h2h, 1)
                    n = FN + 6 * FFULL
                    ahead(n)
                    for t in range(4):
                        act.wait_ge(s_mm, before[n] + t + 1)
                        act.activation(sg[:, t, 0:FREM], bank[t][:, 0:FREM], ACT.Silu).then_inc(s_si, 1)
                    ahead(n + 1)
                    for t in range(4):
                        act.wait_ge(s_ht, 4 * FFULL + t + 1)
                        act.activation(h2h[:, t, 0:FREM // P, :].rearrange("p j t -> p (j t)"),
                                       bank[4 + t % 2][:, 0:FREM], ACT.Copy).then_inc(s_h2h, 1)
                    ahead(n + 2)
                    act.wait_ge(s_da, 8 * (FFULL + 1) + 1)
                    squares(3, lambda t: A[:, t, :])

            act.wait_ge(s_route_in, 16)
            act.activation(wrh[:, :, :], wr[:, :, :], ACT.Copy).then_inc(s_wr, 1)
            act.wait_ge(s_rt, R_DIF)
            act.activation(route[:, EXD:EXD + LB], route[:, DIF:DIF + LB], ACT.Exp).then_inc(s_rx, 1)

            def split_x(E, j, f):
                act.wait_ge(s_raw[j], 16 * ((NU // 3 if j < 3 else 0) + 1) + E * (16 * XS) + f * 16)
                act.wait_ge(s_mm, GM - 2 + j + E * XU + f * 6)
                act.activation(whi[j % 3][:, :], rawm[j][:, :], ACT.Copy).then_inc(s_hi, 1)

            def hidden_x(E, f):
                act.wait_ge(s_ht, H0 + 1 + E * XS + f)
                act.activation(h2hm[:, :, :].rearrange("p j t -> p (j t)"), bank[4][:, :], ACT.Copy).then_inc(s_h2h, 1)

            def gathered(E):
                act.wait_ge(s_xgm, KT * (E + 1))
                act.activation(xgh[:, :, :].rearrange("p k t -> p (k t)"),
                               xgm[:, :, :].rearrange("p k t -> p (k t)"), ACT.Copy).then_inc(s_xgh, 1)

            def first_slice(E):
                split_x(E, 2, 0)
                split_x(E, 3, 0)
                act.wait_ge(s_mm, GM + 2 + E * XU)
                act.activation(sgm[:, :], bank[0][:, :], ACT.Silu).then_inc(s_si, 1)
                split_x(E, 4, 0)
                split_x(E, 5, 0)

            def expert(b, e, last):
                E = e + b * NE
                act.wait_ge(s_gst, E + 1)
                act.activation(Sct[:, :], bank[5][:, 0:LB * P], ACT.Copy).then_inc(s_gsc2, 1)
                hidden_x(E, 0)

                def slice_(f, more=False):
                    split_x(E, 0, f)
                    split_x(E, 1, f)
                    act.wait_ge(s_mm, GM + E * XU + f * 6)
                    act.activation(sgm[:, :], bank[0][:, :], ACT.Silu).then_inc(s_si, 1)
                    for j in range(2, 5):
                        split_x(E, j, f)
                    if more:
                        gathered(E + 1)
                    split_x(E, 5, f)
                    hidden_x(E, f)

                with act.Fori(1, XS - 1) as f:
                    slice_(f)
                slice_(XS - 1, not last)
                if not last:
                    split_x(E, 0, XS)
                    split_x(E, 1, XS)
                act.wait_ge(s_mm, GM + XU + E * XU)
                for h in range(2):
                    act.activation(yslot[:, h * 512:(h + 1) * 512], bank[6 + h][:, :], ACT.Copy).then_inc(s_ysl, 1)
                if not last:
                    first_slice(E + 1)

            def expert_pass(b):
                gathered(b * NE)
                first_slice(b * NE)
                with act.Fori(0, NE - 1) as e:
                    expert(b, e, False)
                expert(b, NE - 1, True)

            split_x(0, 0, 0)
            split_x(0, 1, 0)
            expert_pass(0)
            act.wait_ge(s_flag, 1)
            with act.If(act.value_load(route[0:1, FLAG:FLAG + 1].bitcast(I32), min_val=0, max_val=1) > 0):
                split_x(NE, 0, 0)
                split_x(NE, 1, 0)
                expert_pass(1)
            act.wait_ge(s_moe, 1)
            squares(7, lambda t: yacc[:, t, :])

        @block.vector
        def _(dve):
            def split(n):
                dve.wait_ge(s_hi, n + 1)
                w = plan[n][2] * plan[n][3]
                dve.tensor_tensor(wlo[n % 3][:, 0:w], raw[n % 3][:, 0:w], whi[n % 3][:, 0:w].bitcast(F32),
                                  ALU.subtract).then_inc(s_lo, 1)

            def ahead(n):
                if n + 2 < NU:
                    split(n + 2)

            def mod(l, m):
                n, M = first[f"m{m}.{l}"], MCH * l + m
                ahead(n)
                ahead(n + 1)
                dve.wait_ge(s_mt, M + 1)
                dve.tensor_tensor(modT[:, 4 * m:4 * m + 4, :], bank[7][:, 0:8].rearrange("p (j s) -> p j s", s=2),
                                  VT[:, V_BM + l * MT + 4 * m:V_BM + l * MT + 4 * m + 4, None].to_broadcast([P, 4, 2]),
                                  ALU.add).then_inc(s_md, 1)

            cols = [0]

            def column(out, j0, l, i, plus):
                dve.wait_ge(s_md, MCH * l + j0 // 4 + 2)
                cols[0] += 1
                g0 = V_G + (l * 4 + i) * KT
                dve.scalar_tensor_tensor(out[:, :, :], modT[:, j0:j0 + KT, :], plus,
                                         VT[:, g0:g0 + KT, None].to_broadcast([P, KT, 2]),
                                         ALU.add, ALU.mult).then_inc(s_col, 1)

            def rms(i):
                dve.wait_ge(s_sd, i + 1)
                dve.reciprocal(rstd[:, 0:norm_nb[i]], sdev[:, 0:norm_nb[i]]).then_inc(s_rs, 1)
                dve.wait_ge(s_rs, i + 1)

            def build(i, bi, streams, which):
                rms(i)
                for t in range(norm_nb[i]):
                    dve.tensor_scalar(A[:, t, :], X[:, t, :], rstd[:, t:t + 1], None, ALU.mult).then_inc(s_xn, 1)
                dve.wait_ge(s_col, col_of[bi])
                for k in range(KT + 1):
                    if k < KT:
                        dve.wait_ge(s_tr, KT * bi + k + 1)
                        if k >= 2:
                            dve.wait_ge(s_h, KT * bi + k - 1)
                        for s in range(streams):
                            dve.tensor_scalar(hmod[:, k % 2, s * L:(s + 1) * L], bank[4 + k % 2][:, s * L:(s + 1) * L],
                                              SC[which][:, k, s:s + 1], modT[:, 24 * which + k, s:s + 1],
                                              ALU.mult, ALU.add).then_inc(s_hm, 1)
                    if k:
                        dve.wait_ge(s_hh, KT * bi + k)
                        w = streams * L
                        dve.tensor_tensor(hTl[:, k - 1, 0:w], hmod[:, (k - 1) % 2, 0:w],
                                          hTh[:, k - 1, 0:w].bitcast(F32), ALU.subtract).then_inc(s_h, 1)

            def gain_diag(which, streams):
                for s in range(streams):
                    dve.tensor_tensor(diag[:, s, :, :], ident[:, None, :].to_broadcast([P, KT, P]),
                                      GG[which][:, :, s:s + 1].to_broadcast([P, KT, P]), ALU.mult).then_inc(s_dg, 1)

            def add_normed(i, src):
                rms(i)
                y0 = 2 * xu_at[i]
                for t in range(norm_nb[i]):
                    dve.wait_ge(s_gb, gb_at[i] + t // LB + 1)
                    for h in range(2):
                        dve.scalar_tensor_tensor(src(t)[:, h * 512:(h + 1) * 512], src(t)[:, h * 512:(h + 1) * 512],
                                                 rstd[:, t:t + 1], bank[4 + 2 * (t // LB) + h][:, :],
                                                 ALU.mult, ALU.mult).then_inc(s_ys, 1)
                    dve.wait_ge(s_ys, y0 + 2 * t + 2)
                    dve.tensor_tensor(X[:, t, :], X[:, t, :], src(t), ALU.add).then_inc(s_xu, 1)

            dve.memset(ones[:, :], 1.0).then_inc(s_ini, 1)
            dve.memset(epst[:, :], EPS).then_inc(s_ini, 1)
            dve.memset(csz[:, :, :].bitcast(F32), 0.0).then_inc(s_ini, 1)
            dve.wait_ge(s_vt, 1)
            dve.tensor_copy(VT[:, 0:V_BM], bank[4][:, 0:V_BM]).then_inc(s_vtc, 1)
            dve.wait_ge(s_vt, 2)
            dve.tensor_copy(VT[:, V_BM:V_ALL], bank[5][:, 0:V_ALL - V_BM]).then_inc(s_vtc, 1)
            dve.wait_ge(s_vtc, 2)
            dve.wait_ge(s_const, 64)
            dve.tensor_scalar(nsink[:, :], sinkB[:, :], -1.0, None, ALU.mult).then_inc(s_ini, 1)
            dve.tensor_copy(identb[:, :], ident).then_inc(s_ini, 1)
            dve.tensor_copy(maskb[:, :], K[:, K_MASK:K_MASK + LB * L]).then_inc(s_ini, 1)
            dve.tensor_tensor(sel4[:, :], K[0:4, K_ID:K_ID + 2], K[0:4, K_ID + 2:K_ID + 4], ALU.add).then_inc(s_ini, 1)
            dve.wait_ge(s_csh, 1)
            dve.tensor_tensor(cst[:, :, 2:4].rearrange("p k s -> p s k"), csil[:, :].rearrange("p (s k) -> p s k", s=2),
                              cst[:, :, 0:2].bitcast(F32).rearrange("p k s -> p s k"), ALU.subtract).then_inc(s_cs, 1)
            dve.wait_ge(s_ini, 4)
            dve.tensor_copy(csz[:, :, 0:2], cst[:, :, 0:2].bitcast(F32)).then_inc(s_cs, 1)
            split(0)
            split(1)
            rope = [0]

            def rotate(t, x, out, heads, done, perm, prior, count):
                w = heads * HD
                if count:
                    dve.wait_ge(prior, count)
                cos = K[:, K_COS + t * HD:K_COS + (t + 1) * HD]
                sin = K[:, K_SIN + t * HD:K_SIN + (t + 1) * HD].rearrange("p (a f r) -> p a f r", a=2, f=2)
                dve.tensor_tensor(rope1[:, 0:w].rearrange("p (h d) -> p h d", h=heads), x.rearrange("p (h d) -> p h d", h=heads),
                                  cos[:, None, :].to_broadcast([P, heads, HD]), ALU.mult).then_inc(s_r, 1)
                x4 = x.rearrange("p (h a f r) -> p h a f r", h=heads, a=2, f=2)
                o4 = rope2[:, 0:w].rearrange("p (h a f r) -> p h a f r", h=heads, a=2, f=2)
                for f in range(2):
                    dve.tensor_tensor(o4[:, :, :, f, :], x4[:, :, :, 1 - f, :],
                                      sin[:, None, :, f, :].to_broadcast([P, heads, 2, HD // 4]), ALU.mult).then_inc(s_r, 1)
                dve.wait_ge(s_r, 3 * rope[0] + 3)
                o = out.rearrange("p (c k d) -> p k c d", k=NKV, d=HD) if perm else out
                r1_, r2_ = rope1[:, 0:w], rope2[:, 0:w]
                if perm:
                    r1_, r2_ = (v.rearrange("p (k c d) -> p k c d", k=NKV, d=HD) for v in (r1_, r2_))
                dve.tensor_tensor(o, r1_, r2_, ALU.add).then_inc(done, 1)
                rope[0] += 1

            for l in range(DEPTH):
                nb, streams = blocks(l), blocks(l) // LB
                for m in range(4):
                    mod(l, m)
                column(SC[0], KT, l, 0, 1.0)
                build(4 * l, 2 * l, 2, 0)
                n = first[f"q.{l}"]
                ahead(n)
                ahead(n + 1)
                for t in range(nb):
                    dve.wait_ge(s_mm, before[n + 1] + t + 1)
                    if t < LB:
                        rotate(t, bank[t][:, :], qrot[:, t, :], NH, s_qr, True, s_qr, qb0[l] + t)
                    else:
                        dve.tensor_copy(qrot[:, t, :].rearrange("p (c k d) -> p k c d", k=NKV, d=HD),
                                        bank[t][:, :].rearrange("p (k c d) -> p k c d", k=NKV, d=HD)).then_inc(s_qr, 1)
                mod(l, 4)
                n = first[f"kv.{l}"]
                ahead(n)
                for t in range(2 * LB):
                    dve.wait_ge(s_mm, before[n] + t + 1)
                    if t < LB:
                        rotate(t, bank[t][:, 0:P], krot[:, t, :], NKV, s_kr, False,
                               s_kr if t else s_qr, 4 * l + t if t else qb0[l] + LB)
                    else:
                        dve.tensor_copy(krot[:, t, :], bank[t][:, 0:P]).then_inc(s_kr, 1)
                    dve.tensor_copy(V[:, t, :], bank[t][:, P:2 * P]).then_inc(s_v, 1)
                mod(l, 5)
                column(GG[0], 2 * KT, l, 1, 0.0)
                n = first[f"p.{l}"]
                ahead(n)
                ahead(n + 1)

                units, a0 = units_of(l), att0[l]
                n0 = first[f"g0n0.{l}"]

                def row_max(a):
                    (s, b, h), u = units[a], a0 + a
                    q = slice(u % 2, u % 2 + 1)
                    dve.wait_ge(s_s, u + 1)
                    kw = 2 * L if s == 0 else L
                    dve.tensor_reduce(negmax0[:, q], bank[4 + u % 2][:, 0:kw], AX_X, ALU.max, negate=True).then_inc(s_nm0, 1)
                    dve.wait_ge(s_nm0, u + 1)
                    if u >= 2:
                        dve.wait_ge(s_es, u - 1)
                    dve.tensor_scalar(negmax[:, q], negmax0[:, q], HD ** -0.5, nsink[:, l * NH + h:l * NH + h + 1],
                                      ALU.mult, ALU.min).then_inc(s_nm, 1)

                def denominator(a):
                    u = a0 + a
                    q = slice(u % 2, u % 2 + 1)
                    dve.wait_ge(s_es, u + 1)
                    dve.tensor_tensor(den[:, q], psumP[:, q], esink[:, q], ALU.add).then_inc(s_dn, 1)
                    dve.wait_ge(s_dn, 2 * u + 1)
                    if u >= 2:
                        dve.wait_ge(s_oc, u - 1)
                    dve.reciprocal(rden[:, q], den[:, q]).then_inc(s_dn, 1)

                def att_scaled(a):
                    (s, b, h), u = units[a], a0 + a
                    dve.wait_ge(s_dn, 2 * u + 2)
                    dve.wait_ge(s_pv, u + 1)
                    if h == 0 and u:
                        dve.wait_ge(s_at, u // NH)
                    dve.tensor_scalar(att[:, h * HD:(h + 1) * HD], bank[7][:, h * HD:(h + 1) * HD],
                                      rden[:, u % 2:u % 2 + 1], None, ALU.mult).then_inc(s_oc, 1)

                def att_low(j):
                    T = qb0[l] + j
                    dve.wait_ge(s_ah, T + 1)
                    dve.tensor_tensor(brl[:, :, j * P:(j + 1) * P], bank[7][:, :].rearrange("p (c t) -> p c t", c=QC),
                                      brh[:, :, j * P:(j + 1) * P].bitcast(F32), ALU.subtract).then_inc(s_al, 1)

                for a in range(len(units) + 1):
                    if a % (2 * nb) == 0 and a < len(units):
                        ahead(n0 + a // (2 * nb))
                    if a < len(units):
                        row_max(a)
                    if a:
                        denominator(a - 1)
                    if a % NH == 1 and a > NH:
                        att_low(a // NH - 1)
                    if a:
                        att_scaled(a - 1)
                att_low(nb - 1)
                for h in range(2):
                    n = first[f"ao{h}.{l}"]
                    ahead(n)
                    dve.wait_ge(s_g0s, (0 if l == 0 else 4) + nb)
                    for t in range(nb):
                        dve.wait_ge(s_mm, before[n] + t + 1)
                        dve.tensor_tensor(A[:, t, h * 512:(h + 1) * 512], bank[t][:, :],
                                          A[:, t, h * 512:(h + 1) * 512], ALU.mult).then_inc(s_ao, 1)
                mod(l, 6)
                mod(l, 7)

                def mix_low(g):
                    dve.wait_ge(s_mxh, NG * l + g + 1)
                    dve.scalar_tensor_tensor(brl[:, g, 0:nb * P], bank[6 + g % 2][:, 0:nb * P],
                                             VT[:, V_PS + l * NG + g:V_PS + l * NG + g + 1],
                                             brh[:, g, 0:nb * P].bitcast(F32), ALU.mult, ALU.subtract).then_inc(s_mxl, 1)

                for g in range(NG):
                    dve.wait_ge(s_pl, NG * l + g + 1)
                    if NG * l + g:
                        dve.wait_ge(s_mx, NG * l + g)
                    dve.tensor_copy(pooledT[:, 0:nb * P], bank[4 + g % 2][:, 0:nb * P]).then_inc(s_plc, 1)
                    if g:
                        mix_low(g - 1)
                mix_low(NG - 1)
                for h in range(2):
                    n = first[f"g1n{h}.{l}"]
                    ahead(n)
                    ahead(n + 1)
                    mod(l, 8 + h)
                    n = first[f"po{h}.{l}"]
                    ahead(n)
                    p0 = (0 if l == 0 else 8) + h * nb
                    for t in range(nb):
                        dve.wait_ge(s_mm, before[n] + t + 1)
                        dve.wait_ge(s_g1, p0 + t + 1)
                        dve.tensor_tensor(pin[:, t, :], bank[t][:, :], pin[:, t, :], ALU.mult).then_inc(s_po, 1)
                        dve.wait_ge(s_po, p0 + t + 1)
                        dve.wait_ge(s_ao, p0 + t + 1)
                        dve.tensor_tensor(A[:, t, h * 512:(h + 1) * 512], A[:, t, h * 512:(h + 1) * 512],
                                          pin[:, t, :], ALU.add).then_inc(s_mg, 1)
                column(SC[1], 4 * KT, l, 2, 1.0)
                mod(l, 10)
                mod(l, 11)
                column(GG[1], 5 * KT, l, 3, 0.0)
                for k in range(KT):
                    dve.wait_ge(s_mgh, KT * l + k + 1)
                    dve.tensor_tensor(hTl[:, k, 0:nb * P], bank[4 + k % 2][:, 0:nb * P],
                                      hTh[:, k, 0:nb * P].bitcast(F32), ALU.subtract).then_inc(s_mgl, 1)
                dve.wait_ge(s_col, 4 * l + 4)
                gain_diag(0, streams)
                for h in range(2):
                    n = first[f"o{h}.{l}"]
                    ahead(n)
                    ahead(n + 1)
                    for t in range(nb):
                        dve.wait_ge(s_mm, before[n + 1] + t + 1)
                        dve.tensor_copy(A[:, t, h * 512:(h + 1) * 512], bank[t][:, :]).then_inc(s_y, 1)
                add_normed(4 * l + 1, lambda t: A[:, t, :])
                dve.wait_ge(s_gb, gb_at[4 * l + 1] + streams)
                gain_diag(1, streams)
                dve.wait_ge(s_xu, xu_at[4 * l + 2])
                build(4 * l + 2, 2 * l + 1, streams, 1)
                if l == 0:
                    dve.wait_ge(s_tr, 2 * KT)
                    dve.memset(A[:, :, :], 0.0).then_inc(s_da, 1)

                    def add_down(q, f, h, t, src, c):
                        dve.wait_ge(s_mm, before[FN] + 16 + q + 1 + f * 24)
                        dve.tensor_tensor(A[:, t, c:c + 512], A[:, t, c:c + 512], src, ALU.add).then_inc(s_da, 1)

                    with dve.Fori(0, FFULL) as f:
                        def split_f(j):
                            s = (FN + j) % 3
                            dve.wait_ge(s_hi, FN + j + 1 + f * 6)
                            dve.tensor_tensor(wlo[s][:, :], raw[s][:, :], whi[s][:, :].bitcast(F32),
                                              ALU.subtract).then_inc(s_lo, 1)

                        def gate_f(t):
                            dve.wait_ge(s_mm, before[FN] + 12 + t + 1 + f * 24)
                            dve.wait_ge(s_si, t + 1 + f * 4)
                            dve.tensor_tensor(sg[:, t, :], bank[t][:, :], sg[:, t, :], ALU.mult).then_inc(s_hid, 1)

                        def low_f(t):
                            dve.wait_ge(s_h2h, t + 1 + f * 4)
                            dve.tensor_tensor(h2l[:, t, :, :].rearrange("p j t -> p (j t)"), bank[4 + t % 2][:, :],
                                              h2h[:, t, :, :].bitcast(F32).rearrange("p j t -> p (j t)"),
                                              ALU.subtract).then_inc(s_h2l, 1)

                        for j in range(4):
                            split_f(j + 2)
                        gate_f(0)
                        gate_f(1)
                        low_f(0)
                        gate_f(2)
                        low_f(1)
                        gate_f(3)
                        split_f(6)
                        low_f(2)
                        for q in range(8):
                            if q == 4:
                                split_f(7)
                            dve.wait_ge(s_da, q + 1 + f * 8)
                            add_down(q, f, q // 4, q % 4, bank[6 + q % 2][:, :], (q // 4) * 512)
                            if q == 0:
                                low_f(3)
                    n = FN + 6 * FFULL
                    ahead(n)
                    ahead(n + 1)
                    for t in range(4):
                        dve.wait_ge(s_mm, before[n + 1] + t + 1)
                        dve.wait_ge(s_si, 4 * FFULL + t + 1)
                        dve.tensor_tensor(sg[:, t, 0:FREM], bank[t][:, 0:FREM], sg[:, t, 0:FREM],
                                          ALU.mult).then_inc(s_hid, 1)
                        dve.wait_ge(s_h2h, 4 * FFULL + t + 1)
                        dve.tensor_tensor(h2l[:, t, 0:FREM // P, :].rearrange("p j t -> p (j t)"),
                                          bank[4 + t % 2][:, 0:FREM],
                                          h2h[:, t, 0:FREM // P, :].bitcast(F32).rearrange("p j t -> p (j t)"),
                                          ALU.subtract).then_inc(s_h2l, 1)
                    ahead(n + 2)
                    for q in range(8):
                        dve.wait_ge(s_mm, before[n + 2] + q + 1)
                        dve.wait_ge(s_da, 8 * FFULL + q + 1)
                        dve.tensor_tensor(A[:, q // 2, (q % 2) * 512:(q % 2 + 1) * 512],
                                          A[:, q // 2, (q % 2) * 512:(q % 2 + 1) * 512], bank[6 + q % 2][:, :],
                                          ALU.add).then_inc(s_da, 1)
                    add_normed(3, lambda t: A[:, t, :])

            step = [0]

            def R(c, w=LB * NE):
                return route[:, c:c + w]

            def R3(c):
                return route[:, c:c + LB * NE].rearrange("p (b e) -> p b e", b=LB)

            def did(ins):
                step[0] += 1
                ins.then_inc(s_rt, 1)
                dve.wait_ge(s_rt, step[0])

            dve.wait_ge(s_wr, 1)
            dve.tensor_tensor(wrl[:, :, :], wr[:, :, :], wrh[:, :, :].bitcast(F32), ALU.subtract).then_inc(s_wrl, 1)
            dve.wait_ge(s_lg, 1)
            did(dve.tensor_tensor(R3(LG), bank[0][:, 0:LB * NE].rearrange("p (b e) -> p b e", b=LB),
                                  brB[:, None, :].to_broadcast([P, LB, NE]), ALU.add))
            for b in range(LB):
                did(dve.max(route[:, M8 + 8 * b:M8 + 8 * b + 8], route[:, LG + NE * b:LG + NE * (b + 1)]))
            did(dve.tensor_tensor(R(DIF, LB), route[:, M8 + 1:M8 + 10:8], route[:, M8:M8 + 9:8], ALU.subtract))
            assert step[0] == R_DIF
            for b in range(LB):
                le = route[:, LG + NE * b:LG + NE * (b + 1)]
                lj = le[:, None, :].to_broadcast([P, NE, NE])
                li = le[:, :, None].to_broadcast([P, NE, NE])
                t1 = route[:, T1:T1 + NE * NE].rearrange("p (e j) -> p e j", e=NE)
                t2 = route[:, T2:T2 + NE * NE].rearrange("p (e j) -> p e j", e=NE)
                did(dve.tensor_tensor(t1, lj, li, ALU.is_gt))
                did(dve.tensor_tensor(t2, lj, li, ALU.is_equal))
                did(dve.tensor_tensor(t2, t2, K[:, K_JLT:K_JLT + NE * NE].rearrange("p (e j) -> p e j", e=NE), ALU.mult))
                did(dve.tensor_tensor(t1, t1, t2, ALU.add))
                did(dve.tensor_reduce(route[:, RK + NE * b:RK + NE * (b + 1)], t1, AX_X, ALU.add))
            did(dve.tensor_scalar(R(F1), R(RK), 0.0, None, ALU.is_equal))
            did(dve.tensor_scalar(R(F2), R(RK), 1.0, None, ALU.is_equal))
            did(dve.tensor_tensor(R(SEL), R(F1), R(F2), ALU.add))
            assert step[0] == R_SEL
            dve.wait_ge(s_rx, 1)
            did(dve.tensor_scalar(R(DNR, LB), R(EXD, LB), 1.0, None, ALU.add))
            did(dve.reciprocal(R(W1, LB), R(DNR, LB)))
            did(dve.tensor_tensor(R(W2, LB), R(EXD, LB), R(W1, LB), ALU.mult))
            for f, w in ((F1, W1), (F2, W2)):
                did(dve.tensor_tensor(R3(f), R3(f), route[:, w:w + LB, None].to_broadcast([P, LB, NE]), ALU.mult))
            did(dve.tensor_tensor(R(CW), R(F1), R(F2), ALU.add))
            dve.wait_ge(s_cnt, 1)
            did(dve.scalar_tensor_tensor(R(POS), bank[1][:, 0:LB * NE], 1.0, R(SEL), ALU.add, ALU.mult))
            did(dve.tensor_scalar(R(POSM), R(POS), -1.0, None, ALU.add))
            did(dve.tensor_reduce(R(CNT, 1), bank[1][:, LB * NE:LB * NE + NE], AX_X, ALU.max))
            dve.tensor_scalar(R(FLAG, 1).bitcast(I32), R(CNT, 1), float(P), None, ALU.is_gt).then_inc(s_flag, 1)
            dve.wait_ge(s_flag, 1)
            dve.memset(yacc[:, :, :], 0.0).then_inc(s_sca, 1)
            dve.wait_ge(s_sca, 1)

            def split_x(E, j, f):
                dve.wait_ge(s_hi, NU + j + 1 + E * XU + f * 6)
                dve.tensor_tensor(wlo[j % 3][:, :], rawm[j][:, :], whi[j % 3][:, :].bitcast(F32),
                                  ALU.subtract).then_inc(s_lo, 1)

            def columns_of(src, e, out):
                v = src.rearrange("p (b e) -> p b e", b=LB)
                return dve.tensor_copy(out, v[:, :, e:e + 1] if isinstance(e, int) else v[:, :, bass.ds(e, 1)])

            def gather_matrix(b, e, E):
                columns_of(R(POSM), e, route[:, CURG:CURG + LB, None]).then_inc(s_cur, 1)
                dve.wait_ge(s_cur, E * 3 + 1)
                for t in range(LB):
                    dve.tensor_scalar(Gat[:, t, :], K[:, K_IO:K_IO + P], float(b * P), route[:, CURG + t:CURG + t + 1],
                                      ALU.add, ALU.is_equal).then_inc(s_gat, 1)

            def gathered(E):
                for k in range(KT):
                    dve.wait_ge(s_xg, 2 * E + k // 4 + 1)
                    dve.tensor_scalar(xgm[:, k, :], bank[2 + k // 4][:, (k % 4) * P:(k % 4 + 1) * P],
                                      SC[1][:, k, 0:1], modT[:, 3 * KT + k, 0:1], ALU.mult, ALU.add).then_inc(s_xgm, 1)

            def gathered_low(E):
                dve.wait_ge(s_xgh, E + 1)
                dve.tensor_tensor(xgl[:, :, :].rearrange("p k t -> p (k t)"), xgm[:, :, :].rearrange("p k t -> p (k t)"),
                                  xgh[:, :, :].bitcast(F32).rearrange("p k t -> p (k t)"), ALU.subtract).then_inc(s_xgl, 1)

            def gate_x(E, f, up):
                dve.wait_ge(s_mm, up)
                dve.wait_ge(s_si, H0 + 1 + E * XS + f)
                dve.tensor_tensor(sgm[:, :], bank[1][:, :], sgm[:, :], ALU.mult).then_inc(s_hid, 1)

            def low_x(E, f):
                dve.wait_ge(s_h2h, H0 + 1 + E * XS + f)
                dve.tensor_tensor(h2lm[:, :, :].rearrange("p j t -> p (j t)"), bank[4][:, :],
                                  h2hm[:, :, :].bitcast(F32).rearrange("p j t -> p (j t)"),
                                  ALU.subtract).then_inc(s_h2l, 1)

            def first_slice(b, e, E):
                split_x(E, 2, 0)
                split_x(E, 3, 0)
                columns_of(R(POSM), e, route[:, CURS:CURS + LB, None]).then_inc(s_cur, 1)
                columns_of(R(CW), e, route[:, CURW:CURW + LB, None]).then_inc(s_cur, 1)
                dve.wait_ge(s_cur, 3 + E * 3)
                for t in range(LB):
                    dve.tensor_scalar(Gsc[:, t, :], K[:, K_IO:K_IO + P], float(b * P), route[:, CURS + t:CURS + t + 1],
                                      ALU.add, ALU.is_equal).then_inc(s_gsc, 1)
                    dve.wait_ge(s_gsc, 2 * t + 1 + E * 4)
                    dve.tensor_scalar(Gsc[:, t, :], Gsc[:, t, :], route[:, CURW + t:CURW + t + 1], None,
                                      ALU.mult).then_inc(s_gsc, 1)
                split_x(E, 4, 0)
                split_x(E, 5, 0)
                gate_x(E, 0, GM + 4 + E * XU)

            def expert(b, e, last):
                E = e + b * NE

                def slice_(f, fill=None):
                    for j in range(5):
                        split_x(E, j, f)
                    gate_x(E, f, GM + 2 + E * XU + f * 6)
                    if fill:
                        fill()
                    split_x(E, 5, f)
                    low_x(E, f)

                if not last:
                    gather_matrix(b, e + 1, E + 1)
                low_x(E, 0)
                slice_(1)
                if not last:
                    gathered(E + 1)
                with dve.Fori(2, XS - 1) as f:
                    slice_(f)
                slice_(XS - 1, None if last else lambda: gathered_low(E + 1))
                if not last:
                    split_x(E, 0, XS)
                    split_x(E, 1, XS)
                    first_slice(b, e + 1, E + 1)
                for q in range(2 * LB):
                    dve.wait_ge(s_sc, q + 1 + E * 4)
                    t, h = q // 2, q % 2
                    dve.tensor_tensor(yacc[:, t, h * 512:(h + 1) * 512], yacc[:, t, h * 512:(h + 1) * 512],
                                      bank[2 + q % 2][:, :], ALU.add).then_inc(s_sca, 1)
                dve.wait_ge(s_sca, 5 + E * 4)

            def expert_pass(b):
                gather_matrix(b, 0, b * NE)
                gathered(b * NE)
                gathered_low(b * NE)
                first_slice(b, 0, b * NE)
                with dve.Fori(0, NE - 1) as e:
                    expert(b, e, False)
                expert(b, NE - 1, True)

            split_x(0, 0, 0)
            split_x(0, 1, 0)
            expert_pass(0)
            with dve.If(dve.value_load(route[0:1, FLAG:FLAG + 1].bitcast(I32), min_val=0, max_val=1) > 0):
                split_x(NE, 0, 0)
                split_x(NE, 1, 0)
                expert_pass(1)
            dve.memset(den[:, :], 0.0).then_inc(s_moe, 1)
            add_normed(7, lambda t: yacc[:, t, :])

        @block.tensor
        def _(pe):
            def product(out, hi, lo, wh, wl, start, stop):
                pe.matmul(out, hi, wh, start=start, stop=False)
                pe.matmul(out, hi, wl, start=False, stop=False)
                return pe.matmul(out, lo, wh, start=False, stop=stop)

            def group(slot, rows, width, out, hi, lo, start, stop, col=0, w=None):
                w = w or width
                for j in range(rows):
                    c = j * width + col
                    mm = product(out, hi(j), lo(j), whi[slot][:, c:c + w], wlo[slot][:, c:c + w],
                                 start and j == 0, stop and j == rows - 1)
                mm.then_inc(s_mm, 1)

            def hT(k0, t):
                return ((lambda j: hTh[:, k0 + j, t * P:(t + 1) * P]), (lambda j: hTl[:, k0 + j, t * P:(t + 1) * P]))

            def project(n, nb, free=None):
                rows = plan[n][2]
                npieces = KT // rows
                for i in range(npieces):
                    pe.wait_ge(s_lo, n + i + 1)
                    for t in range(nb):
                        if i == 0 and free:
                            free(t)
                        hi, lo = hT(rows * i, t)
                        group((n + i) % 3, rows, plan[n][3], bank[t][:, 0:plan[n][3]], hi, lo, i == 0, i == npieces - 1)

            def mod(l, m):
                n, M = first[f"m{m}.{l}"], MCH * l + m
                if M:
                    pe.wait_ge(s_mrow, M)
                for i in range(2):
                    pe.wait_ge(s_lo, n + i + 1)
                    s = (n + i) % 3
                    for j in range(4):
                        k = 4 * i + j
                        pe.matmul(bank[6][0:4, :], cst[:, k, :], whi[s][:, j * 512:(j + 1) * 512], start=k == 0, stop=False)
                        mm = pe.matmul(bank[6][0:4, :], csz[:, k, :], wlo[s][:, j * 512:(j + 1) * 512],
                                       start=False, stop=k == KT - 1)
                    mm.then_inc(s_mm, 1)
                pe.wait_ge(s_mrow, M + 1)
                if M:
                    pe.wait_ge(s_md, M)
                for j in range(4):
                    mm = pe.matmul(bank[7][:, 2 * j:2 * j + 2], modrow[:, M % 2, j * P:(j + 1) * P], sel4[:, :],
                                   start=True, stop=True)
                mm.then_inc(s_mt, 1)

            def build(i, bi):
                for k in range(KT):
                    if k >= 2:
                        pe.wait_ge(s_hm, hm_at[bi] + (norm_nb[i] // LB) * (k - 1))
                    for t in range(norm_nb[i]):
                        if k == 0:
                            pe.wait_ge(s_xn, xn_at[i] + t + 1)
                        mm = pe.transpose(bank[4 + k % 2][:, t * P:(t + 1) * P], A[:, t, k * P:(k + 1) * P], ident)
                    mm.then_inc(s_tr, 1)

            def gain_rows(i, streams):
                for s in range(streams):
                    pe.wait_ge(s_dg, gb_at[i] + s + 1)
                    for k in range(KT):
                        mm = pe.matmul(bank[4 + 2 * s + k // 4][:, (k % 4) * P:(k % 4 + 1) * P], ones[:, :],
                                       diag[:, s, k, :], start=True, stop=True)
                    mm.then_inc(s_gb, 1)

            pe.wait_ge(s_const, 64)
            pe.wait_ge(s_small, 80)
            pe.transpose(bank[4][:, 0:V_BM], vst[0:V_BM, 0, :], ident[0:V_BM, 0:V_BM]).then_inc(s_vt, 1)
            pe.transpose(bank[5][:, 0:V_ALL - V_BM], vst[0:V_ALL - V_BM, 1, :],
                         ident[0:V_ALL - V_BM, 0:V_ALL - V_BM]).then_inc(s_vt, 1)
            pe.wait_ge(s_cs, 2)
            pe.wait_ge(s_ini, 7)
            for l in range(DEPTH):
                nb, streams = blocks(l), blocks(l) // LB
                a0 = att0[l]
                for m in range(4):
                    mod(l, m)
                build(4 * l, 2 * l)
                pe.wait_ge(s_h, KT * (2 * l + 1))
                project(first[f"q.{l}"], nb)
                mod(l, 4)
                project(first[f"kv.{l}"], 2 * LB,
                        lambda t: pe.wait_ge(s_qr, qb0[l] + min(t, nb - 1) + 1))
                for t in range(nb):
                    pe.wait_ge(s_qr, qb0[l] + t + 1)
                    if t >= 2:
                        pe.wait_ge(s_qk, qb0[l] + l + t - 1)
                    for c in range(QC):
                        mm = pe.transpose(bank[4 + t % 2][:, c * P:(c + 1) * P], qrot[:, t, c * P:(c + 1) * P], ident)
                    mm.then_inc(s_qt, 1)
                mod(l, 5)
                pe.wait_ge(s_kr, 4 * (l + 1))
                pe.wait_ge(s_qk, qb0[l] + l + nb)
                for t in range(2 * LB):
                    mm = pe.transpose(bank[4][:, t * P:(t + 1) * P], krot[:, t, :], ident)
                mm.then_inc(s_kt, 1)
                project(first[f"p.{l}"], nb, lambda t: pe.wait_ge(s_v, 4 * l + t + 1))

                units = units_of(l)
                n0 = first[f"g0n0.{l}"]

                def scores(a):
                    (s, b, h), u = units[a], a0 + a
                    if a == 0:
                        pe.wait_ge(s_qk, qb0[l] + l + nb + 1)
                    if u >= 2:
                        pe.wait_ge(s_e, u - 1)
                    g, cc = h // QC, h % QC
                    k0, kw = (0, 2 * L) if s == 0 else (L, L)
                    mm = pe.matmul(bank[4 + u % 2][:, 0:kw],
                                   qT[g * HD:(g + 1) * HD, cc, (s * LB + b) * P:(s * LB + b + 1) * P],
                                   kT[g * HD:(g + 1) * HD, k0:k0 + kw], start=True, stop=s == 1)
                    if s == 0:
                        mm = pe.matmul(bank[4 + u % 2][:, 0:L], identb[:, :], maskb[:, b * L:(b + 1) * L],
                                       start=False, stop=True)
                    mm.then_inc(s_s, 1)

                def probs_t(a):
                    (s, _, _), u = units[a], a0 + a
                    pe.wait_ge(s_e, u + 1)
                    if u:
                        pe.wait_ge(s_ptc, u)
                    for kb in range(4 if s == 0 else 2):
                        mm = pe.transpose(bank[6][:, kb * P:(kb + 1) * P], Pb[:, u % 2, kb * P:(kb + 1) * P], ident)
                    mm.then_inc(s_pt, 1)

                def values(a):
                    (s, b, h), u = units[a], a0 + a
                    pe.wait_ge(s_ptc, u + 1)
                    if u:
                        pe.wait_ge(s_oc, u)
                    if h == 0 and u:
                        pe.wait_ge(s_al, u // NH)
                    g = h // QC
                    kbs = range(4) if s == 0 else range(2)
                    for kb in kbs:
                        mm = pe.matmul(bank[7][:, h * HD:(h + 1) * HD], PT[:, a % 2, kb, :],
                                       V[:, (0 if s == 0 else LB) + kb, g * HD:(g + 1) * HD],
                                       start=kb == 0, stop=kb == kbs[-1])
                    mm.then_inc(s_pv, 1)

                def att_t(j):
                    T = qb0[l] + j
                    pe.wait_ge(s_oc, NH * (T + 1))
                    for cc in range(QC):
                        mm = pe.transpose(bank[7][:, cc * P:(cc + 1) * P], att[:, cc * P:(cc + 1) * P], ident)
                    mm.then_inc(s_at, 1)

                def filler(g):
                    n, t = n0 + g // nb, g % nb
                    if t == 0:
                        pe.wait_ge(s_lo, n + 1)
                    half, i = g // (2 * nb), (g // nb) % 2
                    if i == 0 and half == 0:
                        pe.wait_ge(s_pin, qb0[l] + t + 1)
                    if i == 0 and half == 1:
                        pe.wait_ge(s_g0, (0 if l == 0 else 8) + t + 1)
                    hi, lo = hT(4 * i, t)
                    group(n % 3, 4, 512, bank[t][:, :], hi, lo, i == 0, i == 1)

                for a in range(len(units) + 1):
                    if a < len(units):
                        scores(a)
                    if a:
                        probs_t(a - 1)
                    if a % NH == 1 and a > NH:
                        att_t(a // NH - 1)
                    if a % 2 == 0 and a < len(units):
                        filler(a // 2)
                    if a:
                        values(a - 1)
                att_t(nb - 1)

                def br(j, t):
                    return brh[:, j, t * P:(t + 1) * P], brl[:, j, t * P:(t + 1) * P]

                g0 = 0 if l == 0 else 8

                def branch(n, free):
                    pe.wait_ge(s_lo, n + 1)
                    for t in range(nb):
                        free(t)
                        group(n % 3, 4, 512, bank[t][:, :], lambda j: br(j, t)[0], lambda j: br(j, t)[1], True, True)

                pe.wait_ge(s_al, qb0[l] + nb)
                branch(first[f"ao0.{l}"], lambda t: pe.wait_ge(s_g0, g0 + nb + t + 1))
                branch(first[f"ao1.{l}"], lambda t: pe.wait_ge(s_ao, g0 + t + 1))
                mod(l, 6)
                mod(l, 7)

                def pooled(g):
                    if g >= 2:
                        pe.wait_ge(s_plc, NG * l + g - 1)
                    for s in range(streams):
                        for b in range(LB):
                            mm = pe.matmul(bank[4 + g % 2][:, s * L:(s + 1) * L], pin[:, s * LB + b, g * P:(g + 1) * P],
                                           poolM[:, b, g, :], start=b == 0, stop=b == LB - 1)
                    mm.then_inc(s_pl, 1)

                def mixed(g):
                    pe.wait_ge(s_plc, NG * l + g + 1)
                    if g < 2:
                        pe.wait_ge(s_md, MCH * l + 8)
                    else:
                        pe.wait_ge(s_mxl, NG * l + g - 1)
                    pe.matmul(bank[6 + g % 2][:, 0:nb * P], poolW[:, g, :], pooledT[:, 0:nb * P],
                              start=True, stop=True).then_inc(s_mx, 1)

                pe.wait_ge(s_pin, qb0[l] + nb)
                pe.wait_ge(s_poolw, 16 * (l + 1))
                pooled(0)
                for g in range(NG):
                    if g + 1 < NG:
                        pooled(g + 1)
                    mixed(g)
                for h in range(2):
                    free = ((lambda t: pe.wait_ge(s_ao, g0 + nb + t + 1)) if h == 0 else
                            (lambda t: pe.wait_ge(s_po, g0 + t + 1)))
                    project(first[f"g1n{h}.{l}"], nb, free)
                    if h == 0:
                        pe.wait_ge(s_mxl, NG * (l + 1))
                    mod(l, 8 + h)
                    branch(first[f"po{h}.{l}"], lambda t: pe.wait_ge(s_g1, g0 + h * nb + t + 1))
                mod(l, 10)
                mod(l, 11)
                for k in range(KT):
                    if k >= 2:
                        pe.wait_ge(s_mgl, KT * l + k - 1)
                    for t in range(nb):
                        if k in (0, 4):
                            pe.wait_ge(s_mg, g0 + (k // 4) * nb + t + 1)
                        mm = pe.transpose(bank[4 + k % 2][:, t * P:(t + 1) * P], A[:, t, k * P:(k + 1) * P], ident)
                    mm.then_inc(s_mgt, 1)
                pe.wait_ge(s_mgl, KT * (l + 1))
                project(first[f"o0.{l}"], nb)
                project(first[f"o1.{l}"], nb, lambda t: pe.wait_ge(s_y, g0 + t + 1))
                pe.wait_ge(s_md, MCH * (l + 1))
                gain_rows(4 * l + 1, streams)
                pe.wait_ge(s_ys, 2 * xu_at[4 * l + 2])
                build(4 * l + 2, 2 * l + 1)
                pe.wait_ge(s_h, KT * (2 * l + 2))
                if l == 0:
                    pe.wait_ge(s_y, 2 * nb)

                    def hidden_t(t, f, tiles):
                        pe.wait_ge(s_hid, t + 1 + f * 4)
                        if t >= 2:
                            pe.wait_ge(s_h2l, t - 1 + f * 4)
                        for j in range(tiles):
                            mm = pe.transpose(bank[4 + t % 2][:, j * P:(j + 1) * P], sg[:, t, j * P:(j + 1) * P], ident)
                        mm.then_inc(s_ht, 1)

                    def h2(t):
                        return (lambda j: h2h[:, t, j, :]), (lambda j: h2l[:, t, j, :])

                    with pe.Fori(0, FFULL) as f:
                        for j in range(4):
                            pe.wait_ge(s_lo, FN + j + 1 + f * 6)
                            for t in range(4):
                                if j == 2:
                                    pe.wait_ge(s_si, t + 1 + f * 4)
                                if j == 3 and t == 2:
                                    hidden_t(0, f, 4)
                                if j == 3 and t == 3:
                                    hidden_t(1, f, 4)
                                hi, lo = hT(4 * (j % 2), t)
                                group((FN + j) % 3, 4, 512, bank[t][:, :], hi, lo, j % 2 == 0, j % 2 == 1)
                        for h in range(2):
                            pe.wait_ge(s_lo, FN + 4 + h + 1 + f * 6)
                            for t in range(4):
                                q = 4 * h + t
                                if h == 0:
                                    pe.wait_ge(s_h2l, t + 1 + f * 4)
                                pe.wait_ge(s_da, (q if q >= 2 else 1) + f * 8)
                                hi, lo = h2(t)
                                group((FN + 4 + h) % 3, 4, 512, bank[6 + q % 2][:, :], hi, lo, True, True)
                                if h == 0 and t < 2:
                                    hidden_t(2 + t, f, 4)
                    n = FN + 6 * FFULL
                    project(n, 4)
                    project(n + 1, 4, lambda t: pe.wait_ge(s_si, 4 * FFULL + t + 1))
                    for t in range(4):
                        hidden_t(t, FFULL, FREM // P)
                    pe.wait_ge(s_lo, n + 3)
                    for q in range(8):
                        t, h = q // 2, q % 2
                        pe.wait_ge(s_h2l, 4 * FFULL + t + 1)
                        pe.wait_ge(s_da, 8 * FFULL + max(q, 1))
                        hi, lo = h2(t)
                        group((n + 2) % 3, FREM // P, D, bank[6 + q % 2][:, :], hi, lo, True, True, col=h * 512, w=512)
                    pe.wait_ge(s_h2l, H0)
                    pe.wait_ge(s_da, 8 * FFULL + 9)
                    gain_rows(3, streams)
                    pe.wait_ge(s_ys, 16)

            pe.wait_ge(s_wrl, 1)
            pe.wait_ge(s_y, 12)
            for b in range(LB):
                for k in range(KT):
                    hi, lo = hTh[:, k, b * P:(b + 1) * P], hTl[:, k, b * P:(b + 1) * P]
                    o = bank[0][:, b * NE:(b + 1) * NE]
                    product(o, hi, lo, wrh[:, k, :], wrl[:, k, :], k == 0, False)
                    mm = pe.matmul(o, lo, wrl[:, k, :], start=False, stop=k == KT - 1)
            mm.then_inc(s_lg, 1)
            pe.wait_ge(s_rt, R_SEL)
            tri = K[:, K_TRI:K_TRI + P]
            s0, s1 = route[:, SEL:SEL + NE], route[:, SEL + NE:SEL + 2 * NE]
            pe.matmul(bank[1][:, 0:NE], tri, s0, start=True, stop=True)
            pe.matmul(bank[1][:, NE:2 * NE], tri, s1, start=True, stop=False)
            pe.matmul(bank[1][:, NE:2 * NE], ones[:, :], s0, start=False, stop=True)
            pe.matmul(bank[1][:, 2 * NE:3 * NE], ones[:, :], s0, start=True, stop=False)
            pe.matmul(bank[1][:, 2 * NE:3 * NE], ones[:, :], s1, start=False, stop=True).then_inc(s_cnt, 1)

            def gather(E, added):
                pe.wait_ge(s_gat, 2 + E * 2)
                pe.wait_ge(s_sca, added)
                for k in range(KT):
                    for t in range(LB):
                        mm = pe.matmul(bank[2 + k // 4][:, (k % 4) * P:(k % 4 + 1) * P], A[:, t, k * P:(k + 1) * P],
                                       Gat[:, t, :], start=t == 0, stop=t == LB - 1)
                    if k % 4 == 3:
                        mm.then_inc(s_xg, 1)

            def gate_up(E, f, p0):
                for j in range(4):
                    pe.wait_ge(s_lo, NU + p0 + j + 1 + E * XU + f * 6)
                    k0 = 4 * (j % 2)
                    group((p0 + j) % 3, 4, 512, bank[j // 2][:, :], lambda i: xgh[:, k0 + i, :],
                          lambda i: xgl[:, k0 + i, :], j % 2 == 0, j % 2 == 1)

            def first_slice(E):
                pe.wait_ge(s_xgl, E + 1)
                gate_up(E, 0, 0)

            def expert(b, e, last):
                E = e + b * NE

                def hidden_t(f):
                    pe.wait_ge(s_hid, H0 + 1 + E * XS + f)
                    for j in range(4):
                        mm = pe.transpose(bank[4][:, j * P:(j + 1) * P], sgm[:, j * P:(j + 1) * P], ident)
                    mm.then_inc(s_ht, 1)

                def down(f, p0, start, stop):
                    for h in range(2):
                        pe.wait_ge(s_lo, NU + p0 + h + 1 + E * XU + f * 6)
                        if h == 0:
                            pe.wait_ge(s_h2l, H0 + E * XS + f)
                        group((p0 + h) % 3, 4, 512, bank[6 + h][:, :],
                              lambda i: h2hm[:, i, :], lambda i: h2lm[:, i, :], start, stop)

                pe.wait_ge(s_gsc, 4 + E * 4)
                for t in range(LB):
                    mm = pe.transpose(bank[5][:, t * P:(t + 1) * P], Gsc[:, t, :], ident)
                mm.then_inc(s_gst, 1)
                hidden_t(0)
                gate_up(E, 1, -2)
                down(1, 2, True, False)
                if not last:
                    gather(E + 1, 1 + E * 4)
                hidden_t(1)
                with pe.Fori(2, XS) as f:
                    gate_up(E, f, -2)
                    down(f, 2, False, False)
                    hidden_t(f)
                down(XS, -2, False, True)
                if not last:
                    first_slice(E + 1)
                pe.wait_ge(s_gsc2, E + 1)
                pe.wait_ge(s_ysl, 2 + E * 2)
                if not last:
                    pe.wait_ge(s_xgm, KT * 2 + E * KT)
                for q in range(2 * LB):
                    t, h = q // 2, q % 2
                    pe.wait_ge(s_sca, (q if q >= 2 else 1) + E * 4)
                    pe.matmul(bank[2 + q % 2][:, :], Sct[:, t * P:(t + 1) * P], yslot[:, h * 512:(h + 1) * 512],
                              start=True, stop=True).then_inc(s_sc, 1)

            def expert_pass(b):
                gather(b * NE, 1 + b * NE * 4)
                first_slice(b * NE)
                with pe.Fori(0, NE - 1) as e:
                    expert(b, e, False)
                expert(b, NE - 1, True)

            expert_pass(0)
            pe.wait_ge(s_flag, 1)
            with pe.If(pe.value_load(route[0:1, FLAG:FLAG + 1].bitcast(I32), min_val=0, max_val=1) > 0):
                expert_pass(1)
            pe.wait_ge(s_h2l, H0 + XS * NE)
            gain_rows(7, 1)


_INS = ["x", "c", "ctx", "c_ctx", "w_mod", "b_mod", "norm_g", "w_in", "sinks", "w_att_o", "pool_w", "pool_scale",
        "w_pool_o", "w_out", "w_ffn_gate", "w_ffn_up", "w_ffn_down", "w_router", "b_router",
        "w_exp_gate", "w_exp_up", "w_exp_down"]


def kernel(**inputs):
    import numpy as _np
    import concourse.bacc as _bacc
    from concourse import mybir as _mybir
    from concourse.bass_utils import run_bass_kernel_spmd as _run

    nc = _bacc.Bacc("TRN2", target_bir_lowering=False, num_devices=1)
    k_const, k_pool = constants()
    given = {name: inputs[name] for name in _INS}
    given.update(k_const=k_const, k_pool=k_pool)
    arrays, args = {}, []
    for name, a in given.items():
        a = _np.ascontiguousarray(a)
        arrays[f"in_{name}_dram"] = a
        args.append(nc.dram_tensor(f"in_{name}_dram", a.shape, _mybir.dt.from_np(a.dtype), kind="ExternalInput").ap())
    args.append(nc.dram_tensor("out_0_dram", (1, L, D), _mybir.dt.float32, kind="ExternalOutput").ap())
    backbone(nc, *args)
    r = _run(nc, [arrays], core_ids=[0])
    return r.results[0]["out_0_dram"]
```

```python
from contextlib import ExitStack

import numpy as np
import concourse.bass as bass
from concourse import mybir

F32 = mybir.dt.float32
F32R = mybir.dt.float32r
I32 = mybir.dt.int32
BF16 = mybir.dt.bfloat16
ALU = mybir.AluOpType
ACT = mybir.ActivationFunctionType
AX_X = mybir.AxisListType.X

P = 128
D = 1024
KT = D // P
L = 256
LB = L // P
DEPTH = 2
HD, NH, NKV = 64, 8, 2
QC = NH // NKV
ATT = NH * HD
GRID_W, ROPE_BASE, WINDOW = 64, 10000.0, 128
POOL_WINDOWS = (2, 4, 8, 16)
NG = len(POOL_WINDOWS)
N_MOD = 6
MCH = N_MOD * D // 512
MT = N_MOD * KT
D_FF, D_EXP, NE = 2816, 3584, 8
EPS, NEG = 1e-6, -1e30
FFULL = D_FF // 512
FREM = D_FF - FFULL * 512
XS = D_EXP // 512
XU = 6 * XS
KVC, PC, GC = ATT, ATT + 2 * NKV * HD, ATT + 2 * NKV * HD + 512
(LG, T1, T2, RK, RK2, F1, F2, SEL, M8, DIF, EXD, DNR, W1, W2, CW, POS, POSM, CNT, FLAG, CURG, CURS, CURW) = np.cumsum(
    [0, 16, 128, 128, 16, 16, 16, 16, 16, 16, 2, 2, 2, 2, 2, 16, 16, 16, 8, 2, 2, 2]).tolist()

V_G, V_PS, V_BM = 2 * KT, 2 * KT + DEPTH * 4 * KT, 2 * KT + DEPTH * 4 * KT + DEPTH * NG
V_ALL = V_BM + DEPTH * MT
K_ID, K_TRI, K_IO, K_JLT, K_COS, K_SIN, K_MASK = 0, 128, 256, 384, 448, 576, 704
K_ALL = K_MASK + LB * L


def constants():
    k = np.zeros((P, K_ALL), np.float32)
    k[:, K_ID:K_ID + P] = np.eye(P)
    k[:, K_TRI:K_TRI + P] = np.triu(np.ones((P, P)), 1)
    k[:, K_IO:K_IO + P] = np.arange(P)[None]
    k[:, K_JLT:K_JLT + NE * NE] = (np.arange(NE)[None, :] < np.arange(NE)[:, None]).astype(np.float32).reshape(1, -1)
    half = HD // 4
    freqs = (ROPE_BASE ** (-np.arange(half, dtype=np.float32) / half)).astype(np.float32)
    t = np.arange(L)
    for b in range(LB):
        pos = t[b * P:(b + 1) * P]
        for axis, at in enumerate((pos // GRID_W, pos % GRID_W)):
            ang = at.astype(np.float32)[:, None] * freqs[None]
            c0 = K_COS + b * HD + axis * 2 * half
            s0 = K_SIN + b * HD + axis * 2 * half
            k[:, c0:c0 + 2 * half] = np.tile(np.cos(ang), 2)
            k[:, s0:s0 + 2 * half] = np.concatenate([-np.sin(ang), np.sin(ang)], 1)
        far = np.abs(pos[:, None] - t[None, :]) > WINDOW
        k[:, K_MASK + b * L:K_MASK + (b + 1) * L] = np.where(far, NEG, 0.0)
    pool = np.zeros((P, LB, NG, L), np.float32)
    for g, w in enumerate(POOL_WINDOWS):
        lo, hi = np.clip(t - w // 2, 0, L), np.clip(t + w // 2, 0, L)
        m = ((t[:, None] >= lo[None]) & (t[:, None] < hi[None])) / (hi - lo)[None] - np.eye(L)
        pool[:, :, g, :] = m.reshape(LB, P, L).transpose(1, 0, 2)
    return k, pool.reshape(P, -1)


MODS_FIRST = [(0, m) for m in range(4)]
MODS_BUILD = {0: [(0, 4), (0, 5)], 1: [(1, 2), (1, 3)], 2: [(1, 8), (1, 9)], 3: []}
MODS_MID = [[(0, 6), (0, 7), (0, 8), (0, 9)], [None] * 4]
MODS_GAP = {1: [(0, 10), (0, 11), (1, 0), (1, 1)], 3: [(1, 4), (1, 5), (1, 6), (1, 7)], 5: [(1, 10), (1, 11)]}


def weight_plan(w):
    plan = []

    def piece(name, src, rows, width, groups):
        plan.append((name, src.rearrange("(j p) n -> p j n", p=P), rows, width, groups))

    def pair(name, m, c, groups):
        for k0 in (0, 4):
            piece(name, m[k0 * P:(k0 + 4) * P, c:c + 512], 4, 512, groups)

    def mods(chunks):
        for chunk in chunks:
            if chunk:
                pair(f"m{chunk[1]}.{chunk[0]}", w["w_mod"][chunk[0]], chunk[1] * 512, 1)

    for l in range(DEPTH):
        nb = 2 * LB if l + 1 < DEPTH else LB
        wi = w["w_in"][l]
        mid = MODS_MID[l]
        if l == 0:
            mods(MODS_FIRST)
        mods(MODS_BUILD[2 * l])
        pair(f"q.{l}", wi, 0, nb)
        piece(f"kv.{l}", wi[:, KVC:PC], 8, 256, 2 * LB)
        pair(f"p.{l}", wi, PC, nb)
        pair(f"g0n0.{l}", wi, GC, nb)
        pair(f"g0n1.{l}", wi, GC + 512, nb)
        for n in range(2):
            piece(f"ao{n}.{l}", w["w_att_o"][l][:, n * 512:(n + 1) * 512], 4, 512, nb)
            if n == 0:
                mods(mid[0:1])
        for n in range(2):
            pair(f"g1n{n}.{l}", wi, GC + D + n * 512, nb)
            mods(mid[1 + 2 * n:2 + 2 * n])
            piece(f"po{n}.{l}", w["w_pool_o"][l][:, n * 512:(n + 1) * 512], 4, 512, nb)
            if n == 0:
                mods(mid[2:3])
        for n in range(2):
            pair(f"o{n}.{l}", w["w_out"][l], n * 512, nb)
        mods(MODS_GAP[4 * l + 1])
        mods(MODS_BUILD[2 * l + 1])
        if l == 0:
            for f in range(FFULL):
                c = f * 512
                pair(f"fg{f}", w["w_ffn_gate"][0], c, nb)
                pair(f"fu{f}", w["w_ffn_up"][0], c, nb)
                for n in range(2):
                    piece(f"fd{f}.{n}", w["w_ffn_down"][0][c:c + 512, n * 512:(n + 1) * 512], 4, 512, nb)
            c = FFULL * 512
            piece("fgr", w["w_ffn_gate"][0][:, c:], 8, FREM, nb)
            piece("fur", w["w_ffn_up"][0][:, c:], 8, FREM, nb)
            piece("fdr", w["w_ffn_down"][0][c:, :], 2, D, 2 * nb)
            mods(MODS_GAP[3])
    return plan


def backbone(nc, x, c, ctx, c_ctx, w_mod, b_mod, norm_g, w_in, sinks, w_att_o, pool_w, pool_scale,
             w_pool_o, w_out, w_ffn_gate, w_ffn_up, w_ffn_down, w_router, b_router,
             w_exp_gate, w_exp_up, w_exp_down, k_const, k_pool, out):
    plan = weight_plan(dict(w_mod=w_mod, w_in=w_in, w_att_o=w_att_o, w_pool_o=w_pool_o, w_out=w_out,
                            w_ffn_gate=w_ffn_gate, w_ffn_up=w_ffn_up, w_ffn_down=w_ffn_down))
    NU = len(plan)
    assert NU % 3 == 0
    first = {}
    before = [0]
    for n, (name, _, _, _, groups) in enumerate(plan):
        first.setdefault(name, n)
        before.append(before[-1] + groups)
    GM = before[NU]
    FN = first["fg0"]
    split_pieces = [n for n, pc in enumerate(plan) if pc[0][0] != "m"]
    split_of = {n: s for s, n in enumerate(split_pieces)}
    SN = len(split_pieces)
    assert SN % 3 == 0
    SF = split_of[FN]

    def load_key(n):
        if n in split_of:
            return split_of[n], 1, n
        return (0 if n < first["q.0"] else sum(m < n for m in split_pieces) + 2), 0, n

    load_order = sorted(range(NU), key=load_key)
    load_of = {n: i for i, n in enumerate(load_order)}
    LF = load_of[first["fu0"]]

    es = ExitStack()
    with es:
        def sb(name, shape, dt=F32):
            return es.enter_context(nc.sbuf_tensor(name, shape, dt))

        raw = [sb(f"raw{i}", [P, 2048]) for i in range(3)]
        whi = [sb(f"whi{i}", [P, 2048], F32R) for i in range(3)]
        wlo = [sb(f"wlo{i}", [P, 2048], F32R) for i in range(3)]
        X = sb("X", [P, 2 * LB, D])
        K = sb("K", [P, K_ALL])
        ones = sb("ones", [P, P])
        VT = sb("VT", [P, V_ALL])
        csil = sb("csil", [P, KT, 2])
        modT = sb("modT", [P, MT, 2])
        SC = [sb(f"SC{i}", [P, KT, 2]) for i in range(2)]
        GG = [sb(f"GG{i}", [P, KT, 2]) for i in range(2)]
        ssq = sb("ssq", [P, 4])
        sdev = sb("sdev", [P, 4])
        rstd = sb("rstd", [P, 4])
        epst = sb("epst", [P, 1])
        identb = sb("identb", [P, P], BF16)
        maskb = sb("maskb", [P, LB * L], BF16)
        sinkB = sb("sinkB", [P, DEPTH * NH])
        nsink = sb("nsink", [P, DEPTH * NH])
        brB = sb("brB", [P, NE])
        negmax0 = sb("negmax0", [P, 2])
        negmax = sb("negmax", [P, 2])
        psumP = sb("psumP", [P, 2])
        esink = sb("esink", [P, 2])
        den = sb("den", [P, 2])
        rden = sb("rden", [P, 2])

        arena_kb = 106
        base = -(-nc.sbuf_base // 32) * 32
        arena = sb("arena", [P, arena_kb * 256])

        def at(name, kb, shape, dt=F32):
            return nc.alloc_sbuf_tensor_at(name, shape, dt, offset=base + int(kb * 1024))

        hTh = at("hTh", 0, [P, KT, 512], F32R)
        hTl = at("hTl", 16, [P, KT, 512], F32R)
        A = at("A", 32, [P, 2 * LB, D])
        rope1 = at("rope1", 32, [P, 512])
        rope2 = at("rope2", 34, [P, 512])
        qrot = at("qrot", 36, [P, 2 * LB, 512])
        krot = at("krot", 44, [P, 2 * LB, P])
        r1 = 48
        pin = at("pin", r1, [P, 2 * LB, 512])
        qT = at("qT", r1 + 8, [P, QC, 512])
        diag = at("diag", r1 + 8, [P, 2, KT, P])
        brh = at("brh", r1 + 16, [P, 4, 512], F32R)
        brl = at("brl", r1 + 24, [P, 4, 512], F32R)
        poolM = at("poolM", r1 + 32, [P, LB, NG, L])
        kT = at("kT", r1 + 40, [P, 512])
        V = at("V", r1 + 42, [P, 2 * LB, P])
        Pb = at("Pb", r1 + 45, [P, 2, 512])
        modrow = at("modrow", r1 + 40, [2, 2, 512])
        hmod = at("hmod", r1 + 45, [P, 2, 512])
        PT = at("PT", r1 + 49, [P, 2, 4, P])
        junk = at("junk", r1 + 49, [P, D])
        pooledT = at("pooledT", r1 + 53, [P, 512])
        att = at("att", r1 + 53, [P, ATT])
        poolW = at("poolW", r1 + 55, [P, NG, P])
        vst = at("vst", r1 + 16, [P, 2, P])
        sg = at("sg", r1, [P, 2 * LB, 512])
        h2h = at("h2h", r1 + 16, [P, 2 * LB, 4, P], F32R)
        h2l = at("h2l", r1 + 24, [P, 2 * LB, 4, P], F32R)
        rawm = raw + [at(f"raw{3 + i}", r1 + 16 + 8 * i, [P, 2048]) for i in range(3)]
        wr = at("wr", r1 + 57, [P, KT, NE])
        wrh = at("wrh", r1 + 44, [P, KT, NE], F32R)
        wrl = at("wrl", r1 + 44.25, [P, KT, NE], F32R)
        xn = A[:, 0:LB, :]
        yacc = A[:, LB:2 * LB, :]
        xgm = at("xgm", 0, [P, KT, P])
        xgh = at("xgh", r1, [P, KT, P], F32R)
        xgl = at("xgl", r1 + 4, [P, KT, P], F32R)
        yslot = at("yslot", r1 + 40, [P, D])
        sgm = at("sgm", 4, [P, 512])
        h2hm = at("h2hm", 8, [P, 4, P], F32R)
        h2lm = at("h2lm", 10, [P, 4, P], F32R)
        Gat = at("Gat", 12, [P, LB, P])
        Gsc = at("Gsc", 13, [P, LB, P])
        Sct = at("Sct", 14, [P, LB * P])
        route = at("route", r1 + 53, [P, 1024])

        bank = [es.enter_context(nc.psum_tensor(f"bank{i}", [P, 512], F32)) for i in range(8)]

        def sem(name):
            return es.enter_context(nc.semaphore(name))

        s_small = sem("small_in")
        s_const = sem("const_in")
        s_rows = sem("broadcast_rows_in")
        s_x = sem("x_in")
        s_poolw = sem("poolw_in")
        s_poolm = sem("poolm_in")
        s_route_in = sem("router_in")
        s_raw = [sem(f"raw_full{i}") for i in range(6)]
        s_hi = sem("hi_done")
        s_lo = sem("lo_done")
        s_mm = sem("mm_done")
        s_ini = sem("ini")
        s_vt = sem("vt")
        s_vtc = sem("vt_copied")
        s_csil = sem("csil")
        s_mrow = sem("modrow_ready")
        s_mt = sem("modT_psum")
        s_md = sem("modT_ready")
        s_col = sem("columns_ready")
        s_sq = sem("squares")
        s_sd = sem("sdev_ready")
        s_rs = sem("rstd_ready")
        s_xn = sem("xn_ready")
        s_tr = sem("xn_transposed")
        s_hm = sem("hmod_ready")
        s_hh = sem("h_high")
        s_h = sem("h_ready")
        s_r = sem("rope_steps")
        s_qr = sem("q_rotated")
        s_qt = sem("q_transposed")
        s_qk = sem("qT_copied")
        s_kr = sem("k_rotated")
        s_kt = sem("k_transposed")
        s_v = sem("v_copied")
        s_pin = sem("pool_in_copied")
        s_g0 = sem("gate0_copied")
        s_g0s = sem("gate0_sigmoid")
        s_s = sem("scores_ready")
        s_nm0 = sem("rowmax")
        s_nm = sem("negmax_ready")
        s_e = sem("exp_ready")
        s_es = sem("sink_exp")
        s_dn = sem("den_steps")
        s_pt = sem("probs_transposed")
        s_ptc = sem("probsT_copied")
        s_pv = sem("att_ready")
        s_oc = sem("att_scaled")
        s_at = sem("att_transposed")
        s_ah = sem("att_high")
        s_al = sem("att_low")
        s_ao = sem("att_gated")
        s_pl = sem("pooled")
        s_plc = sem("pooled_copied")
        s_mx = sem("pool_mixed")
        s_mxh = sem("pool_high")
        s_mxl = sem("pool_low")
        s_g1 = sem("gate1_sigmoid")
        s_po = sem("pool_gated")
        s_mg = sem("merged")
        s_mgt = sem("merged_transposed")
        s_mgh = sem("merged_high")
        s_mgl = sem("merged_low")
        s_y = sem("y_copied")
        s_dg = sem("diag_ready")
        s_gb = sem("gain_rows")
        s_ys = sem("y_scaled")
        s_xu = sem("x_updated")
        s_si = sem("silu_ready")
        s_hid = sem("hidden_ready")
        s_ht = sem("hidden_transposed")
        s_h2h = sem("hidden_high")
        s_h2l = sem("hidden_low")
        s_da = sem("down_added")
        s_wr = sem("router_high")
        s_wrl = sem("router_low")
        s_lg = sem("logits_psum")
        s_rt = sem("router_steps")
        s_rx = sem("router_exp")
        s_cnt = sem("counts_psum")
        s_flag = sem("flag_ready")
        s_gat = sem("gather_matrix")
        s_gsc = sem("scatter_weights")
        s_gst = sem("scatter_transposed")
        s_gsc2 = sem("scatter_copied")
        s_cur = sem("expert_columns")
        s_xg = sem("gathered")
        s_xgm = sem("gathered_modulated")
        s_xgh = sem("gathered_high")
        s_xgl = sem("gathered_low")
        s_ysl = sem("yslot_copied")
        s_sc = sem("scattered")
        s_sca = sem("scatter_added")
        s_moe = sem("experts_done")
        s_out = sem("out_stored")

        block = es.enter_context(nc.Block())

        ident = K[:, K_ID:K_ID + P]

        hm_at = [0, 16, 32, 48]
        col_of = [1, 3, 5, 7]
        gb_at = {1: 0, 3: 2, 5: 4, 7: 5}
        R_SEL = 17
        R_DIF = 4
        H0 = 4 * (FFULL + 1)

        def blocks(l):
            return 2 * LB if l + 1 < DEPTH else LB

        def units_of(l):
            return [(s, b, h) for s in range(blocks(l) // LB) for b in range(LB) for h in range(NH)]

        att0 = [0, len(units_of(0))]
        qb0 = [0, 2 * LB]
        norm_nb = [4, 4, 4, 4, 4, 2, 2, 2]
        norm_at = [sum(norm_nb[:i]) for i in range(9)]
        xu_at = [0, 0, 4, 4, 8, 8, 10, 10]
        xn_at = [0, 0, 4, 4, 8, 8, 12, 12]

        gap_mods = {MCH * l + m for chunks in MODS_GAP.values() for l, m in chunks}

        def mod_bank(M):
            return bank[M % 2 if M in gap_mods else 6 + M % 2]

        @block.sync
        def _(sp):
            def slot_free(i):
                n = load_order[i]
                if n in split_of:
                    sp.wait_ge(s_lo, split_of[n] + 1)
                else:
                    sp.wait_ge(s_mm, before[n + 1])

            sp.dma_start(K[:, :], k_const).then_inc(s_const, 16)
            sp.dma_start(vst[0:KT, 0, :], c[0].rearrange("(k p) -> k p", p=P)).then_inc(s_small, 16)
            sp.dma_start(vst[KT:2 * KT, 0, :], c_ctx.rearrange("(k p) -> k p", p=P)).then_inc(s_small, 16)
            sp.dma_start(vst[V_G:V_PS, 0, :], norm_g.rearrange("l i (k p) -> (l i k) p", p=P)).then_inc(s_small, 16)
            sp.dma_start(vst[V_PS:V_BM, 0, :], pool_scale.rearrange("l (g p) -> (l g) p", p=P)).then_inc(s_small, 16)
            sp.dma_start(vst[0:V_ALL - V_BM, 1, :],
                         b_mod.rearrange("l (k p) -> (l k) p", p=P)).then_inc(s_small, 16)
            n = 0
            while n < NU:
                if n == 3:
                    sp.dma_start(X[:, 0:LB, :], x[0].rearrange("(b p) d -> p b d", p=P)).then_inc(s_x, 16)
                    sp.dma_start(X[:, LB:2 * LB, :], ctx[0].rearrange("(b p) d -> p b d", p=P)).then_inc(s_x, 16)
                if n == LF + 6:
                    with sp.Fori(1, FFULL - 1) as f:
                        for j in range(6):
                            s = (LF + j) % 3
                            if j in (2, 3):
                                src = w_ffn_down[0][bass.ds(f * 512, 512), (j % 2) * 512:(j % 2) * 512 + 512]
                            else:
                                m, c0 = (w_ffn_up[0], 0) if j < 2 else (w_ffn_gate[0], 512)
                                src = m[(j % 2) * 512:(j % 2) * 512 + 512, bass.ds(f * 512 + c0, 512)]
                            sp.wait_ge(s_lo, SF + 2 + j - 2 + f * 6)
                            sp.dma_start(raw[s][:, :].rearrange("p (j n) -> p j n", j=4),
                                         src.rearrange("(j p) n -> p j n", p=P)).then_inc(s_raw[s], 16)
                    n += 6 * (FFULL - 2)
                    continue
                _, src, rows, width, _ = plan[load_order[n]]
                if n >= 3:
                    slot_free(n - 3)
                sp.dma_start(raw[n % 3][:, 0:rows * width].rearrange("p (j n) -> p j n", j=rows),
                             src).then_inc(s_raw[n % 3], 16)
                n += 1

            def expert_loads(b, e):
                i0 = XU * NE * b + XU * e

                def go(i, slot, kind, src, cold):
                    if not cold:
                        sp.wait_ge(s_lo, SN - 5 + i)
                    sp.dma_start(rawm[slot][:, :].rearrange("p (j n) -> p j n", j=4),
                                 src.rearrange("(j p) n -> p j n", p=P)).then_inc(s_raw[slot], 16)

                def up(kind, f):
                    m = (w_exp_gate if kind < 2 else w_exp_up)[0].rearrange("e d f -> (e d) f")
                    return m[bass.ds(e * D + (kind % 2) * 512, 512), bass.ds(f * 512, 512)]

                def down(h, f):
                    m = w_exp_down[0].rearrange("e f d -> (e f) d")
                    return m[bass.ds(e * D_EXP + f * 512, 512), h * 512:h * 512 + 512]

                for j in range(4):
                    if b == 0 and isinstance(e, int) and e == 0 and j < 3:
                        slot_free(NU - 3 + j)
                        go(i0 + j, j, j, up(j, 0), True)
                    else:
                        go(i0 + j, j, j, up(j, 0), b == 0 and isinstance(e, int) and e == 0)
                with sp.Fori(1, XS) as f:
                    for j in range(6):
                        src = up(j, f) if j < 4 else down(j - 4, f - 1)
                        go(i0 + f * 6 + (j - 2), (4 + j) % 6, j, src, False)
                for j in range(2):
                    go(i0 + XU - 2 + j, 4 + j, 4 + j, down(j, XS - 1), False)

            sp.wait_ge(s_mm, before[first["po1.1"] + 1])
            expert_loads(0, 0)
            with sp.Fori(1, NE) as e:
                expert_loads(0, e)
            sp.wait_ge(s_flag, 1)
            with sp.If(sp.value_load(route[0:1, FLAG:FLAG + 1].bitcast(I32), min_val=0, max_val=1) > 0):
                with sp.Fori(0, NE) as e:
                    expert_loads(1, e)
            sp.wait_ge(s_xu, 2 * 2 * LB + LB + LB)
            sp.dma_start(out[0].rearrange("(b p) d -> p b d", p=P), X[:, 0:LB, :]).then_inc(s_out, 16)
            sp.wait_ge(s_out, 16)

        @block.gpsimd
        def _(pool):
            pool.dma_start(sinkB[:, :],
                           sinks.rearrange("(o l) h -> o (l h)", o=1).to_broadcast([P, DEPTH * NH])).then_inc(s_rows, 16)
            pool.dma_start(brB[:, :], b_router.to_broadcast([P, NE])).then_inc(s_rows, 16)
            pool.dma_start(wr[:, :, :], w_router[0].rearrange("(k p) e -> p k e", p=P)).then_inc(s_route_in, 16)
            for l in range(DEPTH):
                if l:
                    pool.wait_ge(s_mx, NG * l)
                pool.dma_start(poolW[:, :, :], pool_w[l].rearrange("g c d -> c g d")).then_inc(s_poolw, 16)
                if l == 0:
                    pool.dma_start(poolM[:, :, :, :].rearrange("p b g t -> p (b g t)"), k_pool).then_inc(s_poolm, 16)

        @block.scalar
        def _(act):
            def split(s):
                n = split_pieces[s]
                i = load_of[n]
                act.wait_ge(s_raw[i % 3], 16 * (i // 3 + 1))
                if s >= 3:
                    act.wait_ge(s_mm, before[split_pieces[s - 3] + 1])
                w = plan[n][2] * plan[n][3]
                act.activation(whi[s % 3][:, 0:w], raw[i % 3][:, 0:w], ACT.Copy).then_inc(s_hi, 1)

            def ahead(n):
                if split_of[n] + 2 < SN:
                    split(split_of[n] + 2)

            def mod(chunk):
                l, m = chunk
                n, M = first[f"m{m}.{l}"], MCH * l + m
                act.wait_ge(s_mm, before[n + 2])
                if M >= 2:
                    act.wait_ge(s_mt, M - 1)
                act.activation(modrow[:, M % 2, :], mod_bank(M)[0:2, :], ACT.Copy).then_inc(s_mrow, 1)

            def squares(i, src):
                nb = norm_nb[i]
                for t in range(nb):
                    if i + t:
                        act.wait_ge(s_sq, norm_at[i] + t)
                    act.activation(junk[:, :], src(t), ACT.Square, accum_out=ssq[:, t:t + 1]).then_inc(s_sq, 1)
                act.wait_ge(s_sq, norm_at[i] + nb)
                if i:
                    act.wait_ge(s_rs, i)
                act.activation(sdev[:, 0:nb], ssq[:, 0:nb], ACT.Sqrt, bias=epst[:, 0:1], scale=1.0 / D).then_inc(s_sd, 1)

            def build(i, bi, streams):
                gap, inside = MODS_GAP.get(i - 1, []), MODS_BUILD[bi]
                for chunk in gap[2:]:
                    mod(chunk)
                for k in range(KT):
                    act.wait_ge(s_hm, hm_at[bi] + streams * (k + 1))
                    w = streams * L
                    act.activation(hTh[:, k, 0:w], hmod[:, k % 2, 0:w], ACT.Copy).then_inc(s_hh, 1)
                    if k == 3 and inside:
                        mod(inside[0])

            def norms(i, src):
                squares(i, src)
                for chunk in MODS_GAP[i][0:2]:
                    mod(chunk)
                act.wait_ge(s_xu, xu_at[i + 1])
                squares(i + 1, lambda t: X[:, t, :])

            act.wait_ge(s_vtc, 1)
            act.activation(csil[:, :, :].rearrange("p k s -> p s k"), VT[:, 0:2 * KT].rearrange("p (s k) -> p s k", s=2),
                           ACT.Silu).then_inc(s_csil, 1)
            act.wait_ge(s_x, 32)
            act.wait_ge(s_ini, 2)
            squares(0, lambda t: X[:, t, :])
            for chunk in MODS_FIRST:
                mod(chunk)
            for l in range(DEPTH):
                nb, streams = blocks(l), blocks(l) // LB
                build(4 * l, 2 * l, 2)
                if l == 0:
                    split(0)
                    split(1)
                mod(MODS_BUILD[2 * l][1])
                n = first[f"q.{l}"]
                ahead(n)
                ahead(n + 1)
                ahead(first[f"kv.{l}"])
                for t in range(nb):
                    act.wait_ge(s_qt, qb0[l] + t + 1)
                    act.activation(qT[:, :, t * P:(t + 1) * P],
                                   bank[4 + t % 2][:, :].rearrange("p (c t) -> p c t", c=QC), ACT.Copy).then_inc(s_qk, 1)
                act.wait_ge(s_kt, l + 1)
                act.activation(kT[:, :], bank[4][:, :], ACT.Copy).then_inc(s_qk, 1)
                n = first[f"p.{l}"]
                ahead(n)
                ahead(n + 1)
                for t in range(nb):
                    act.wait_ge(s_mm, before[n + 1] + t + 1)
                    act.activation(pin[:, t, :], bank[t][:, :], ACT.Copy).then_inc(s_pin, 1)

                units, a0 = units_of(l), att0[l]
                n0 = first[f"g0n0.{l}"]

                def probs_t(a):
                    act.wait_ge(s_pt, a0 + a + 1)
                    if a0 + a >= 2:
                        act.wait_ge(s_pv, a0 + a - 1)
                    act.activation(PT[:, a % 2, :, :].rearrange("p k t -> p (k t)"), bank[6][:, :],
                                   ACT.Copy).then_inc(s_ptc, 1)

                def att_high(j):
                    T = qb0[l] + j
                    act.wait_ge(s_at, T + 1)
                    act.activation(brh[:, :, j * P:(j + 1) * P], bank[7][:, :].rearrange("p (c t) -> p c t", c=QC),
                                   ACT.Copy).then_inc(s_ah, 1)

                for a in range(len(units) + 1):
                    g = a // 2
                    if a % (2 * nb) == 0 and a < len(units):
                        ahead(n0 + g // nb)
                    if a:
                        probs_t(a - 1)
                    if a < len(units):
                        h, u = units[a][2], a0 + a
                        act.wait_ge(s_nm, u + 1)
                        if u >= 2:
                            act.wait_ge(s_dn, 2 * u - 3)
                            act.wait_ge(s_pt, u - 1)
                        kw = 2 * L if units[a][0] == 0 else L
                        act.activation(Pb[:, u % 2, 0:kw], bank[4 + u % 2][:, 0:kw], ACT.Exp,
                                       bias=negmax[:, u % 2:u % 2 + 1], scale=HD ** -0.5,
                                       accum_out=psumP[:, u % 2:u % 2 + 1]).then_inc(s_e, 1)
                        act.activation(esink[:, u % 2:u % 2 + 1], negmax[:, u % 2:u % 2 + 1], ACT.Exp,
                                       bias=sinkB[:, l * NH + h:l * NH + h + 1]).then_inc(s_es, 1)
                    if a % NH == 1 and a > NH:
                        att_high(a // NH - 1)
                    if a % 2 == 1 and (g // nb) % 2 == 1:
                        t, half = g % nb, g // (2 * nb)
                        act.wait_ge(s_mm, before[n0] + g + 1)
                        act.activation(A[:, t, half * 512:(half + 1) * 512], bank[t][:, :], ACT.Copy).then_inc(s_g0, 1)
                att_high(nb - 1)
                for t in range(nb):
                    act.wait_ge(s_g0, (0 if l == 0 else 8) + nb + t + 1)
                    act.activation(A[:, t, :], A[:, t, :], ACT.Sigmoid).then_inc(s_g0s, 1)
                mid = MODS_MID[l]
                ahead(first[f"ao0.{l}"])
                ahead(first[f"ao1.{l}"])
                if mid[0]:
                    mod(mid[0])
                for g in range(NG):
                    act.wait_ge(s_mx, NG * l + g + 1)
                    act.activation(brh[:, g, 0:nb * P], bank[6 + g % 2][:, 0:nb * P], ACT.Copy,
                                   scale=VT[:, V_PS + l * NG + g:V_PS + l * NG + g + 1]).then_inc(s_mxh, 1)
                for half in range(2):
                    n = first[f"g1n{half}.{l}"]
                    ahead(n)
                    if half and mid[2]:
                        mod(mid[2])
                    ahead(n + 1)
                    for t in range(nb):
                        if half:
                            act.wait_ge(s_mg, (0 if l == 0 else 8) + t + 1)
                        act.wait_ge(s_mm, before[n + 1] + t + 1)
                        act.activation(pin[:, t, :], bank[t][:, :], ACT.Sigmoid).then_inc(s_g1, 1)
                    if mid[1 + 2 * half]:
                        mod(mid[1 + 2 * half])
                    ahead(first[f"po{half}.{l}"])
                for k in range(KT):
                    act.wait_ge(s_mgt, KT * l + k + 1)
                    act.activation(hTh[:, k, 0:nb * P], bank[4 + k % 2][:, 0:nb * P], ACT.Copy).then_inc(s_mgh, 1)
                for half in range(2):
                    n = first[f"o{half}.{l}"]
                    ahead(n)
                    ahead(n + 1)
                act.wait_ge(s_y, (0 if l == 0 else 8) + 2 * nb)
                norms(4 * l + 1, lambda t: A[:, t, :])
                build(4 * l + 2, 2 * l + 1, streams)
                if l == 0:
                    mod(MODS_BUILD[1][1])
                    with act.Fori(0, FFULL) as f:
                        def split_f(j):
                            s, i = (SF + j) % 3, LF + j - 2
                            act.wait_ge(s_raw[i % 3], 16 * (i // 3 + 1) + f * 32)
                            act.wait_ge(s_mm, before[FN] + 4 * (j - 2) + f * 24)
                            act.activation(whi[s][:, :], raw[i % 3][:, :], ACT.Copy).then_inc(s_hi, 1)

                        for j in range(6):
                            if j == 2:
                                for t in range(4):
                                    act.wait_ge(s_mm, before[FN] + 4 + t + 1 + f * 24)
                                    act.activation(sg[:, t, :], bank[t][:, :], ACT.Silu).then_inc(s_si, 1)
                            if j == 4:
                                for t in range(2):
                                    act.wait_ge(s_ht, t + 1 + f * 4)
                                    act.activation(h2h[:, t, :, :].rearrange("p j t -> p (j t)"), bank[4 + t][:, :],
                                                   ACT.Copy).then_inc(s_h2h, 1)
                            if j < 4:
                                split_f(j + 2)
                            else:
                                split_f(j + 2)
                            if j == 4:
                                for t in range(2, 4):
                                    act.wait_ge(s_ht, t + 1 + f * 4)
                                    act.activation(h2h[:, t, :, :].rearrange("p j t -> p (j t)"), bank[2 + t][:, :],
                                                   ACT.Copy).then_inc(s_h2h, 1)
                    n = FN + 6 * FFULL
                    ahead(n)
                    for t in range(4):
                        act.wait_ge(s_mm, before[n] + t + 1)
                        act.activation(sg[:, t, 0:FREM], bank[t][:, 0:FREM], ACT.Silu).then_inc(s_si, 1)
                    ahead(n + 1)
                    for t in range(4):
                        act.wait_ge(s_ht, 4 * FFULL + t + 1)
                        act.activation(h2h[:, t, 0:FREM // P, :].rearrange("p j t -> p (j t)"),
                                       bank[4 + t % 2][:, 0:FREM], ACT.Copy).then_inc(s_h2h, 1)
                    ahead(n + 2)
                    act.wait_ge(s_da, 8 * (FFULL + 1) + 1)
                    norms(3, lambda t: A[:, t, :])

            act.wait_ge(s_route_in, 16)
            act.activation(wrh[:, :, :], wr[:, :, :], ACT.Copy).then_inc(s_wr, 1)
            act.wait_ge(s_rt, R_DIF)
            act.activation(route[:, EXD:EXD + LB], route[:, DIF:DIF + LB], ACT.Exp).then_inc(s_rx, 1)

            def split_x(E, j, f):
                act.wait_ge(s_raw[j], 16 * ((NU // 3 if j < 3 else 0) + 1) + E * (16 * XS) + f * 16)
                act.wait_ge(s_mm, GM - 2 + j + E * XU + f * 6)
                act.activation(whi[j % 3][:, :], rawm[j][:, :], ACT.Copy).then_inc(s_hi, 1)

            def hidden_x(E, f):
                act.wait_ge(s_ht, H0 + 1 + E * XS + f)
                act.activation(h2hm[:, :, :].rearrange("p j t -> p (j t)"), bank[4][:, :], ACT.Copy).then_inc(s_h2h, 1)

            def gathered(E):
                act.wait_ge(s_xgm, KT * (E + 1))
                act.activation(xgh[:, :, :].rearrange("p k t -> p (k t)"),
                               xgm[:, :, :].rearrange("p k t -> p (k t)"), ACT.Copy).then_inc(s_xgh, 1)

            def first_slice(E):
                split_x(E, 2, 0)
                split_x(E, 3, 0)
                act.wait_ge(s_mm, GM + 2 + E * XU)
                act.activation(sgm[:, :], bank[0][:, :], ACT.Silu).then_inc(s_si, 1)
                split_x(E, 4, 0)
                split_x(E, 5, 0)

            def expert(b, e, last):
                E = e + b * NE
                act.wait_ge(s_gst, E + 1)
                act.activation(Sct[:, :], bank[5][:, 0:LB * P], ACT.Copy).then_inc(s_gsc2, 1)
                hidden_x(E, 0)

                def slice_(f, more=False):
                    split_x(E, 0, f)
                    split_x(E, 1, f)
                    act.wait_ge(s_mm, GM + E * XU + f * 6)
                    act.activation(sgm[:, :], bank[0][:, :], ACT.Silu).then_inc(s_si, 1)
                    for j in range(2, 5):
                        split_x(E, j, f)
                    if more:
                        gathered(E + 1)
                    split_x(E, 5, f)
                    hidden_x(E, f)

                with act.Fori(1, XS - 1) as f:
                    slice_(f)
                slice_(XS - 1, not last)
                if not last:
                    split_x(E, 0, XS)
                    split_x(E, 1, XS)
                act.wait_ge(s_mm, GM + XU + E * XU)
                for h in range(2):
                    act.activation(yslot[:, h * 512:(h + 1) * 512], bank[6 + h][:, :], ACT.Copy).then_inc(s_ysl, 1)
                if not last:
                    first_slice(E + 1)

            def expert_pass(b):
                gathered(b * NE)
                first_slice(b * NE)
                with act.Fori(0, NE - 1) as e:
                    expert(b, e, False)
                expert(b, NE - 1, True)

            split_x(0, 0, 0)
            split_x(0, 1, 0)
            expert_pass(0)
            act.wait_ge(s_flag, 1)
            with act.If(act.value_load(route[0:1, FLAG:FLAG + 1].bitcast(I32), min_val=0, max_val=1) > 0):
                split_x(NE, 0, 0)
                split_x(NE, 1, 0)
                expert_pass(1)
            act.wait_ge(s_moe, 1)
            squares(7, lambda t: yacc[:, t, :])

        @block.vector
        def _(dve):
            def split(s):
                n = split_pieces[s]
                dve.wait_ge(s_hi, s + 1)
                w = plan[n][2] * plan[n][3]
                dve.tensor_tensor(wlo[s % 3][:, 0:w], raw[load_of[n] % 3][:, 0:w], whi[s % 3][:, 0:w].bitcast(F32),
                                  ALU.subtract).then_inc(s_lo, 1)

            def ahead(n):
                if split_of[n] + 2 < SN:
                    split(split_of[n] + 2)

            def mod(chunk):
                l, m = chunk
                M = MCH * l + m
                dve.wait_ge(s_mt, M + 1)
                dve.tensor_tensor(modT[:, 4 * m:4 * m + 4, :], mod_bank(M)[:, 0:8].rearrange("p (j s) -> p j s", s=2),
                                  VT[:, V_BM + l * MT + 4 * m:V_BM + l * MT + 4 * m + 4, None].to_broadcast([P, 4, 2]),
                                  ALU.add).then_inc(s_md, 1)

            cols = [0]

            def column(out, j0, l, i, plus):
                dve.wait_ge(s_md, MCH * l + j0 // 4 + 2)
                cols[0] += 1
                g0 = V_G + (l * 4 + i) * KT
                dve.scalar_tensor_tensor(out[:, :, :], modT[:, j0:j0 + KT, :], plus,
                                         VT[:, g0:g0 + KT, None].to_broadcast([P, KT, 2]),
                                         ALU.add, ALU.mult).then_inc(s_col, 1)

            def rms(i):
                dve.wait_ge(s_sd, i + 1)
                dve.reciprocal(rstd[:, 0:norm_nb[i]], sdev[:, 0:norm_nb[i]]).then_inc(s_rs, 1)
                dve.wait_ge(s_rs, i + 1)

            def normalised(i):
                rms(i)
                for t in range(norm_nb[i]):
                    dve.tensor_scalar(A[:, t, :], X[:, t, :], rstd[:, t:t + 1], None, ALU.mult).then_inc(s_xn, 1)

            def build(i, bi, streams, which):
                gap, inside = MODS_GAP.get(i - 1, []), MODS_BUILD[bi]
                for chunk in gap[1:3]:
                    mod(chunk)
                if gap and which == 0:
                    column(SC[0], KT, bi // 2, 0, 1.0)
                dve.wait_ge(s_col, col_of[bi])
                for k in range(KT + 1):
                    if k < KT:
                        dve.wait_ge(s_tr, KT * bi + k + 1)
                        if k >= 2:
                            dve.wait_ge(s_h, KT * bi + k - 1)
                        for s in range(streams):
                            dve.tensor_scalar(hmod[:, k % 2, s * L:(s + 1) * L], bank[4 + k % 2][:, s * L:(s + 1) * L],
                                              SC[which][:, k, s:s + 1], modT[:, 24 * which + k, s:s + 1],
                                              ALU.mult, ALU.add).then_inc(s_hm, 1)
                    if k:
                        dve.wait_ge(s_hh, KT * bi + k)
                        w = streams * L
                        dve.tensor_tensor(hTl[:, k - 1, 0:w], hmod[:, (k - 1) % 2, 0:w],
                                          hTh[:, k - 1, 0:w].bitcast(F32), ALU.subtract).then_inc(s_h, 1)
                    if k == 1 and gap[3:]:
                        mod(gap[3])
                    if k == 5 and inside:
                        mod(inside[0])

            def gain_diag(which, streams):
                for s in range(streams):
                    dve.tensor_tensor(diag[:, s, :, :], ident[:, None, :].to_broadcast([P, KT, P]),
                                      GG[which][:, :, s:s + 1].to_broadcast([P, KT, P]), ALU.mult).then_inc(s_dg, 1)

            def add_normed(i, src):
                rms(i)
                y0 = 2 * xu_at[i]
                for t in range(norm_nb[i]):
                    dve.wait_ge(s_gb, gb_at[i] + t // LB + 1)
                    for h in range(2):
                        dve.scalar_tensor_tensor(src(t)[:, h * 512:(h + 1) * 512], src(t)[:, h * 512:(h + 1) * 512],
                                                 rstd[:, t:t + 1], bank[4 + 2 * (t // LB) + h][:, :],
                                                 ALU.mult, ALU.mult).then_inc(s_ys, 1)
                    dve.wait_ge(s_ys, y0 + 2 * t + 2)
                    dve.tensor_tensor(X[:, t, :], X[:, t, :], src(t), ALU.add).then_inc(s_xu, 1)

            dve.memset(ones[:, :], 1.0).then_inc(s_ini, 1)
            dve.memset(epst[:, :], EPS).then_inc(s_ini, 1)
            dve.wait_ge(s_vt, 1)
            dve.tensor_copy(VT[:, 0:V_BM], bank[4][:, 0:V_BM]).then_inc(s_vtc, 1)
            dve.wait_ge(s_vt, 2)
            dve.tensor_copy(VT[:, V_BM:V_ALL], bank[5][:, 0:V_ALL - V_BM]).then_inc(s_vtc, 1)
            dve.wait_ge(s_vtc, 2)
            dve.wait_ge(s_const, 16)
            dve.wait_ge(s_rows, 32)
            dve.tensor_scalar(nsink[:, :], sinkB[:, :], -1.0, None, ALU.mult).then_inc(s_ini, 1)
            dve.tensor_copy(identb[:, :], ident).then_inc(s_ini, 1)
            dve.tensor_copy(maskb[:, :], K[:, K_MASK:K_MASK + LB * L]).then_inc(s_ini, 1)
            normalised(0)
            for chunk in MODS_FIRST:
                mod(chunk)
            column(SC[0], KT, 0, 0, 1.0)
            rope = [0]

            def rotate(t, x, out, heads, done, perm, prior, count):
                w = heads * HD
                if count:
                    dve.wait_ge(prior, count)
                cos = K[:, K_COS + t * HD:K_COS + (t + 1) * HD]
                sin = K[:, K_SIN + t * HD:K_SIN + (t + 1) * HD].rearrange("p (a f r) -> p a f r", a=2, f=2)
                dve.tensor_tensor(rope1[:, 0:w].rearrange("p (h d) -> p h d", h=heads), x.rearrange("p (h d) -> p h d", h=heads),
                                  cos[:, None, :].to_broadcast([P, heads, HD]), ALU.mult).then_inc(s_r, 1)
                x4 = x.rearrange("p (h a f r) -> p h a f r", h=heads, a=2, f=2)
                o4 = rope2[:, 0:w].rearrange("p (h a f r) -> p h a f r", h=heads, a=2, f=2)
                for f in range(2):
                    dve.tensor_tensor(o4[:, :, :, f, :], x4[:, :, :, 1 - f, :],
                                      sin[:, None, :, f, :].to_broadcast([P, heads, 2, HD // 4]), ALU.mult).then_inc(s_r, 1)
                dve.wait_ge(s_r, 3 * rope[0] + 3)
                o = out.rearrange("p (c k d) -> p k c d", k=NKV, d=HD) if perm else out
                r1_, r2_ = rope1[:, 0:w], rope2[:, 0:w]
                if perm:
                    r1_, r2_ = (v.rearrange("p (k c d) -> p k c d", k=NKV, d=HD) for v in (r1_, r2_))
                dve.tensor_tensor(o, r1_, r2_, ALU.add).then_inc(done, 1)
                rope[0] += 1

            for l in range(DEPTH):
                nb, streams = blocks(l), blocks(l) // LB
                build(4 * l, 2 * l, 2, 0)
                if l == 0:
                    split(0)
                    split(1)
                n = first[f"q.{l}"]
                ahead(n)
                ahead(n + 1)
                for t in range(nb):
                    dve.wait_ge(s_mm, before[n + 1] + t + 1)
                    if t < LB:
                        rotate(t, bank[t][:, :], qrot[:, t, :], NH, s_qr, True, s_qr, qb0[l] + t)
                    else:
                        dve.tensor_copy(qrot[:, t, :].rearrange("p (c k d) -> p k c d", k=NKV, d=HD),
                                        bank[t][:, :].rearrange("p (k c d) -> p k c d", k=NKV, d=HD)).then_inc(s_qr, 1)
                mod(MODS_BUILD[2 * l][1])
                column(GG[0], 2 * KT, l, 1, 0.0)
                n = first[f"kv.{l}"]
                ahead(n)
                for t in range(2 * LB):
                    dve.wait_ge(s_mm, before[n] + t + 1)
                    if t < LB:
                        rotate(t, bank[t][:, 0:P], krot[:, t, :], NKV, s_kr, False,
                               s_kr if t else s_qr, 4 * l + t if t else qb0[l] + LB)
                    else:
                        dve.tensor_copy(krot[:, t, :], bank[t][:, 0:P]).then_inc(s_kr, 1)
                    dve.tensor_copy(V[:, t, :], bank[t][:, P:2 * P]).then_inc(s_v, 1)
                n = first[f"p.{l}"]
                ahead(n)
                ahead(n + 1)

                units, a0 = units_of(l), att0[l]
                n0 = first[f"g0n0.{l}"]

                def row_max(a):
                    (s, b, h), u = units[a], a0 + a
                    q = slice(u % 2, u % 2 + 1)
                    dve.wait_ge(s_s, u + 1)
                    kw = 2 * L if s == 0 else L
                    dve.tensor_reduce(negmax0[:, q], bank[4 + u % 2][:, 0:kw], AX_X, ALU.max, negate=True).then_inc(s_nm0, 1)
                    dve.wait_ge(s_nm0, u + 1)
                    if u >= 2:
                        dve.wait_ge(s_es, u - 1)
                    dve.tensor_scalar(negmax[:, q], negmax0[:, q], HD ** -0.5, nsink[:, l * NH + h:l * NH + h + 1],
                                      ALU.mult, ALU.min).then_inc(s_nm, 1)

                def denominator(a):
                    u = a0 + a
                    q = slice(u % 2, u % 2 + 1)
                    dve.wait_ge(s_es, u + 1)
                    dve.tensor_tensor(den[:, q], psumP[:, q], esink[:, q], ALU.add).then_inc(s_dn, 1)
                    dve.wait_ge(s_dn, 2 * u + 1)
                    if u >= 2:
                        dve.wait_ge(s_oc, u - 1)
                    dve.reciprocal(rden[:, q], den[:, q]).then_inc(s_dn, 1)

                def att_scaled(a):
                    (s, b, h), u = units[a], a0 + a
                    dve.wait_ge(s_dn, 2 * u + 2)
                    dve.wait_ge(s_pv, u + 1)
                    if h == 0 and u:
                        dve.wait_ge(s_at, u // NH)
                    dve.tensor_scalar(att[:, h * HD:(h + 1) * HD], bank[7][:, h * HD:(h + 1) * HD],
                                      rden[:, u % 2:u % 2 + 1], None, ALU.mult).then_inc(s_oc, 1)

                def att_low(j):
                    T = qb0[l] + j
                    dve.wait_ge(s_ah, T + 1)
                    dve.tensor_tensor(brl[:, :, j * P:(j + 1) * P], bank[7][:, :].rearrange("p (c t) -> p c t", c=QC),
                                      brh[:, :, j * P:(j + 1) * P].bitcast(F32), ALU.subtract).then_inc(s_al, 1)

                for a in range(len(units) + 1):
                    if a % (2 * nb) == 0 and a < len(units):
                        ahead(n0 + a // (2 * nb))
                    if a < len(units):
                        row_max(a)
                    if a:
                        denominator(a - 1)
                    if a % NH == 1 and a > NH:
                        att_low(a // NH - 1)
                    if a:
                        att_scaled(a - 1)
                att_low(nb - 1)
                mid = MODS_MID[l]
                for h in range(2):
                    n = first[f"ao{h}.{l}"]
                    ahead(n)
                    dve.wait_ge(s_g0s, (0 if l == 0 else 4) + nb)
                    for t in range(nb):
                        dve.wait_ge(s_mm, before[n] + t + 1)
                        dve.tensor_tensor(A[:, t, h * 512:(h + 1) * 512], bank[t][:, :],
                                          A[:, t, h * 512:(h + 1) * 512], ALU.mult).then_inc(s_ao, 1)
                if mid[0]:
                    mod(mid[0])

                def mix_low(g):
                    dve.wait_ge(s_mxh, NG * l + g + 1)
                    dve.scalar_tensor_tensor(brl[:, g, 0:nb * P], bank[6 + g % 2][:, 0:nb * P],
                                             VT[:, V_PS + l * NG + g:V_PS + l * NG + g + 1],
                                             brh[:, g, 0:nb * P].bitcast(F32), ALU.mult, ALU.subtract).then_inc(s_mxl, 1)

                for g in range(NG):
                    dve.wait_ge(s_pl, NG * l + g + 1)
                    if NG * l + g:
                        dve.wait_ge(s_mx, NG * l + g)
                    dve.tensor_copy(pooledT[:, 0:nb * P], bank[4 + g % 2][:, 0:nb * P]).then_inc(s_plc, 1)
                    if g:
                        mix_low(g - 1)
                mix_low(NG - 1)
                for h in range(2):
                    n = first[f"g1n{h}.{l}"]
                    ahead(n)
                    ahead(n + 1)
                    if h and mid[2]:
                        mod(mid[2])
                    n = first[f"po{h}.{l}"]
                    ahead(n)
                    p0 = (0 if l == 0 else 8) + h * nb
                    for t in range(nb):
                        dve.wait_ge(s_mm, before[n] + t + 1)
                        dve.wait_ge(s_g1, p0 + t + 1)
                        dve.tensor_tensor(pin[:, t, :], bank[t][:, :], pin[:, t, :], ALU.mult).then_inc(s_po, 1)
                        dve.wait_ge(s_po, p0 + t + 1)
                        dve.wait_ge(s_ao, p0 + t + 1)
                        dve.tensor_tensor(A[:, t, h * 512:(h + 1) * 512], A[:, t, h * 512:(h + 1) * 512],
                                          pin[:, t, :], ALU.add).then_inc(s_mg, 1)
                    if mid[1 + 2 * h]:
                        mod(mid[1 + 2 * h])
                column(SC[1], 4 * KT, l, 2, 1.0)
                for k in range(KT):
                    dve.wait_ge(s_mgh, KT * l + k + 1)
                    dve.tensor_tensor(hTl[:, k, 0:nb * P], bank[4 + k % 2][:, 0:nb * P],
                                      hTh[:, k, 0:nb * P].bitcast(F32), ALU.subtract).then_inc(s_mgl, 1)
                dve.wait_ge(s_col, 4 * l + 2)
                gain_diag(0, streams)
                for h in range(2):
                    n = first[f"o{h}.{l}"]
                    ahead(n)
                    ahead(n + 1)
                    for t in range(nb):
                        dve.wait_ge(s_mm, before[n + 1] + t + 1)
                        dve.tensor_copy(A[:, t, h * 512:(h + 1) * 512], bank[t][:, :]).then_inc(s_y, 1)
                add_normed(4 * l + 1, lambda t: A[:, t, :])
                mod(MODS_GAP[4 * l + 1][0])
                dve.wait_ge(s_xu, xu_at[4 * l + 2])
                normalised(4 * l + 2)
                build(4 * l + 2, 2 * l + 1, streams, 1)
                column(GG[1], 5 * KT, l, 3, 0.0)
                dve.wait_ge(s_gb, gb_at[4 * l + 1] + streams)
                dve.wait_ge(s_col, 4 * l + 4)
                gain_diag(1, streams)
                if l == 0:
                    mod(MODS_BUILD[1][1])
                    dve.wait_ge(s_tr, 2 * KT)
                    dve.memset(A[:, :, :], 0.0).then_inc(s_da, 1)

                    def add_down(q, f, h, t, src, c):
                        dve.wait_ge(s_mm, before[FN] + 16 + q + 1 + f * 24)
                        dve.tensor_tensor(A[:, t, c:c + 512], A[:, t, c:c + 512], src, ALU.add).then_inc(s_da, 1)

                    with dve.Fori(0, FFULL) as f:
                        def split_f(j):
                            s = (SF + j) % 3
                            dve.wait_ge(s_hi, SF + j + 1 + f * 6)
                            dve.tensor_tensor(wlo[s][:, :], raw[(LF + j - 2) % 3][:, :], whi[s][:, :].bitcast(F32),
                                              ALU.subtract).then_inc(s_lo, 1)

                        def gate_f(t):
                            dve.wait_ge(s_mm, before[FN] + 12 + t + 1 + f * 24)
                            dve.wait_ge(s_si, t + 1 + f * 4)
                            dve.tensor_tensor(sg[:, t, :], bank[t][:, :], sg[:, t, :], ALU.mult).then_inc(s_hid, 1)

                        def low_f(t):
                            dve.wait_ge(s_h2h, t + 1 + f * 4)
                            dve.tensor_tensor(h2l[:, t, :, :].rearrange("p j t -> p (j t)"), bank[4 + t % 2][:, :],
                                              h2h[:, t, :, :].bitcast(F32).rearrange("p j t -> p (j t)"),
                                              ALU.subtract).then_inc(s_h2l, 1)

                        for j in range(4):
                            split_f(j + 2)
                        gate_f(0)
                        gate_f(1)
                        low_f(0)
                        gate_f(2)
                        low_f(1)
                        gate_f(3)
                        split_f(6)
                        low_f(2)
                        for q in range(8):
                            if q == 4:
                                split_f(7)
                            dve.wait_ge(s_da, q + 1 + f * 8)
                            add_down(q, f, q // 4, q % 4, bank[6 + q % 2][:, :], (q // 4) * 512)
                            if q == 0:
                                low_f(3)
                    n = FN + 6 * FFULL
                    ahead(n)
                    ahead(n + 1)
                    for t in range(4):
                        dve.wait_ge(s_mm, before[n + 1] + t + 1)
                        dve.wait_ge(s_si, 4 * FFULL + t + 1)
                        dve.tensor_tensor(sg[:, t, 0:FREM], bank[t][:, 0:FREM], sg[:, t, 0:FREM],
                                          ALU.mult).then_inc(s_hid, 1)
                        dve.wait_ge(s_h2h, 4 * FFULL + t + 1)
                        dve.tensor_tensor(h2l[:, t, 0:FREM // P, :].rearrange("p j t -> p (j t)"),
                                          bank[4 + t % 2][:, 0:FREM],
                                          h2h[:, t, 0:FREM // P, :].bitcast(F32).rearrange("p j t -> p (j t)"),
                                          ALU.subtract).then_inc(s_h2l, 1)
                    ahead(n + 2)
                    for q in range(8):
                        dve.wait_ge(s_mm, before[n + 2] + q + 1)
                        dve.wait_ge(s_da, 8 * FFULL + q + 1)
                        dve.tensor_tensor(A[:, q // 2, (q % 2) * 512:(q % 2 + 1) * 512],
                                          A[:, q // 2, (q % 2) * 512:(q % 2 + 1) * 512], bank[6 + q % 2][:, :],
                                          ALU.add).then_inc(s_da, 1)
                    add_normed(3, lambda t: A[:, t, :])
                    mod(MODS_GAP[3][0])
                    dve.wait_ge(s_xu, xu_at[4])
                    normalised(4)

            step = [0]

            def R(c, w=LB * NE):
                return route[:, c:c + w]

            def R3(c):
                return route[:, c:c + LB * NE].rearrange("p (b e) -> p b e", b=LB)

            def did(ins):
                step[0] += 1
                ins.then_inc(s_rt, 1)
                dve.wait_ge(s_rt, step[0])

            dve.wait_ge(s_wr, 1)
            dve.tensor_tensor(wrl[:, :, :], wr[:, :, :], wrh[:, :, :].bitcast(F32), ALU.subtract).then_inc(s_wrl, 1)
            dve.wait_ge(s_lg, 1)
            did(dve.tensor_tensor(R3(LG), bank[0][:, 0:LB * NE].rearrange("p (b e) -> p b e", b=LB),
                                  brB[:, None, :].to_broadcast([P, LB, NE]), ALU.add))
            for b in range(LB):
                did(dve.max(route[:, M8 + 8 * b:M8 + 8 * b + 8], route[:, LG + NE * b:LG + NE * (b + 1)]))
            did(dve.tensor_tensor(R(DIF, LB), route[:, M8 + 1:M8 + 10:8], route[:, M8:M8 + 9:8], ALU.subtract))
            assert step[0] == R_DIF
            for b in range(LB):
                le = route[:, LG + NE * b:LG + NE * (b + 1)]
                lj = le[:, None, :].to_broadcast([P, NE, NE])
                li = le[:, :, None].to_broadcast([P, NE, NE])
                t1 = route[:, T1:T1 + NE * NE].rearrange("p (e j) -> p e j", e=NE)
                t2 = route[:, T2:T2 + NE * NE].rearrange("p (e j) -> p e j", e=NE)
                did(dve.tensor_tensor(t1, lj, li, ALU.is_gt))
                did(dve.tensor_tensor(t2, lj, li, ALU.is_equal))
                did(dve.tensor_tensor(t2, t2, K[:, K_JLT:K_JLT + NE * NE].rearrange("p (e j) -> p e j", e=NE), ALU.mult))
                did(dve.tensor_tensor(t1, t1, t2, ALU.add))
                did(dve.tensor_reduce(route[:, RK + NE * b:RK + NE * (b + 1)], t1, AX_X, ALU.add))
            did(dve.tensor_scalar(R(F1), R(RK), 0.0, None, ALU.is_equal))
            did(dve.tensor_scalar(R(F2), R(RK), 1.0, None, ALU.is_equal))
            did(dve.tensor_tensor(R(SEL), R(F1), R(F2), ALU.add))
            assert step[0] == R_SEL
            dve.wait_ge(s_rx, 1)
            did(dve.tensor_scalar(R(DNR, LB), R(EXD, LB), 1.0, None, ALU.add))
            did(dve.reciprocal(R(W1, LB), R(DNR, LB)))
            did(dve.tensor_tensor(R(W2, LB), R(EXD, LB), R(W1, LB), ALU.mult))
            for f, w in ((F1, W1), (F2, W2)):
                did(dve.tensor_tensor(R3(f), R3(f), route[:, w:w + LB, None].to_broadcast([P, LB, NE]), ALU.mult))
            did(dve.tensor_tensor(R(CW), R(F1), R(F2), ALU.add))
            dve.wait_ge(s_cnt, 1)
            did(dve.scalar_tensor_tensor(R(POS), bank[1][:, 0:LB * NE], 1.0, R(SEL), ALU.add, ALU.mult))
            did(dve.tensor_scalar(R(POSM), R(POS), -1.0, None, ALU.add))
            did(dve.tensor_reduce(R(CNT, 1), bank[1][:, LB * NE:LB * NE + NE], AX_X, ALU.max))
            dve.tensor_scalar(R(FLAG, 1).bitcast(I32), R(CNT, 1), float(P), None, ALU.is_gt).then_inc(s_flag, 1)
            dve.wait_ge(s_flag, 1)
            dve.memset(yacc[:, :, :], 0.0).then_inc(s_sca, 1)
            dve.wait_ge(s_sca, 1)

            def split_x(E, j, f):
                dve.wait_ge(s_hi, SN + j + 1 + E * XU + f * 6)
                dve.tensor_tensor(wlo[j % 3][:, :], rawm[j][:, :], whi[j % 3][:, :].bitcast(F32),
                                  ALU.subtract).then_inc(s_lo, 1)

            def columns_of(src, e, out):
                v = src.rearrange("p (b e) -> p b e", b=LB)
                return dve.tensor_copy(out, v[:, :, e:e + 1] if isinstance(e, int) else v[:, :, bass.ds(e, 1)])

            def gather_matrix(b, e, E):
                columns_of(R(POSM), e, route[:, CURG:CURG + LB, None]).then_inc(s_cur, 1)
                dve.wait_ge(s_cur, E * 3 + 1)
                for t in range(LB):
                    dve.tensor_scalar(Gat[:, t, :], K[:, K_IO:K_IO + P], float(b * P), route[:, CURG + t:CURG + t + 1],
                                      ALU.add, ALU.is_equal).then_inc(s_gat, 1)

            def gathered(E):
                for k in range(KT):
                    dve.wait_ge(s_xg, 2 * E + k // 4 + 1)
                    dve.tensor_scalar(xgm[:, k, :], bank[2 + k // 4][:, (k % 4) * P:(k % 4 + 1) * P],
                                      SC[1][:, k, 0:1], modT[:, 3 * KT + k, 0:1], ALU.mult, ALU.add).then_inc(s_xgm, 1)

            def gathered_low(E):
                dve.wait_ge(s_xgh, E + 1)
                dve.tensor_tensor(xgl[:, :, :].rearrange("p k t -> p (k t)"), xgm[:, :, :].rearrange("p k t -> p (k t)"),
                                  xgh[:, :, :].bitcast(F32).rearrange("p k t -> p (k t)"), ALU.subtract).then_inc(s_xgl, 1)

            def gate_x(E, f, up):
                dve.wait_ge(s_mm, up)
                dve.wait_ge(s_si, H0 + 1 + E * XS + f)
                dve.tensor_tensor(sgm[:, :], bank[1][:, :], sgm[:, :], ALU.mult).then_inc(s_hid, 1)

            def low_x(E, f):
                dve.wait_ge(s_h2h, H0 + 1 + E * XS + f)
                dve.tensor_tensor(h2lm[:, :, :].rearrange("p j t -> p (j t)"), bank[4][:, :],
                                  h2hm[:, :, :].bitcast(F32).rearrange("p j t -> p (j t)"),
                                  ALU.subtract).then_inc(s_h2l, 1)

            def first_slice(b, e, E):
                split_x(E, 2, 0)
                split_x(E, 3, 0)
                columns_of(R(POSM), e, route[:, CURS:CURS + LB, None]).then_inc(s_cur, 1)
                columns_of(R(CW), e, route[:, CURW:CURW + LB, None]).then_inc(s_cur, 1)
                dve.wait_ge(s_cur, 3 + E * 3)
                for t in range(LB):
                    dve.tensor_scalar(Gsc[:, t, :], K[:, K_IO:K_IO + P], float(b * P), route[:, CURS + t:CURS + t + 1],
                                      ALU.add, ALU.is_equal).then_inc(s_gsc, 1)
                    dve.wait_ge(s_gsc, 2 * t + 1 + E * 4)
                    dve.tensor_scalar(Gsc[:, t, :], Gsc[:, t, :], route[:, CURW + t:CURW + t + 1], None,
                                      ALU.mult).then_inc(s_gsc, 1)
                split_x(E, 4, 0)
                split_x(E, 5, 0)
                gate_x(E, 0, GM + 4 + E * XU)

            def expert(b, e, last):
                E = e + b * NE

                def slice_(f, fill=None):
                    for j in range(5):
                        split_x(E, j, f)
                    gate_x(E, f, GM + 2 + E * XU + f * 6)
                    if fill:
                        fill()
                    split_x(E, 5, f)
                    low_x(E, f)

                if not last:
                    gather_matrix(b, e + 1, E + 1)
                low_x(E, 0)
                slice_(1)
                if not last:
                    gathered(E + 1)
                with dve.Fori(2, XS - 1) as f:
                    slice_(f)
                slice_(XS - 1, None if last else lambda: gathered_low(E + 1))
                if not last:
                    split_x(E, 0, XS)
                    split_x(E, 1, XS)
                    first_slice(b, e + 1, E + 1)
                for q in range(2 * LB):
                    dve.wait_ge(s_sc, q + 1 + E * 4)
                    t, h = q // 2, q % 2
                    dve.tensor_tensor(yacc[:, t, h * 512:(h + 1) * 512], yacc[:, t, h * 512:(h + 1) * 512],
                                      bank[2 + q % 2][:, :], ALU.add).then_inc(s_sca, 1)
                dve.wait_ge(s_sca, 5 + E * 4)

            def expert_pass(b):
                gather_matrix(b, 0, b * NE)
                gathered(b * NE)
                gathered_low(b * NE)
                first_slice(b, 0, b * NE)
                with dve.Fori(0, NE - 1) as e:
                    expert(b, e, False)
                expert(b, NE - 1, True)

            split_x(0, 0, 0)
            split_x(0, 1, 0)
            expert_pass(0)
            with dve.If(dve.value_load(route[0:1, FLAG:FLAG + 1].bitcast(I32), min_val=0, max_val=1) > 0):
                split_x(NE, 0, 0)
                split_x(NE, 1, 0)
                expert_pass(1)
            dve.memset(den[:, :], 0.0).then_inc(s_moe, 1)
            add_normed(7, lambda t: yacc[:, t, :])

        @block.tensor
        def _(pe):
            def product(out, hi, lo, wh, wl, start, stop):
                pe.matmul(out, hi, wh, start=start, stop=False)
                pe.matmul(out, hi, wl, start=False, stop=False)
                return pe.matmul(out, lo, wh, start=False, stop=stop)

            def group(slot, rows, width, out, hi, lo, start, stop, col=0, w=None):
                w = w or width
                for j in range(rows):
                    c = j * width + col
                    mm = product(out, hi(j), lo(j), whi[slot][:, c:c + w], wlo[slot][:, c:c + w],
                                 start and j == 0, stop and j == rows - 1)
                mm.then_inc(s_mm, 1)

            def hT(k0, t):
                return ((lambda j: hTh[:, k0 + j, t * P:(t + 1) * P]), (lambda j: hTl[:, k0 + j, t * P:(t + 1) * P]))

            def project(n, nb, free=None):
                rows = plan[n][2]
                npieces = KT // rows
                for i in range(npieces):
                    s = split_of[n + i]
                    pe.wait_ge(s_lo, s + 1)
                    for t in range(nb):
                        if i == 0 and free:
                            free(t)
                        hi, lo = hT(rows * i, t)
                        group(s % 3, rows, plan[n][3], bank[t][:, 0:plan[n][3]], hi, lo, i == 0, i == npieces - 1)

            def mod_piece(chunk, i):
                l, m = chunk
                n, M = first[f"m{m}.{l}"] + i, MCH * l + m
                if i == 0 and M >= 2:
                    pe.wait_ge(s_md, M - 1)
                r = load_of[n]
                pe.wait_ge(s_raw[r % 3], 16 * (r // 3 + 1))
                for j in range(4):
                    mm = pe.matmul(mod_bank(M)[0:2, :], csil[:, 4 * i + j, :], raw[r % 3][:, j * 512:(j + 1) * 512],
                                   start=i + j == 0, stop=4 * i + j == KT - 1)
                mm.then_inc(s_mm, 1)

            def mod_rows(chunk):
                mod_piece(chunk, 0)
                mod_piece(chunk, 1)

            def mod_t(chunk):
                M = MCH * chunk[0] + chunk[1]
                pe.wait_ge(s_mrow, M + 1)
                for j in range(4):
                    mm = pe.transpose(mod_bank(M)[:, 2 * j:2 * j + 2], modrow[:, M % 2, j * P:(j + 1) * P],
                                      ident[0:2, 0:2])
                mm.then_inc(s_mt, 1)

            def mod_run(chunks):
                for j, chunk in enumerate(chunks):
                    mod_rows(chunk)
                    if j:
                        mod_t(chunks[j - 1])

            def build(i, bi):
                gap, inside = MODS_GAP.get(i - 1, []), MODS_BUILD[bi]
                if gap and not inside:
                    mod_t(gap[-1])
                for k in range(KT):
                    if k >= 2:
                        pe.wait_ge(s_hm, hm_at[bi] + (norm_nb[i] // LB) * (k - 1))
                    for t in range(norm_nb[i]):
                        if k == 0:
                            pe.wait_ge(s_xn, xn_at[i] + t + 1)
                        mm = pe.transpose(bank[4 + k % 2][:, t * P:(t + 1) * P], A[:, t, k * P:(k + 1) * P], ident)
                    mm.then_inc(s_tr, 1)
                    if inside and k % 2:
                        if k == 1 and gap:
                            mod_t(gap[-1])
                        if k == 5:
                            mod_t(inside[0])
                        mod_piece(inside[k // 4], k // 2 % 2)

            def gain_rows(i, streams):
                for s in range(streams):
                    pe.wait_ge(s_dg, gb_at[i] + s + 1)
                    for k in range(KT):
                        mm = pe.matmul(bank[4 + 2 * s + k // 4][:, (k % 4) * P:(k % 4 + 1) * P], ones[:, :],
                                       diag[:, s, k, :], start=True, stop=True)
                    mm.then_inc(s_gb, 1)

            pe.wait_ge(s_const, 16)
            pe.wait_ge(s_small, 80)
            pe.transpose(bank[4][:, 0:V_BM], vst[0:V_BM, 0, :], ident[0:V_BM, 0:V_BM]).then_inc(s_vt, 1)
            pe.transpose(bank[5][:, 0:V_ALL - V_BM], vst[0:V_ALL - V_BM, 1, :],
                         ident[0:V_ALL - V_BM, 0:V_ALL - V_BM]).then_inc(s_vt, 1)
            pe.wait_ge(s_csil, 1)
            pe.wait_ge(s_ini, 5)
            mod_run(MODS_FIRST)
            mod_t(MODS_FIRST[-1])
            for l in range(DEPTH):
                nb, streams = blocks(l), blocks(l) // LB
                a0 = att0[l]
                build(4 * l, 2 * l)
                pe.wait_ge(s_h, KT * (2 * l + 1))
                if l:
                    pe.wait_ge(s_md, MCH + 8)
                project(first[f"q.{l}"], nb)
                mod_t(MODS_BUILD[2 * l][1])
                project(first[f"kv.{l}"], 2 * LB,
                        lambda t: pe.wait_ge(s_qr, qb0[l] + min(t, nb - 1) + 1))
                for t in range(nb):
                    pe.wait_ge(s_qr, qb0[l] + t + 1)
                    if t >= 2:
                        pe.wait_ge(s_qk, qb0[l] + l + t - 1)
                    for c in range(QC):
                        mm = pe.transpose(bank[4 + t % 2][:, c * P:(c + 1) * P], qrot[:, t, c * P:(c + 1) * P], ident)
                    mm.then_inc(s_qt, 1)
                pe.wait_ge(s_kr, 4 * (l + 1))
                pe.wait_ge(s_qk, qb0[l] + l + nb)
                for t in range(2 * LB):
                    mm = pe.transpose(bank[4][:, t * P:(t + 1) * P], krot[:, t, :], ident)
                mm.then_inc(s_kt, 1)
                project(first[f"p.{l}"], nb, lambda t: pe.wait_ge(s_v, 4 * l + t + 1))

                units = units_of(l)
                n0 = first[f"g0n0.{l}"]

                def scores(a):
                    (s, b, h), u = units[a], a0 + a
                    if a == 0:
                        pe.wait_ge(s_qk, qb0[l] + l + nb + 1)
                        last = MODS_BUILD[2 * l][1]
                        pe.wait_ge(s_md, MCH * last[0] + last[1] + 1)
                    if u >= 2:
                        pe.wait_ge(s_e, u - 1)
                    g, cc = h // QC, h % QC
                    k0, kw = (0, 2 * L) if s == 0 else (L, L)
                    mm = pe.matmul(bank[4 + u % 2][:, 0:kw],
                                   qT[g * HD:(g + 1) * HD, cc, (s * LB + b) * P:(s * LB + b + 1) * P],
                                   kT[g * HD:(g + 1) * HD, k0:k0 + kw], start=True, stop=s == 1)
                    if s == 0:
                        mm = pe.matmul(bank[4 + u % 2][:, 0:L], identb[:, :], maskb[:, b * L:(b + 1) * L],
                                       start=False, stop=True)
                    mm.then_inc(s_s, 1)

                def probs_t(a):
                    (s, _, _), u = units[a], a0 + a
                    pe.wait_ge(s_e, u + 1)
                    if u:
                        pe.wait_ge(s_ptc, u)
                    for kb in range(4 if s == 0 else 2):
                        mm = pe.transpose(bank[6][:, kb * P:(kb + 1) * P], Pb[:, u % 2, kb * P:(kb + 1) * P], ident)
                    mm.then_inc(s_pt, 1)

                def values(a):
                    (s, b, h), u = units[a], a0 + a
                    pe.wait_ge(s_ptc, u + 1)
                    if u:
                        pe.wait_ge(s_oc, u)
                    if h == 0 and u:
                        pe.wait_ge(s_al, u // NH)
                    g = h // QC
                    kbs = range(4) if s == 0 else range(2)
                    for kb in kbs:
                        mm = pe.matmul(bank[7][:, h * HD:(h + 1) * HD], PT[:, a % 2, kb, :],
                                       V[:, (0 if s == 0 else LB) + kb, g * HD:(g + 1) * HD],
                                       start=kb == 0, stop=kb == kbs[-1])
                    mm.then_inc(s_pv, 1)

                def att_t(j):
                    T = qb0[l] + j
                    pe.wait_ge(s_oc, NH * (T + 1))
                    for cc in range(QC):
                        mm = pe.transpose(bank[7][:, cc * P:(cc + 1) * P], att[:, cc * P:(cc + 1) * P], ident)
                    mm.then_inc(s_at, 1)

                def filler(g):
                    n, t = n0 + g // nb, g % nb
                    if t == 0:
                        pe.wait_ge(s_lo, split_of[n] + 1)
                    half, i = g // (2 * nb), (g // nb) % 2
                    if i == 0 and half == 0:
                        pe.wait_ge(s_pin, qb0[l] + t + 1)
                    if i == 0 and half == 1:
                        pe.wait_ge(s_g0, (0 if l == 0 else 8) + t + 1)
                    hi, lo = hT(4 * i, t)
                    group(split_of[n] % 3, 4, 512, bank[t][:, :], hi, lo, i == 0, i == 1)

                for a in range(len(units) + 1):
                    if a < len(units):
                        scores(a)
                    if a:
                        probs_t(a - 1)
                    if a % NH == 1 and a > NH:
                        att_t(a // NH - 1)
                    if a % 2 == 0 and a < len(units):
                        filler(a // 2)
                    if a:
                        values(a - 1)
                att_t(nb - 1)

                def br(j, t):
                    return brh[:, j, t * P:(t + 1) * P], brl[:, j, t * P:(t + 1) * P]

                g0 = 0 if l == 0 else 8

                def branch(n, free):
                    pe.wait_ge(s_lo, split_of[n] + 1)
                    for t in range(nb):
                        free(t)
                        group(split_of[n] % 3, 4, 512, bank[t][:, :], lambda j: br(j, t)[0], lambda j: br(j, t)[1], True, True)

                pe.wait_ge(s_al, qb0[l] + nb)
                branch(first[f"ao0.{l}"], lambda t: pe.wait_ge(s_g0, g0 + nb + t + 1))
                mid = MODS_MID[l]
                if mid[0]:
                    mod_rows(mid[0])
                branch(first[f"ao1.{l}"], lambda t: pe.wait_ge(s_ao, g0 + t + 1))
                if mid[0]:
                    mod_t(mid[0])

                def pooled(g):
                    if g >= 2:
                        pe.wait_ge(s_plc, NG * l + g - 1)
                    for s in range(streams):
                        for b in range(LB):
                            mm = pe.matmul(bank[4 + g % 2][:, s * L:(s + 1) * L], pin[:, s * LB + b, g * P:(g + 1) * P],
                                           poolM[:, b, g, :], start=b == 0, stop=b == LB - 1)
                    mm.then_inc(s_pl, 1)

                def mixed(g):
                    pe.wait_ge(s_plc, NG * l + g + 1)
                    if g < 2:
                        if mid[0]:
                            pe.wait_ge(s_md, mid[0][1] + 1)
                    else:
                        pe.wait_ge(s_mxl, NG * l + g - 1)
                    pe.matmul(bank[6 + g % 2][:, 0:nb * P], poolW[:, g, :], pooledT[:, 0:nb * P],
                              start=True, stop=True).then_inc(s_mx, 1)

                pe.wait_ge(s_pin, qb0[l] + nb)
                pe.wait_ge(s_poolw, 16 * (l + 1))
                pe.wait_ge(s_poolm, 16)
                pooled(0)
                for g in range(NG):
                    if g + 1 < NG:
                        pooled(g + 1)
                    mixed(g)
                for h in range(2):
                    free = ((lambda t: pe.wait_ge(s_ao, g0 + nb + t + 1)) if h == 0 else
                            (lambda t: pe.wait_ge(s_po, g0 + t + 1)))
                    project(first[f"g1n{h}.{l}"], nb, free)
                    if h == 0:
                        pe.wait_ge(s_mxl, NG * (l + 1))
                    if h and mid[2]:
                        mod_t(mid[2])
                    if mid[1 + 2 * h]:
                        mod_rows(mid[1 + 2 * h])
                    branch(first[f"po{h}.{l}"], lambda t: pe.wait_ge(s_g1, g0 + h * nb + t + 1))
                    if mid[1 + 2 * h]:
                        mod_t(mid[1 + 2 * h])
                    if h == 0 and mid[2]:
                        mod_rows(mid[2])
                for k in range(KT):
                    if k >= 2:
                        pe.wait_ge(s_mgl, KT * l + k - 1)
                    for t in range(nb):
                        if k in (0, 4):
                            pe.wait_ge(s_mg, g0 + (k // 4) * nb + t + 1)
                        mm = pe.transpose(bank[4 + k % 2][:, t * P:(t + 1) * P], A[:, t, k * P:(k + 1) * P], ident)
                    mm.then_inc(s_mgt, 1)
                pe.wait_ge(s_mgl, KT * (l + 1))
                project(first[f"o0.{l}"], nb)
                project(first[f"o1.{l}"], nb, lambda t: pe.wait_ge(s_y, g0 + t + 1))
                if mid[3]:
                    pe.wait_ge(s_md, mid[3][1] + 1)
                gain_rows(4 * l + 1, streams)
                pe.wait_ge(s_y, g0 + 2 * nb)
                mod_run(MODS_GAP[4 * l + 1])
                pe.wait_ge(s_ys, 2 * xu_at[4 * l + 2])
                build(4 * l + 2, 2 * l + 1)
                pe.wait_ge(s_h, KT * (2 * l + 2))
                if l == 0:
                    mod_t(MODS_BUILD[1][1])
                    pe.wait_ge(s_md, MCH + 4)

                    def hidden_t(t, f, tiles):
                        pe.wait_ge(s_hid, t + 1 + f * 4)
                        if t >= 2:
                            pe.wait_ge(s_h2l, t - 1 + f * 4)
                        for j in range(tiles):
                            mm = pe.transpose(bank[4 + t % 2][:, j * P:(j + 1) * P], sg[:, t, j * P:(j + 1) * P], ident)
                        mm.then_inc(s_ht, 1)

                    def h2(t):
                        return (lambda j: h2h[:, t, j, :]), (lambda j: h2l[:, t, j, :])

                    with pe.Fori(0, FFULL) as f:
                        for j in range(4):
                            pe.wait_ge(s_lo, SF + j + 1 + f * 6)
                            for t in range(4):
                                if j == 2:
                                    pe.wait_ge(s_si, t + 1 + f * 4)
                                if j == 3 and t == 2:
                                    hidden_t(0, f, 4)
                                if j == 3 and t == 3:
                                    hidden_t(1, f, 4)
                                hi, lo = hT(4 * (j % 2), t)
                                group((SF + j) % 3, 4, 512, bank[t][:, :], hi, lo, j % 2 == 0, j % 2 == 1)
                        for h in range(2):
                            pe.wait_ge(s_lo, SF + 4 + h + 1 + f * 6)
                            for t in range(4):
                                q = 4 * h + t
                                if h == 0:
                                    pe.wait_ge(s_h2l, t + 1 + f * 4)
                                pe.wait_ge(s_da, (q if q >= 2 else 1) + f * 8)
                                hi, lo = h2(t)
                                group((SF + 4 + h) % 3, 4, 512, bank[6 + q % 2][:, :], hi, lo, True, True)
                                if h == 0 and t < 2:
                                    hidden_t(2 + t, f, 4)
                    n = FN + 6 * FFULL
                    project(n, 4)
                    project(n + 1, 4, lambda t: pe.wait_ge(s_si, 4 * FFULL + t + 1))
                    for t in range(4):
                        hidden_t(t, FFULL, FREM // P)
                    pe.wait_ge(s_lo, split_of[n + 2] + 1)
                    for q in range(8):
                        t, h = q // 2, q % 2
                        pe.wait_ge(s_h2l, 4 * FFULL + t + 1)
                        pe.wait_ge(s_da, 8 * FFULL + max(q, 1))
                        hi, lo = h2(t)
                        group(split_of[n + 2] % 3, FREM // P, D, bank[6 + q % 2][:, :], hi, lo, True, True, col=h * 512, w=512)
                    pe.wait_ge(s_h2l, H0)
                    pe.wait_ge(s_da, 8 * FFULL + 9)
                    gain_rows(3, streams)
                    mod_run(MODS_GAP[3])
                    pe.wait_ge(s_ys, 16)

            pe.wait_ge(s_wrl, 1)
            pe.wait_ge(s_md, MCH * DEPTH)
            for b in range(LB):
                for k in range(KT):
                    hi, lo = hTh[:, k, b * P:(b + 1) * P], hTl[:, k, b * P:(b + 1) * P]
                    o = bank[0][:, b * NE:(b + 1) * NE]
                    product(o, hi, lo, wrh[:, k, :], wrl[:, k, :], k == 0, False)
                    mm = pe.matmul(o, lo, wrl[:, k, :], start=False, stop=k == KT - 1)
            mm.then_inc(s_lg, 1)
            pe.wait_ge(s_rt, R_SEL)
            tri = K[:, K_TRI:K_TRI + P]
            s0, s1 = route[:, SEL:SEL + NE], route[:, SEL + NE:SEL + 2 * NE]
            pe.matmul(bank[1][:, 0:NE], tri, s0, start=True, stop=True)
            pe.matmul(bank[1][:, NE:2 * NE], tri, s1, start=True, stop=False)
            pe.matmul(bank[1][:, NE:2 * NE], ones[:, :], s0, start=False, stop=True)
            pe.matmul(bank[1][:, 2 * NE:3 * NE], ones[:, :], s0, start=True, stop=False)
            pe.matmul(bank[1][:, 2 * NE:3 * NE], ones[:, :], s1, start=False, stop=True).then_inc(s_cnt, 1)

            def gather(E, added):
                pe.wait_ge(s_gat, 2 + E * 2)
                pe.wait_ge(s_sca, added)
                for k in range(KT):
                    for t in range(LB):
                        mm = pe.matmul(bank[2 + k // 4][:, (k % 4) * P:(k % 4 + 1) * P], A[:, t, k * P:(k + 1) * P],
                                       Gat[:, t, :], start=t == 0, stop=t == LB - 1)
                    if k % 4 == 3:
                        mm.then_inc(s_xg, 1)

            def gate_up(E, f, p0):
                for j in range(4):
                    pe.wait_ge(s_lo, SN + p0 + j + 1 + E * XU + f * 6)
                    k0 = 4 * (j % 2)
                    group((p0 + j) % 3, 4, 512, bank[j // 2][:, :], lambda i: xgh[:, k0 + i, :],
                          lambda i: xgl[:, k0 + i, :], j % 2 == 0, j % 2 == 1)

            def first_slice(E):
                pe.wait_ge(s_xgl, E + 1)
                gate_up(E, 0, 0)

            def expert(b, e, last):
                E = e + b * NE

                def hidden_t(f):
                    pe.wait_ge(s_hid, H0 + 1 + E * XS + f)
                    for j in range(4):
                        mm = pe.transpose(bank[4][:, j * P:(j + 1) * P], sgm[:, j * P:(j + 1) * P], ident)
                    mm.then_inc(s_ht, 1)

                def down(f, p0, start, stop):
                    for h in range(2):
                        pe.wait_ge(s_lo, SN + p0 + h + 1 + E * XU + f * 6)
                        if h == 0:
                            pe.wait_ge(s_h2l, H0 + E * XS + f)
                        group((p0 + h) % 3, 4, 512, bank[6 + h][:, :],
                              lambda i: h2hm[:, i, :], lambda i: h2lm[:, i, :], start, stop)

                pe.wait_ge(s_gsc, 4 + E * 4)
                for t in range(LB):
                    mm = pe.transpose(bank[5][:, t * P:(t + 1) * P], Gsc[:, t, :], ident)
                mm.then_inc(s_gst, 1)
                hidden_t(0)
                gate_up(E, 1, -2)
                down(1, 2, True, False)
                if not last:
                    gather(E + 1, 1 + E * 4)
                hidden_t(1)
                with pe.Fori(2, XS) as f:
                    gate_up(E, f, -2)
                    down(f, 2, False, False)
                    hidden_t(f)
                down(XS, -2, False, True)
                if not last:
                    first_slice(E + 1)
                pe.wait_ge(s_gsc2, E + 1)
                pe.wait_ge(s_ysl, 2 + E * 2)
                if not last:
                    pe.wait_ge(s_xgm, KT * 2 + E * KT)
                for q in range(2 * LB):
                    t, h = q // 2, q % 2
                    pe.wait_ge(s_sca, (q if q >= 2 else 1) + E * 4)
                    pe.matmul(bank[2 + q % 2][:, :], Sct[:, t * P:(t + 1) * P], yslot[:, h * 512:(h + 1) * 512],
                              start=True, stop=True).then_inc(s_sc, 1)

            def expert_pass(b):
                gather(b * NE, 1 + b * NE * 4)
                first_slice(b * NE)
                with pe.Fori(0, NE - 1) as e:
                    expert(b, e, False)
                expert(b, NE - 1, True)

            expert_pass(0)
            pe.wait_ge(s_flag, 1)
            with pe.If(pe.value_load(route[0:1, FLAG:FLAG + 1].bitcast(I32), min_val=0, max_val=1) > 0):
                expert_pass(1)
            pe.wait_ge(s_h2l, H0 + XS * NE)
            gain_rows(7, 1)


_INS = ["x", "c", "ctx", "c_ctx", "w_mod", "b_mod", "norm_g", "w_in", "sinks", "w_att_o", "pool_w", "pool_scale",
        "w_pool_o", "w_out", "w_ffn_gate", "w_ffn_up", "w_ffn_down", "w_router", "b_router",
        "w_exp_gate", "w_exp_up", "w_exp_down"]


def kernel(**inputs):
    import numpy as _np
    import concourse.bacc as _bacc
    from concourse import mybir as _mybir
    from concourse.bass_utils import run_bass_kernel_spmd as _run

    nc = _bacc.Bacc("TRN2", target_bir_lowering=False, num_devices=1)
    k_const, k_pool = constants()
    given = {name: inputs[name] for name in _INS}
    given.update(k_const=k_const, k_pool=k_pool)
    arrays, args = {}, []
    for name, a in given.items():
        a = _np.ascontiguousarray(a)
        arrays[f"in_{name}_dram"] = a
        args.append(nc.dram_tensor(f"in_{name}_dram", a.shape, _mybir.dt.from_np(a.dtype), kind="ExternalInput").ap())
    args.append(nc.dram_tensor("out_0_dram", (1, L, D), _mybir.dt.float32, kind="ExternalOutput").ap())
    backbone(nc, *args)
    r = _run(nc, [arrays], core_ids=[0])
    return r.results[0]["out_0_dram"]
```

```python
from contextlib import ExitStack

import numpy as np
import concourse.bass as bass
from concourse import mybir

F32 = mybir.dt.float32
F32R = mybir.dt.float32r
I32 = mybir.dt.int32
BF16 = mybir.dt.bfloat16
ALU = mybir.AluOpType
ACT = mybir.ActivationFunctionType
AX_X = mybir.AxisListType.X

P = 128
D = 1024
KT = D // P
L = 256
LB = L // P
DEPTH = 2
HD, NH, NKV = 64, 8, 2
QC = NH // NKV
ATT = NH * HD
GRID_W, ROPE_BASE, WINDOW = 64, 10000.0, 128
POOL_WINDOWS = (2, 4, 8, 16)
NG = len(POOL_WINDOWS)
N_MOD = 6
MCH = N_MOD * D // 512
MT = N_MOD * KT
D_FF, D_EXP, NE = 2816, 3584, 8
EPS, NEG = 1e-6, -1e30
FFULL = D_FF // 512
FREM = D_FF - FFULL * 512
XS = D_EXP // 512
XU = 6 * XS
KVC, PC, GC = ATT, ATT + 2 * NKV * HD, ATT + 2 * NKV * HD + 512
(LG, T1, T2, RK, RK2, F1, F2, SEL, M8, DIF, EXD, DNR, W1, W2, CW, POS, POSM, CNT, FLAG, CURG, CURS, CURW) = np.cumsum(
    [0, 16, 128, 128, 16, 16, 16, 16, 16, 16, 2, 2, 2, 2, 2, 16, 16, 16, 8, 2, 2, 2]).tolist()

V_G, V_PS, V_BM = 2 * KT, 2 * KT + DEPTH * 4 * KT, 2 * KT + DEPTH * 4 * KT + DEPTH * NG
V_ALL = V_BM + DEPTH * MT
K_ID, K_TRI, K_IO, K_JLT, K_COS, K_SIN, K_MASK = 0, 128, 256, 384, 448, 576, 704
K_ALL = K_MASK + LB * L


def constants():
    k = np.zeros((P, K_ALL), np.float32)
    k[:, K_ID:K_ID + P] = np.eye(P)
    k[:, K_TRI:K_TRI + P] = np.triu(np.ones((P, P)), 1)
    k[:, K_IO:K_IO + P] = np.arange(P)[None]
    k[:, K_JLT:K_JLT + NE * NE] = (np.arange(NE)[None, :] < np.arange(NE)[:, None]).astype(np.float32).reshape(1, -1)
    half = HD // 4
    freqs = (ROPE_BASE ** (-np.arange(half, dtype=np.float32) / half)).astype(np.float32)
    t = np.arange(L)
    for b in range(LB):
        pos = t[b * P:(b + 1) * P]
        for axis, at in enumerate((pos // GRID_W, pos % GRID_W)):
            ang = at.astype(np.float32)[:, None] * freqs[None]
            c0 = K_COS + b * HD + axis * 2 * half
            s0 = K_SIN + b * HD + axis * 2 * half
            k[:, c0:c0 + 2 * half] = np.tile(np.cos(ang), 2)
            k[:, s0:s0 + 2 * half] = np.concatenate([-np.sin(ang), np.sin(ang)], 1)
        far = np.abs(pos[:, None] - t[None, :]) > WINDOW
        k[:, K_MASK + b * L:K_MASK + (b + 1) * L] = np.where(far, NEG, 0.0)
    pool = np.zeros((P, LB, NG, L), np.float32)
    for g, w in enumerate(POOL_WINDOWS):
        lo, hi = np.clip(t - w // 2, 0, L), np.clip(t + w // 2, 0, L)
        m = ((t[:, None] >= lo[None]) & (t[:, None] < hi[None])) / (hi - lo)[None] - np.eye(L)
        pool[:, :, g, :] = m.reshape(LB, P, L).transpose(1, 0, 2)
    return k, pool.reshape(P, -1)


MODS_FIRST = [(0, m) for m in range(4)]
MODS_BUILD = {0: [(0, 4), (0, 5)], 1: [(1, 2), (1, 3)], 2: [(1, 8), (1, 9)], 3: []}
MODS_MID = [[(0, 6), (0, 7), (0, 8), (0, 9)], [None] * 4]
MODS_SPLIT = MODS_MID[0][:3]
MODS_GAP = {1: [(0, 10), (0, 11), (1, 0), (1, 1)], 3: [(1, 4), (1, 5), (1, 6), (1, 7)], 5: [(1, 10), (1, 11)]}


def weight_plan(w):
    plan = []

    def piece(name, src, rows, width, groups):
        plan.append((name, src.rearrange("(j p) n -> p j n", p=P), rows, width, groups))

    def pair(name, m, c, groups):
        for k0 in (0, 4):
            piece(name, m[k0 * P:(k0 + 4) * P, c:c + 512], 4, 512, groups)

    def mods(chunks):
        for chunk in chunks:
            if chunk:
                pair(f"m{chunk[1]}.{chunk[0]}", w["w_mod"][chunk[0]], chunk[1] * 512, 1)

    for l in range(DEPTH):
        nb = 2 * LB if l + 1 < DEPTH else LB
        wi = w["w_in"][l]
        mid = MODS_MID[l]
        if l == 0:
            mods(MODS_FIRST)
        mods(MODS_BUILD[2 * l])
        pair(f"q.{l}", wi, 0, nb)
        piece(f"kv.{l}", wi[:, KVC:PC], 8, 256, 2 * LB)
        pair(f"p.{l}", wi, PC, nb)
        pair(f"g0n0.{l}", wi, GC, nb)
        pair(f"g0n1.{l}", wi, GC + 512, nb)
        for n in range(2):
            if n == 0:
                mods(mid[0:1])
            piece(f"ao{n}.{l}", w["w_att_o"][l][:, n * 512:(n + 1) * 512], 4, 512, nb)
        for n in range(2):
            pair(f"g1n{n}.{l}", wi, GC + D + n * 512, nb)
            if n == 0:
                mods(mid[1:2])
            piece(f"po{n}.{l}", w["w_pool_o"][l][:, n * 512:(n + 1) * 512], 4, 512, nb)
            mods(mid[2 + n:3 + n])
        for n in range(2):
            pair(f"o{n}.{l}", w["w_out"][l], n * 512, nb)
        mods(MODS_GAP[4 * l + 1])
        mods(MODS_BUILD[2 * l + 1])
        if l == 0:
            for f in range(FFULL):
                c = f * 512
                pair(f"fg{f}", w["w_ffn_gate"][0], c, nb)
                pair(f"fu{f}", w["w_ffn_up"][0], c, nb)
                for n in range(2):
                    piece(f"fd{f}.{n}", w["w_ffn_down"][0][c:c + 512, n * 512:(n + 1) * 512], 4, 512, nb)
            c = FFULL * 512
            piece("fgr", w["w_ffn_gate"][0][:, c:], 8, FREM, nb)
            piece("fur", w["w_ffn_up"][0][:, c:], 8, FREM, nb)
            piece("fdr", w["w_ffn_down"][0][c:, :], 2, D, 2 * nb)
            mods(MODS_GAP[3])
    return plan


def backbone(nc, x, c, ctx, c_ctx, w_mod, b_mod, norm_g, w_in, sinks, w_att_o, pool_w, pool_scale,
             w_pool_o, w_out, w_ffn_gate, w_ffn_up, w_ffn_down, w_router, b_router,
             w_exp_gate, w_exp_up, w_exp_down, k_const, k_pool, out):
    plan = weight_plan(dict(w_mod=w_mod, w_in=w_in, w_att_o=w_att_o, w_pool_o=w_pool_o, w_out=w_out,
                            w_ffn_gate=w_ffn_gate, w_ffn_up=w_ffn_up, w_ffn_down=w_ffn_down))
    NU = len(plan)
    assert NU % 3 == 0
    first = {}
    before = [0]
    for n, (name, _, _, _, groups) in enumerate(plan):
        first.setdefault(name, n)
        before.append(before[-1] + groups)
    GM = before[NU]
    FN = first["fg0"]
    split_mods = [f"m{m}.{l}" for l, m in MODS_SPLIT]
    split_pieces = [n for n, pc in enumerate(plan) if pc[0][0] != "m" or pc[0] in split_mods]
    split_of = {n: s for s, n in enumerate(split_pieces)}
    SN = len(split_pieces)
    assert SN % 3 == 0
    SF = split_of[FN]

    def load_key(n):
        if n in split_of:
            return split_of[n], 1, n
        return (0 if n < first["q.0"] else sum(m < n for m in split_pieces) + 2), 0, n

    load_order = sorted(range(NU), key=load_key)
    load_of = {n: i for i, n in enumerate(load_order)}
    LF = load_of[first["fu0"]]

    es = ExitStack()
    with es:
        def sb(name, shape, dt=F32):
            return es.enter_context(nc.sbuf_tensor(name, shape, dt))

        raw = [sb(f"raw{i}", [P, 2048]) for i in range(3)]
        whi = [sb(f"whi{i}", [P, 2048], F32R) for i in range(3)]
        wlo = [sb(f"wlo{i}", [P, 2048], F32R) for i in range(3)]
        X = sb("X", [P, 2 * LB, D])
        K = sb("K", [P, K_ALL])
        ones = sb("ones", [P, P])
        VT = sb("VT", [P, V_ALL])
        csil = sb("csil", [P, KT, 2])
        cst = sb("cst", [P, KT, 4], F32R)
        csz = sb("csz", [P, KT, 4], F32R)
        sel4 = sb("sel4", [4, 2])
        modT = sb("modT", [P, MT, 2])
        SC = [sb(f"SC{i}", [P, KT, 2]) for i in range(2)]
        GG = [sb(f"GG{i}", [P, KT, 2]) for i in range(2)]
        ssq = sb("ssq", [P, 4])
        sdev = sb("sdev", [P, 4])
        rstd = sb("rstd", [P, 4])
        epst = sb("epst", [P, 1])
        identb = sb("identb", [P, P], BF16)
        maskb = sb("maskb", [P, LB * L], BF16)
        sinkB = sb("sinkB", [P, DEPTH * NH])
        nsink = sb("nsink", [P, DEPTH * NH])
        brB = sb("brB", [P, NE])
        negmax0 = sb("negmax0", [P, 2])
        negmax = sb("negmax", [P, 2])
        psumP = sb("psumP", [P, 2])
        esink = sb("esink", [P, 2])
        den = sb("den", [P, 2])
        rden = sb("rden", [P, 2])

        arena_kb = 106
        base = -(-nc.sbuf_base // 32) * 32
        arena = sb("arena", [P, arena_kb * 256])

        def at(name, kb, shape, dt=F32):
            return nc.alloc_sbuf_tensor_at(name, shape, dt, offset=base + int(kb * 1024))

        hTh = at("hTh", 0, [P, KT, 512], F32R)
        hTl = at("hTl", 16, [P, KT, 512], F32R)
        A = at("A", 32, [P, 2 * LB, D])
        rope1 = at("rope1", 32, [P, 512])
        rope2 = at("rope2", 34, [P, 512])
        qrot = at("qrot", 36, [P, 2 * LB, 512])
        krot = at("krot", 44, [P, 2 * LB, P])
        r1 = 48
        pin = at("pin", r1, [P, 2 * LB, 512])
        qT = at("qT", r1 + 8, [P, QC, 512])
        diag = at("diag", r1 + 8, [P, 2, KT, P])
        brh = at("brh", r1 + 16, [P, 4, 512], F32R)
        brl = at("brl", r1 + 24, [P, 4, 512], F32R)
        poolM = at("poolM", r1 + 32, [P, LB, NG, L])
        kT = at("kT", r1 + 40, [P, 512])
        V = at("V", r1 + 42, [P, 2 * LB, P])
        Pb = at("Pb", r1 + 45, [P, 2, 512])
        modrow = at("modrow", r1 + 40, [4, 2, 512])
        hmod = at("hmod", r1 + 45, [P, 2, 512])
        PT = at("PT", r1 + 49, [P, 2, 4, P])
        junk = at("junk", r1 + 49, [P, D])
        pooledT = at("pooledT", r1 + 53, [P, 512])
        att = at("att", r1 + 53, [P, ATT])
        poolW = at("poolW", r1 + 55, [P, NG, P])
        vst = at("vst", r1 + 16, [P, 2, P])
        sg = at("sg", r1, [P, 2 * LB, 512])
        h2h = at("h2h", r1 + 16, [P, 2 * LB, 4, P], F32R)
        h2l = at("h2l", r1 + 24, [P, 2 * LB, 4, P], F32R)
        rawm = raw + [at(f"raw{3 + i}", r1 + 16 + 8 * i, [P, 2048]) for i in range(3)]
        wr = at("wr", r1 + 57, [P, KT, NE])
        wrs = at("wrs", r1 + 44, [P, KT, 2, NE], F32R)
        yacc = A[:, LB:2 * LB, :]
        xgm = at("xgm", 0, [P, KT, P])
        xgh = at("xgh", r1, [P, KT, P], F32R)
        xgl = at("xgl", r1 + 4, [P, KT, P], F32R)
        yslot = at("yslot", r1 + 40, [P, D])
        sgm = at("sgm", 4, [P, 512])
        h2hm = at("h2hm", 8, [P, 4, P], F32R)
        h2lm = at("h2lm", 10, [P, 4, P], F32R)
        Gat = at("Gat", 12, [P, LB, P])
        Gsc = at("Gsc", 13, [P, LB, P])
        Sct = at("Sct", 14, [P, LB * P])
        route = at("route", r1 + 53, [P, 1024])

        bank = [es.enter_context(nc.psum_tensor(f"bank{i}", [P, 512], F32)) for i in range(8)]

        def sem(name):
            return es.enter_context(nc.semaphore(name))

        s_small = sem("small_in")
        s_const = sem("const_in")
        s_rows = sem("broadcast_rows_in")
        s_x = [sem("x_in"), sem("ctx_in")]
        s_poolw = sem("poolw_in")
        s_poolm = sem("poolm_in")
        s_route_in = sem("router_in")
        s_raw = [sem(f"raw_full{i}") for i in range(6)]
        s_hi = sem("hi_done")
        s_lo = sem("lo_done")
        s_mm = sem("mm_done")
        s_ini = sem("ini")
        s_vt = sem("vt")
        s_vtc = sem("vt_copied")
        s_csil = sem("csil")
        s_csh = sem("csil_high")
        s_cs = sem("csil_split")
        s_mrow = sem("modrow_ready")
        s_mt = sem("modT_psum")
        s_md = sem("modT_ready")
        s_col = sem("columns_ready")
        s_sq = sem("squares")
        s_sd = sem("sdev_ready")
        s_rs = sem("rstd_ready")
        s_xn = sem("xn_ready")
        s_tr = sem("xn_transposed")
        s_hm = sem("hmod_ready")
        s_hh = sem("h_high")
        s_h = sem("h_ready")
        s_r = sem("rope_steps")
        s_qr = sem("q_rotated")
        s_qt = sem("q_transposed")
        s_qk = sem("qT_copied")
        s_kr = sem("k_rotated")
        s_kt = sem("k_transposed")
        s_v = sem("v_copied")
        s_pin = sem("pool_in_copied")
        s_g0 = sem("gate0_copied")
        s_g0s = sem("gate0_sigmoid")
        s_s = sem("scores_ready")
        s_nm0 = sem("rowmax")
        s_nm = sem("negmax_ready")
        s_e = sem("exp_ready")
        s_es = sem("sink_exp")
        s_dn = sem("den_steps")
        s_pt = sem("probs_transposed")
        s_ptc = sem("probsT_copied")
        s_pv = sem("att_ready")
        s_oc = sem("att_scaled")
        s_at = sem("att_transposed")
        s_ah = sem("att_high")
        s_al = sem("att_low")
        s_ao = sem("att_gated")
        s_pl = sem("pooled")
        s_plc = sem("pooled_copied")
        s_mx = sem("pool_mixed")
        s_mxh = sem("pool_high")
        s_mxl = sem("pool_low")
        s_g1 = sem("gate1_sigmoid")
        s_po = sem("pool_gated")
        s_mg = sem("merged")
        s_mgt = sem("merged_transposed")
        s_mgh = sem("merged_high")
        s_mgl = sem("merged_low")
        s_y = sem("y_copied")
        s_dg = sem("diag_ready")
        s_gb = sem("gain_rows")
        s_ys = sem("y_scaled")
        s_xu = sem("x_updated")
        s_si = sem("silu_ready")
        s_hid = sem("hidden_ready")
        s_ht = sem("hidden_transposed")
        s_h2h = sem("hidden_high")
        s_h2l = sem("hidden_low")
        s_da = sem("down_added")
        s_wr = sem("router_high")
        s_wrl = sem("router_low")
        s_lg = sem("logits_psum")
        s_rt = sem("router_steps")
        s_rx = sem("router_exp")
        s_cnt = sem("counts_psum")
        s_flag = sem("flag_ready")
        s_gat = sem("gather_matrix")
        s_gsc = sem("scatter_weights")
        s_gst = sem("scatter_transposed")
        s_gsc2 = sem("scatter_copied")
        s_cur = sem("expert_columns")
        s_xg = sem("gathered")
        s_xgm = sem("gathered_modulated")
        s_xgh = sem("gathered_high")
        s_xgl = sem("gathered_low")
        s_ysl = sem("yslot_copied")
        s_sc = sem("scattered")
        s_sca = sem("scatter_added")
        s_moe = sem("experts_done")
        s_out = sem("out_stored")

        block = es.enter_context(nc.Block())

        ident = K[:, K_ID:K_ID + P]

        hm_at = [0, 16, 32, 48]
        col_of = [1, 3, 5, 7]
        gb_at = {1: 0, 3: 2, 5: 4, 7: 5}
        R_SEL = 13
        R_DIF = 5
        H0 = 4 * (FFULL + 1)

        def blocks(l):
            return 2 * LB if l + 1 < DEPTH else LB

        def units_of(l):
            return [(s, b, h) for s in range(blocks(l) // LB) for b in range(LB) for h in range(NH)]

        att0 = [0, len(units_of(0))]
        qb0 = [0, 2 * LB]
        norm_nb = [4, 4, 4, 4, 4, 2, 2, 2]
        norm_at = [sum(norm_nb[:i]) for i in range(9)]
        xu_at = [0, 0, 4, 4, 8, 8, 10, 10]
        xn_at = [0, 0, 4, 4, 8, 8, 12, 12]

        gap_mods = {MCH * l + m for chunks in MODS_GAP.values() for l, m in chunks}

        def mod_bank(M):
            return bank[M % 2 if M in gap_mods else 6 + M % 2]

        @block.sync
        def _(sp):
            def slot_free(i):
                n = load_order[i]
                if n in split_of:
                    sp.wait_ge(s_lo, split_of[n] + 1)
                else:
                    sp.wait_ge(s_mm, before[n + 1])

            sp.dma_start(K[:, :], k_const).then_inc(s_const, 16)
            sp.dma_start(vst[0:KT, 0, :], c[0].rearrange("(k p) -> k p", p=P)).then_inc(s_small, 16)
            sp.dma_start(vst[KT:2 * KT, 0, :], c_ctx.rearrange("(k p) -> k p", p=P)).then_inc(s_small, 16)
            sp.dma_start(vst[V_G:V_PS, 0, :], norm_g.rearrange("l i (k p) -> (l i k) p", p=P)).then_inc(s_small, 16)
            sp.dma_start(vst[V_PS:V_BM, 0, :], pool_scale.rearrange("l (g p) -> (l g) p", p=P)).then_inc(s_small, 16)
            sp.dma_start(vst[0:V_ALL - V_BM, 1, :],
                         b_mod.rearrange("l (k p) -> (l k) p", p=P)).then_inc(s_small, 16)
            n = 0
            while n < NU:
                if n == 3:
                    sp.dma_start(X[:, 0:LB, :], x[0].rearrange("(b p) d -> p b d", p=P)).then_inc(s_x[0], 16)
                if n == 5:
                    sp.dma_start(X[:, LB:2 * LB, :], ctx[0].rearrange("(b p) d -> p b d", p=P)).then_inc(s_x[1], 16)
                if n == LF + 6:
                    with sp.Fori(1, FFULL - 1) as f:
                        for j in range(6):
                            s = (LF + j) % 3
                            if j in (2, 3):
                                src = w_ffn_down[0][bass.ds(f * 512, 512), (j % 2) * 512:(j % 2) * 512 + 512]
                            else:
                                m, c0 = (w_ffn_up[0], 0) if j < 2 else (w_ffn_gate[0], 512)
                                src = m[(j % 2) * 512:(j % 2) * 512 + 512, bass.ds(f * 512 + c0, 512)]
                            sp.wait_ge(s_lo, SF + 2 + j - 2 + f * 6)
                            sp.dma_start(raw[s][:, :].rearrange("p (j n) -> p j n", j=4),
                                         src.rearrange("(j p) n -> p j n", p=P)).then_inc(s_raw[s], 16)
                    n += 6 * (FFULL - 2)
                    continue
                _, src, rows, width, _ = plan[load_order[n]]
                if n >= 3:
                    slot_free(n - 3)
                sp.dma_start(raw[n % 3][:, 0:rows * width].rearrange("p (j n) -> p j n", j=rows),
                             src).then_inc(s_raw[n % 3], 16)
                n += 1

            def go(i, slot, src, cold=False):
                if not cold:
                    sp.wait_ge(s_lo, SN - 5 + i)
                sp.dma_start(rawm[slot][:, :].rearrange("p (j n) -> p j n", j=4),
                             src.rearrange("(j p) n -> p j n", p=P)).then_inc(s_raw[slot], 16)

            def up(e, j, f):
                m = (w_exp_gate if j < 2 else w_exp_up)[0].rearrange("e d f -> (e d) f")
                return m[bass.ds(e * D + (j % 2) * 512, 512), bass.ds(f * 512, 512)]

            def down(e, h, f):
                m = w_exp_down[0].rearrange("e f d -> (e f) d")
                return m[bass.ds(e * D_EXP + f * 512, 512), h * 512:h * 512 + 512]

            def expert_loads(b, e, last):
                i0 = XU * NE * b + XU * e
                with sp.Fori(1, XS) as f:
                    for j in range(6):
                        go(i0 + f * 6 + (j - 2), (4 + j) % 6, up(e, j, f) if j < 4 else down(e, j - 4, f - 1))
                for j in range(4, 6) if last else range(6):
                    i = XU - 2 + (j - 4 if last else j)
                    go(i0 + i, i % 6, up(e + 1, j, 0) if j < 4 else down(e, j - 4, XS - 1))

            def pass_loads(b):
                for j in range(4):
                    if b == 0 and j < 3:
                        slot_free(NU - 3 + j)
                    go(XU * NE * b + j, j, up(0, j, 0), b == 0)
                with sp.Fori(0, NE - 1) as e:
                    expert_loads(b, e, False)
                expert_loads(b, NE - 1, True)

            sp.wait_ge(s_mm, before[first["po1.1"] + 1])
            pass_loads(0)
            sp.wait_ge(s_flag, 1)
            with sp.If(sp.value_load(route[0:1, FLAG:FLAG + 1].bitcast(I32), min_val=0, max_val=1) > 0):
                pass_loads(1)
            for t in range(LB):
                sp.wait_ge(s_xu, xu_at[7] + t + 1)
                sp.dma_start(out[0, t * P:(t + 1) * P, :], X[:, t, :]).then_inc(s_out, 16)
            sp.wait_ge(s_out, 16 * LB)

        @block.gpsimd
        def _(pool):
            pool.dma_start(sinkB[:, :],
                           sinks.rearrange("(o l) h -> o (l h)", o=1).to_broadcast([P, DEPTH * NH])).then_inc(s_rows, 16)
            pool.dma_start(brB[:, :], b_router.to_broadcast([P, NE])).then_inc(s_rows, 16)
            pool.dma_start(wr[:, :, :], w_router[0].rearrange("(k p) e -> p k e", p=P)).then_inc(s_route_in, 16)
            for l in range(DEPTH):
                if l:
                    pool.wait_ge(s_mx, NG * l)
                pool.dma_start(poolW[:, :, :], pool_w[l].rearrange("g c d -> c g d")).then_inc(s_poolw, 16)
                if l == 0:
                    pool.dma_start(poolM[:, :, :, :].rearrange("p b g t -> p (b g t)"), k_pool).then_inc(s_poolm, 16)

        @block.scalar
        def _(act):
            def split(s):
                n = split_pieces[s]
                i = load_of[n]
                act.wait_ge(s_raw[i % 3], 16 * (i // 3 + 1))
                if s >= 3:
                    act.wait_ge(s_mm, before[split_pieces[s - 3] + 1])
                w = plan[n][2] * plan[n][3]
                act.activation(whi[s % 3][:, 0:w], raw[i % 3][:, 0:w], ACT.Copy).then_inc(s_hi, 1)

            def ahead(n):
                if split_of[n] + 2 < SN:
                    split(split_of[n] + 2)

            def mod(chunk):
                l, m = chunk
                n, M = first[f"m{m}.{l}"], MCH * l + m
                act.wait_ge(s_mm, before[n + 2])
                if M >= 2:
                    act.wait_ge(s_mt, M - 1)
                rows = 4 if chunk in MODS_SPLIT else 2
                act.activation(modrow[0:rows, M % 2, :], mod_bank(M)[0:rows, :], ACT.Copy).then_inc(s_mrow, 1)

            def ahead_mod(chunk):
                if chunk in MODS_SPLIT:
                    n = first[f"m{chunk[1]}.{chunk[0]}"]
                    ahead(n)
                    ahead(n + 1)

            def squares(i, src):
                nb = norm_nb[i]
                for t in range(nb):
                    if i + t:
                        act.wait_ge(s_sq, norm_at[i] + t)
                    act.activation(junk[:, :], src(t), ACT.Square, accum_out=ssq[:, t:t + 1]).then_inc(s_sq, 1)
                act.wait_ge(s_sq, norm_at[i] + nb)
                if i:
                    act.wait_ge(s_rs, i)
                act.activation(sdev[:, 0:nb], ssq[:, 0:nb], ACT.Sqrt, bias=epst[:, 0:1], scale=1.0 / D).then_inc(s_sd, 1)

            def build(i, bi, streams):
                gap, inside = MODS_GAP.get(i - 1, []), MODS_BUILD[bi]
                for chunk in gap[2:]:
                    mod(chunk)
                for k in range(KT):
                    act.wait_ge(s_hm, hm_at[bi] + streams * (k + 1))
                    w = streams * L
                    act.activation(hTh[:, k, 0:w], hmod[:, k % 2, 0:w], ACT.Copy).then_inc(s_hh, 1)
                    if k == 3 and inside:
                        mod(inside[0])
                    if k == 6 and bi == 0:
                        split(0)

            def norms(i, src):
                squares(i, src)
                mod(MODS_GAP[i][0])
                act.wait_ge(s_xu, xu_at[i + 1])
                squares(i + 1, lambda t: X[:, t, :])
                mod(MODS_GAP[i][1])

            act.wait_ge(s_vtc, 1)
            act.activation(csil[:, :, :].rearrange("p k s -> p s k"), VT[:, 0:2 * KT].rearrange("p (s k) -> p s k", s=2),
                           ACT.Silu).then_inc(s_csil, 1)
            act.wait_ge(s_csil, 1)
            act.activation(cst[:, :, 0:2], csil[:, :, :], ACT.Copy).then_inc(s_csh, 1)
            act.wait_ge(s_ini, 2)
            for chunk in MODS_FIRST[:2]:
                mod(chunk)
            act.wait_ge(s_x[0], 16)
            act.wait_ge(s_x[1], 16)
            squares(0, lambda t: X[:, t, :])
            for chunk in MODS_FIRST[2:]:
                mod(chunk)
            for l in range(DEPTH):
                nb, streams = blocks(l), blocks(l) // LB
                build(4 * l, 2 * l, 2)
                if l == 0:
                    split(1)
                mod(MODS_BUILD[2 * l][1])
                n = first[f"q.{l}"]
                ahead(n)
                ahead(n + 1)
                ahead(first[f"kv.{l}"])
                for t in range(nb):
                    act.wait_ge(s_qt, qb0[l] + t + 1)
                    act.activation(qT[:, :, t * P:(t + 1) * P],
                                   bank[4 + t % 2][:, :].rearrange("p (c t) -> p c t", c=QC), ACT.Copy).then_inc(s_qk, 1)
                act.wait_ge(s_kt, l + 1)
                act.activation(kT[:, :], bank[4][:, :], ACT.Copy).then_inc(s_qk, 1)
                n = first[f"p.{l}"]
                ahead(n)
                ahead(n + 1)
                for t in range(nb):
                    act.wait_ge(s_mm, before[n + 1] + t + 1)
                    act.activation(pin[:, t, :], bank[t][:, :], ACT.Copy).then_inc(s_pin, 1)

                units, a0 = units_of(l), att0[l]
                n0 = first[f"g0n0.{l}"]

                def probs_t(a):
                    act.wait_ge(s_pt, a0 + a + 1)
                    if a0 + a >= 2:
                        act.wait_ge(s_pv, a0 + a - 1)
                    act.activation(PT[:, a % 2, :, :].rearrange("p k t -> p (k t)"), bank[6][:, :],
                                   ACT.Copy).then_inc(s_ptc, 1)

                def att_high(j):
                    T = qb0[l] + j
                    act.wait_ge(s_at, T + 1)
                    act.activation(brh[:, :, j * P:(j + 1) * P], bank[7][:, :].rearrange("p (c t) -> p c t", c=QC),
                                   ACT.Copy).then_inc(s_ah, 1)

                for a in range(len(units) + 1):
                    g = a // 2
                    if a:
                        probs_t(a - 1)
                    if a < len(units):
                        h, u = units[a][2], a0 + a
                        act.wait_ge(s_nm, u + 1)
                        if u >= 2:
                            act.wait_ge(s_dn, 2 * u - 3)
                            act.wait_ge(s_pt, u - 1)
                        kw = 2 * L if units[a][0] == 0 else L
                        act.activation(Pb[:, u % 2, 0:kw], bank[4 + u % 2][:, 0:kw], ACT.Exp,
                                       bias=negmax[:, u % 2:u % 2 + 1], scale=HD ** -0.5,
                                       accum_out=psumP[:, u % 2:u % 2 + 1]).then_inc(s_e, 1)
                        act.activation(esink[:, u % 2:u % 2 + 1], negmax[:, u % 2:u % 2 + 1], ACT.Exp,
                                       bias=sinkB[:, l * NH + h:l * NH + h + 1]).then_inc(s_es, 1)
                    if a % NH == 1 and a > NH:
                        att_high(a // NH - 1)
                    if a % (2 * nb) == 0 and a < len(units):
                        ahead(n0 + g // nb)
                    if a % 2 == 1 and (g // nb) % 2 == 1:
                        t, half = g % nb, g // (2 * nb)
                        act.wait_ge(s_mm, before[n0] + g + 1)
                        act.activation(A[:, t, half * 512:(half + 1) * 512], bank[t][:, :], ACT.Copy).then_inc(s_g0, 1)
                att_high(nb - 1)
                mid = MODS_MID[l]
                ahead_mod(mid[0])
                for t in range(nb):
                    act.wait_ge(s_g0, (0 if l == 0 else 8) + nb + t + 1)
                    act.activation(A[:, t, :], A[:, t, :], ACT.Sigmoid).then_inc(s_g0s, 1)
                ahead(first[f"ao0.{l}"])
                ahead(first[f"ao1.{l}"])
                if mid[0]:
                    mod(mid[0])
                for g in range(NG):
                    act.wait_ge(s_mx, NG * l + g + 1)
                    act.activation(brh[:, g, 0:nb * P], bank[6 + g % 2][:, 0:nb * P], ACT.Copy,
                                   scale=VT[:, V_PS + l * NG + g:V_PS + l * NG + g + 1]).then_inc(s_mxh, 1)
                for half in range(2):
                    n = first[f"g1n{half}.{l}"]
                    if half:
                        ahead_mod(mid[2])
                    ahead(n)
                    if half and mid[2]:
                        mod(mid[2])
                    ahead(n + 1)
                    for t in range(nb):
                        if half:
                            act.wait_ge(s_mg, (0 if l == 0 else 8) + t + 1)
                        act.wait_ge(s_mm, before[n + 1] + t + 1)
                        act.activation(pin[:, t, :], bank[t][:, :], ACT.Sigmoid).then_inc(s_g1, 1)
                    if half == 0 and mid[1]:
                        ahead_mod(mid[1])
                        mod(mid[1])
                    ahead(first[f"po{half}.{l}"])
                for k in range(KT):
                    act.wait_ge(s_mgt, KT * l + k + 1)
                    act.activation(hTh[:, k, 0:nb * P], bank[4 + k % 2][:, 0:nb * P], ACT.Copy).then_inc(s_mgh, 1)
                    if k == 3 and mid[3]:
                        mod(mid[3])
                for half in range(2):
                    n = first[f"o{half}.{l}"]
                    ahead(n)
                    ahead(n + 1)
                act.wait_ge(s_y, (0 if l == 0 else 8) + 2 * nb)
                norms(4 * l + 1, lambda t: A[:, t, :])
                if l + 1 == DEPTH:
                    act.wait_ge(s_route_in, 16)
                    act.activation(wrs[:, :, 0, :], wr[:, :, :], ACT.Copy).then_inc(s_wr, 1)
                build(4 * l + 2, 2 * l + 1, streams)
                if l == 0:
                    mod(MODS_BUILD[1][1])
                    with act.Fori(0, FFULL) as f:
                        def split_f(j):
                            s, i = (SF + j) % 3, LF + j - 2
                            act.wait_ge(s_raw[i % 3], 16 * (i // 3 + 1) + f * 32)
                            act.wait_ge(s_mm, before[FN] + 4 * (j - 2) + f * 24)
                            act.activation(whi[s][:, :], raw[i % 3][:, :], ACT.Copy).then_inc(s_hi, 1)

                        for j in range(6):
                            if j == 2:
                                for t in range(4):
                                    act.wait_ge(s_mm, before[FN] + 4 + t + 1 + f * 24)
                                    act.activation(sg[:, t, :], bank[t][:, :], ACT.Silu).then_inc(s_si, 1)
                            if j == 4:
                                for t in range(2):
                                    act.wait_ge(s_ht, t + 1 + f * 4)
                                    act.activation(h2h[:, t, :, :].rearrange("p j t -> p (j t)"), bank[4 + t][:, :],
                                                   ACT.Copy).then_inc(s_h2h, 1)
                            split_f(j + 2)
                            if j == 4:
                                for t in range(2, 4):
                                    act.wait_ge(s_ht, t + 1 + f * 4)
                                    act.activation(h2h[:, t, :, :].rearrange("p j t -> p (j t)"), bank[2 + t][:, :],
                                                   ACT.Copy).then_inc(s_h2h, 1)
                    n = FN + 6 * FFULL
                    ahead(n)
                    for t in range(4):
                        act.wait_ge(s_mm, before[n] + t + 1)
                        act.activation(sg[:, t, 0:FREM], bank[t][:, 0:FREM], ACT.Silu).then_inc(s_si, 1)
                    ahead(n + 1)
                    for t in range(4):
                        act.wait_ge(s_ht, 4 * FFULL + t + 1)
                        act.activation(h2h[:, t, 0:FREM // P, :].rearrange("p j t -> p (j t)"),
                                       bank[4 + t % 2][:, 0:FREM], ACT.Copy).then_inc(s_h2h, 1)
                    ahead(n + 2)
                    act.wait_ge(s_da, 8 * (FFULL + 1) + 1)
                    norms(3, lambda t: A[:, t, :])

            def split_x(E, j, f):
                act.wait_ge(s_raw[j], 16 * ((NU // 3 if j < 3 else 0) + 1) + E * (16 * XS) + f * 16)
                act.wait_ge(s_mm, GM - 2 + j + E * XU + f * 6)
                act.activation(whi[j % 3][:, :], rawm[j][:, :], ACT.Copy).then_inc(s_hi, 1)

            split_x(0, 0, 0)
            split_x(0, 1, 0)
            act.wait_ge(s_rt, R_DIF)
            act.activation(route[:, EXD:EXD + LB], route[:, DIF:DIF + LB], ACT.Exp).then_inc(s_rx, 1)

            def hidden_x(E, f):
                act.wait_ge(s_ht, H0 + 1 + E * XS + f)
                act.activation(h2hm[:, :, :].rearrange("p j t -> p (j t)"), bank[4][:, :], ACT.Copy).then_inc(s_h2h, 1)

            def modulate(E, half):
                for k in range(half * KT // 2, (half + 1) * KT // 2):
                    act.wait_ge(s_xg, 2 * E + k // 4 + 1)
                    act.activation(xgm[:, k, :], bank[2 + k // 4][:, (k % 4) * P:(k % 4 + 1) * P], ACT.Identity,
                                   bias=modT[:, 3 * KT + k, 0:1], scale=SC[1][:, k, 0:1]).then_inc(s_xgm, 1)

            def gathered(E):
                for half in range(2):
                    gathered_half(E, half)

            def gathered_half(E, half):
                ks = slice(half * KT // 2, (half + 1) * KT // 2)
                act.wait_ge(s_xgm, KT * E + (half + 1) * KT // 2)
                act.activation(xgh[:, ks, :].rearrange("p k t -> p (k t)"),
                               xgm[:, ks, :].rearrange("p k t -> p (k t)"), ACT.Copy).then_inc(s_xgh, 1)

            def output(E, done):
                act.wait_ge(s_mm, GM + done + E * XU)
                for h in range(2):
                    act.activation(yslot[:, h * 512:(h + 1) * 512], bank[6 + h][:, :], ACT.Copy).then_inc(s_ysl, 1)

            def slice_(E, f, out=None, high=None):
                split_x(E, 0, f)
                if out is not None:
                    output(out, XU + 4)
                split_x(E, 1, f)
                act.wait_ge(s_mm, GM + E * XU + f * 6)
                act.activation(sgm[:, :], bank[0][:, :], ACT.Silu).then_inc(s_si, 1)
                for j in range(2, 6):
                    if high is not None and j == 4:
                        act.wait_ge(s_mm, GM + E * XU + f * 6 + 2)
                        gathered(high)
                    split_x(E, j, f)

            def expert(b, e, last):
                E = e + b * NE
                slice_(E, 2)
                hidden_x(E, 2)
                act.wait_ge(s_gst, E + 1)
                act.activation(Sct[:, :], bank[5][:, 0:LB * P], ACT.Copy).then_inc(s_gsc2, 1)
                if not last:
                    modulate(E + 1, 0)
                    modulate(E + 1, 1)
                with act.Fori(3, XS - 1) as f:
                    slice_(E, f)
                    hidden_x(E, f)
                slice_(E, XS - 1, high=None if last else E + 1)
                hidden_x(E, XS - 1)
                if last:
                    output(E, XU)
                else:
                    slice_(E, XS)
                    hidden_x(E, XS)
                    slice_(E, XS + 1, E)
                    hidden_x(E, XS + 1)

            def expert_pass(b):
                E = b * NE
                for half in range(2):
                    modulate(E, half)
                    gathered_half(E, half)
                split_x(E, 2, 0)
                split_x(E, 3, 0)
                act.wait_ge(s_mm, GM + 2 + E * XU)
                act.activation(sgm[:, :], bank[0][:, :], ACT.Silu).then_inc(s_si, 1)
                split_x(E, 4, 0)
                split_x(E, 5, 0)
                hidden_x(E, 0)
                slice_(E, 1)
                hidden_x(E, 1)
                with act.Fori(0, NE - 1) as e:
                    expert(b, e, False)
                expert(b, NE - 1, True)

            expert_pass(0)
            act.wait_ge(s_flag, 1)
            with act.If(act.value_load(route[0:1, FLAG:FLAG + 1].bitcast(I32), min_val=0, max_val=1) > 0):
                split_x(NE, 0, 0)
                split_x(NE, 1, 0)
                expert_pass(1)
            act.wait_ge(s_moe, 1)
            squares(7, lambda t: yacc[:, t, :])

        @block.vector
        def _(dve):
            def split(s):
                n = split_pieces[s]
                dve.wait_ge(s_hi, s + 1)
                w = plan[n][2] * plan[n][3]
                dve.tensor_tensor(wlo[s % 3][:, 0:w], raw[load_of[n] % 3][:, 0:w], whi[s % 3][:, 0:w].bitcast(F32),
                                  ALU.subtract).then_inc(s_lo, 1)

            def ahead(n):
                if split_of[n] + 2 < SN:
                    split(split_of[n] + 2)

            def mod(chunk):
                l, m = chunk
                M = MCH * l + m
                dve.wait_ge(s_mt, M + 1)
                dve.tensor_tensor(modT[:, 4 * m:4 * m + 4, :], mod_bank(M)[:, 0:8].rearrange("p (j s) -> p j s", s=2),
                                  VT[:, V_BM + l * MT + 4 * m:V_BM + l * MT + 4 * m + 4, None].to_broadcast([P, 4, 2]),
                                  ALU.add).then_inc(s_md, 1)

            def ahead_mod(chunk):
                if chunk in MODS_SPLIT:
                    n = first[f"m{chunk[1]}.{chunk[0]}"]
                    ahead(n)
                    ahead(n + 1)

            cols = [0]

            def column(out, j0, l, i, plus):
                dve.wait_ge(s_md, MCH * l + j0 // 4 + 2)
                cols[0] += 1
                g0 = V_G + (l * 4 + i) * KT
                dve.scalar_tensor_tensor(out[:, :, :], modT[:, j0:j0 + KT, :], plus,
                                         VT[:, g0:g0 + KT, None].to_broadcast([P, KT, 2]),
                                         ALU.add, ALU.mult).then_inc(s_col, 1)

            def rms(i):
                dve.wait_ge(s_sd, i + 1)
                dve.reciprocal(rstd[:, 0:norm_nb[i]], sdev[:, 0:norm_nb[i]]).then_inc(s_rs, 1)
                dve.wait_ge(s_rs, i + 1)

            def normalised(i):
                rms(i)
                for t in range(norm_nb[i]):
                    dve.tensor_scalar(A[:, t, :], X[:, t, :], rstd[:, t:t + 1], None, ALU.mult).then_inc(s_xn, 1)

            def build(i, bi, streams, which):
                gap, inside = MODS_GAP.get(i - 1, []), MODS_BUILD[bi]
                for chunk in gap[1:3] if inside else []:
                    mod(chunk)
                if gap and which == 0:
                    column(SC[0], KT, bi // 2, 0, 1.0)
                dve.wait_ge(s_col, col_of[bi])
                for k in range(KT + 1):
                    if k < KT:
                        dve.wait_ge(s_tr, KT * bi + k + 1)
                        if k >= 2:
                            dve.wait_ge(s_h, KT * bi + k - 1)
                        for s in range(streams):
                            dve.tensor_scalar(hmod[:, k % 2, s * L:(s + 1) * L], bank[4 + k % 2][:, s * L:(s + 1) * L],
                                              SC[which][:, k, s:s + 1], modT[:, 24 * which + k, s:s + 1],
                                              ALU.mult, ALU.add).then_inc(s_hm, 1)
                    if k:
                        dve.wait_ge(s_hh, KT * bi + k)
                        w = streams * L
                        dve.tensor_tensor(hTl[:, k - 1, 0:w], hmod[:, (k - 1) % 2, 0:w],
                                          hTh[:, k - 1, 0:w].bitcast(F32), ALU.subtract).then_inc(s_h, 1)
                    if k == 1 and gap[3:]:
                        mod(gap[3])
                    if k == 5 and inside:
                        mod(inside[0])
                    if k == 6 and bi == 0:
                        split(0)
                if gap and not inside:
                    mod(gap[1])

            def gain_diag(which, streams):
                for s in range(streams):
                    dve.tensor_tensor(diag[:, s, :, :], ident[:, None, :].to_broadcast([P, KT, P]),
                                      GG[which][:, :, s:s + 1].to_broadcast([P, KT, P]), ALU.mult).then_inc(s_dg, 1)

            def add_normed(i, src):
                rms(i)
                y0 = 2 * xu_at[i]
                for t in range(norm_nb[i]):
                    dve.wait_ge(s_gb, gb_at[i] + t // LB + 1)
                    for h in range(2):
                        dve.scalar_tensor_tensor(src(t)[:, h * 512:(h + 1) * 512], src(t)[:, h * 512:(h + 1) * 512],
                                                 rstd[:, t:t + 1], bank[4 + 2 * (t // LB) + h][:, :],
                                                 ALU.mult, ALU.mult).then_inc(s_ys, 1)
                    dve.wait_ge(s_ys, y0 + 2 * t + 2)
                    dve.tensor_tensor(X[:, t, :], X[:, t, :], src(t), ALU.add).then_inc(s_xu, 1)

            dve.memset(ones[:, :], 1.0).then_inc(s_ini, 1)
            dve.memset(epst[:, :], EPS).then_inc(s_ini, 1)
            dve.wait_ge(s_vt, 1)
            dve.tensor_copy(VT[:, 0:V_BM], bank[4][:, 0:V_BM]).then_inc(s_vtc, 1)
            dve.wait_ge(s_vt, 2)
            dve.tensor_copy(VT[:, V_BM:V_ALL], bank[5][:, 0:V_ALL - V_BM]).then_inc(s_vtc, 1)
            dve.wait_ge(s_vtc, 2)
            dve.wait_ge(s_const, 16)
            dve.wait_ge(s_rows, 32)
            dve.tensor_scalar(nsink[:, :], sinkB[:, :], -1.0, None, ALU.mult).then_inc(s_ini, 1)
            dve.tensor_copy(identb[:, :], ident).then_inc(s_ini, 1)
            dve.tensor_copy(maskb[:, :], K[:, K_MASK:K_MASK + LB * L]).then_inc(s_ini, 1)
            dve.tensor_tensor(sel4[:, :], K[0:4, K_ID:K_ID + 2], K[0:4, K_ID + 2:K_ID + 4], ALU.add).then_inc(s_cs, 1)
            dve.wait_ge(s_csh, 1)
            dve.tensor_tensor(cst[:, :, 2:4], csil[:, :, :], cst[:, :, 0:2].bitcast(F32), ALU.subtract).then_inc(s_cs, 1)
            dve.memset(csz[:, :, :].bitcast(F32), 0.0).then_inc(s_cs, 1)
            dve.wait_ge(s_cs, 3)
            dve.tensor_copy(csz[:, :, 0:2], cst[:, :, 0:2].bitcast(F32)).then_inc(s_cs, 1)
            for chunk in MODS_FIRST[:2]:
                mod(chunk)
            normalised(0)
            for chunk in MODS_FIRST[2:]:
                mod(chunk)
            column(SC[0], KT, 0, 0, 1.0)
            rope = [0]

            def rotate(t, x, out, heads, done, perm, prior, count):
                w = heads * HD
                if count:
                    dve.wait_ge(prior, count)
                cos = K[:, K_COS + t * HD:K_COS + (t + 1) * HD]
                sin = K[:, K_SIN + t * HD:K_SIN + (t + 1) * HD].rearrange("p (a f r) -> p a f r", a=2, f=2)
                dve.tensor_tensor(rope1[:, 0:w].rearrange("p (h d) -> p h d", h=heads), x.rearrange("p (h d) -> p h d", h=heads),
                                  cos[:, None, :].to_broadcast([P, heads, HD]), ALU.mult).then_inc(s_r, 1)
                x4 = x.rearrange("p (h a f r) -> p h a f r", h=heads, a=2, f=2)
                o4 = rope2[:, 0:w].rearrange("p (h a f r) -> p h a f r", h=heads, a=2, f=2)
                for f in range(2):
                    dve.tensor_tensor(o4[:, :, :, f, :], x4[:, :, :, 1 - f, :],
                                      sin[:, None, :, f, :].to_broadcast([P, heads, 2, HD // 4]), ALU.mult).then_inc(s_r, 1)
                dve.wait_ge(s_r, 3 * rope[0] + 3)
                o = out.rearrange("p (c k d) -> p k c d", k=NKV, d=HD) if perm else out
                r1_, r2_ = rope1[:, 0:w], rope2[:, 0:w]
                if perm:
                    r1_, r2_ = (v.rearrange("p (k c d) -> p k c d", k=NKV, d=HD) for v in (r1_, r2_))
                dve.tensor_tensor(o, r1_, r2_, ALU.add).then_inc(done, 1)
                rope[0] += 1

            for l in range(DEPTH):
                nb, streams = blocks(l), blocks(l) // LB
                build(4 * l, 2 * l, 2, 0)
                if l == 0:
                    split(1)
                n = first[f"q.{l}"]
                ahead(n)
                ahead(n + 1)
                for t in range(nb):
                    dve.wait_ge(s_mm, before[n + 1] + t + 1)
                    if t < LB:
                        rotate(t, bank[t][:, :], qrot[:, t, :], NH, s_qr, True, s_qr, qb0[l] + t)
                    else:
                        dve.tensor_copy(qrot[:, t, :].rearrange("p (c k d) -> p k c d", k=NKV, d=HD),
                                        bank[t][:, :].rearrange("p (k c d) -> p k c d", k=NKV, d=HD)).then_inc(s_qr, 1)
                mod(MODS_BUILD[2 * l][1])
                column(GG[0], 2 * KT, l, 1, 0.0)
                n = first[f"kv.{l}"]
                ahead(n)
                for t in range(2 * LB):
                    dve.wait_ge(s_mm, before[n] + t + 1)
                    if t < LB:
                        rotate(t, bank[t][:, 0:P], krot[:, t, :], NKV, s_kr, False,
                               s_kr if t else s_qr, 4 * l + t if t else qb0[l] + LB)
                    else:
                        dve.tensor_copy(krot[:, t, :], bank[t][:, 0:P]).then_inc(s_kr, 1)
                    dve.tensor_copy(V[:, t, :], bank[t][:, P:2 * P]).then_inc(s_v, 1)
                n = first[f"p.{l}"]
                ahead(n)
                ahead(n + 1)

                units, a0 = units_of(l), att0[l]
                n0 = first[f"g0n0.{l}"]

                def row_max(a):
                    (s, b, h), u = units[a], a0 + a
                    q = slice(u % 2, u % 2 + 1)
                    dve.wait_ge(s_s, u + 1)
                    kw = 2 * L if s == 0 else L
                    dve.tensor_reduce(negmax0[:, q], bank[4 + u % 2][:, 0:kw], AX_X, ALU.max, negate=True).then_inc(s_nm0, 1)
                    dve.wait_ge(s_nm0, u + 1)
                    if u >= 2:
                        dve.wait_ge(s_es, u - 1)
                    dve.tensor_scalar(negmax[:, q], negmax0[:, q], HD ** -0.5, nsink[:, l * NH + h:l * NH + h + 1],
                                      ALU.mult, ALU.min).then_inc(s_nm, 1)

                def denominator(a):
                    u = a0 + a
                    q = slice(u % 2, u % 2 + 1)
                    dve.wait_ge(s_es, u + 1)
                    dve.tensor_tensor(den[:, q], psumP[:, q], esink[:, q], ALU.add).then_inc(s_dn, 1)
                    dve.wait_ge(s_dn, 2 * u + 1)
                    if u >= 2:
                        dve.wait_ge(s_oc, u - 1)
                    dve.reciprocal(rden[:, q], den[:, q]).then_inc(s_dn, 1)

                def att_scaled(a):
                    (s, b, h), u = units[a], a0 + a
                    dve.wait_ge(s_dn, 2 * u + 2)
                    dve.wait_ge(s_pv, u + 1)
                    if h == 0 and u:
                        dve.wait_ge(s_at, u // NH)
                    dve.tensor_scalar(att[:, h * HD:(h + 1) * HD], bank[7][:, h * HD:(h + 1) * HD],
                                      rden[:, u % 2:u % 2 + 1], None, ALU.mult).then_inc(s_oc, 1)

                def att_low(j):
                    T = qb0[l] + j
                    dve.wait_ge(s_ah, T + 1)
                    dve.tensor_tensor(brl[:, :, j * P:(j + 1) * P], bank[7][:, :].rearrange("p (c t) -> p c t", c=QC),
                                      brh[:, :, j * P:(j + 1) * P].bitcast(F32), ALU.subtract).then_inc(s_al, 1)

                for a in range(len(units) + 1):
                    if a < len(units):
                        row_max(a)
                    if a:
                        denominator(a - 1)
                    if a % NH == 1 and a > NH:
                        att_low(a // NH - 1)
                    if a % (2 * nb) == 1 and a < len(units):
                        ahead(n0 + a // (2 * nb))
                    if a:
                        att_scaled(a - 1)
                att_low(nb - 1)
                mid = MODS_MID[l]
                ahead_mod(mid[0])
                for h in range(2):
                    n = first[f"ao{h}.{l}"]
                    ahead(n)
                    dve.wait_ge(s_g0s, (0 if l == 0 else 4) + nb)
                    for t in range(nb):
                        dve.wait_ge(s_mm, before[n] + t + 1)
                        dve.tensor_tensor(A[:, t, h * 512:(h + 1) * 512], bank[t][:, :],
                                          A[:, t, h * 512:(h + 1) * 512], ALU.mult).then_inc(s_ao, 1)
                if mid[0]:
                    mod(mid[0])

                def mix_low(g):
                    dve.wait_ge(s_mxh, NG * l + g + 1)
                    dve.scalar_tensor_tensor(brl[:, g, 0:nb * P], bank[6 + g % 2][:, 0:nb * P],
                                             VT[:, V_PS + l * NG + g:V_PS + l * NG + g + 1],
                                             brh[:, g, 0:nb * P].bitcast(F32), ALU.mult, ALU.subtract).then_inc(s_mxl, 1)

                for g in range(NG):
                    dve.wait_ge(s_pl, NG * l + g + 1)
                    if NG * l + g:
                        dve.wait_ge(s_mx, NG * l + g)
                    dve.tensor_copy(pooledT[:, 0:nb * P], bank[4 + g % 2][:, 0:nb * P]).then_inc(s_plc, 1)
                    if g:
                        mix_low(g - 1)
                mix_low(NG - 1)
                for h in range(2):
                    n = first[f"g1n{h}.{l}"]
                    if h:
                        ahead_mod(mid[2])
                    ahead(n)
                    ahead(n + 1)
                    if h == 0:
                        ahead_mod(mid[1])
                    if h and mid[2]:
                        mod(mid[2])
                    n = first[f"po{h}.{l}"]
                    ahead(n)
                    p0 = (0 if l == 0 else 8) + h * nb
                    for t in range(nb):
                        dve.wait_ge(s_mm, before[n] + t + 1)
                        dve.wait_ge(s_g1, p0 + t + 1)
                        dve.tensor_tensor(pin[:, t, :], bank[t][:, :], pin[:, t, :], ALU.mult).then_inc(s_po, 1)
                        dve.wait_ge(s_po, p0 + t + 1)
                        dve.wait_ge(s_ao, p0 + t + 1)
                        dve.tensor_tensor(A[:, t, h * 512:(h + 1) * 512], A[:, t, h * 512:(h + 1) * 512],
                                          pin[:, t, :], ALU.add).then_inc(s_mg, 1)
                    if h == 0 and mid[1]:
                        mod(mid[1])
                for k in range(KT):
                    dve.wait_ge(s_mgh, KT * l + k + 1)
                    dve.tensor_tensor(hTl[:, k, 0:nb * P], bank[4 + k % 2][:, 0:nb * P],
                                      hTh[:, k, 0:nb * P].bitcast(F32), ALU.subtract).then_inc(s_mgl, 1)
                    if k == 5 and mid[3]:
                        mod(mid[3])
                column(SC[1], 4 * KT, l, 2, 1.0)
                dve.wait_ge(s_col, 4 * l + 2)
                gain_diag(0, streams)
                for h in range(2):
                    n = first[f"o{h}.{l}"]
                    ahead(n)
                    ahead(n + 1)
                    for t in range(nb):
                        dve.wait_ge(s_mm, before[n + 1] + t + 1)
                        dve.tensor_copy(A[:, t, h * 512:(h + 1) * 512], bank[t][:, :]).then_inc(s_y, 1)
                add_normed(4 * l + 1, lambda t: A[:, t, :])
                mod(MODS_GAP[4 * l + 1][0])
                dve.wait_ge(s_xu, xu_at[4 * l + 2])
                normalised(4 * l + 2)
                if l + 1 == DEPTH:
                    dve.wait_ge(s_wr, 1)
                    dve.tensor_tensor(wrs[:, :, 1, :], wr[:, :, :], wrs[:, :, 0, :].bitcast(F32),
                                      ALU.subtract).then_inc(s_wrl, 1)
                build(4 * l + 2, 2 * l + 1, streams, 1)
                column(GG[1], 5 * KT, l, 3, 0.0)
                dve.wait_ge(s_gb, gb_at[4 * l + 1] + streams)
                dve.wait_ge(s_col, 4 * l + 4)
                gain_diag(1, streams)
                if l == 0:
                    mod(MODS_BUILD[1][1])
                    dve.wait_ge(s_tr, 2 * KT)
                    dve.memset(A[:, :, :], 0.0).then_inc(s_da, 1)

                    def add_down(q, f, h, t, src, c):
                        dve.wait_ge(s_mm, before[FN] + 16 + q + 1 + f * 24)
                        dve.tensor_tensor(A[:, t, c:c + 512], A[:, t, c:c + 512], src, ALU.add).then_inc(s_da, 1)

                    with dve.Fori(0, FFULL) as f:
                        def split_f(j):
                            s = (SF + j) % 3
                            dve.wait_ge(s_hi, SF + j + 1 + f * 6)
                            dve.tensor_tensor(wlo[s][:, :], raw[(LF + j - 2) % 3][:, :], whi[s][:, :].bitcast(F32),
                                              ALU.subtract).then_inc(s_lo, 1)

                        def gate_f(t):
                            dve.wait_ge(s_mm, before[FN] + 12 + t + 1 + f * 24)
                            dve.wait_ge(s_si, t + 1 + f * 4)
                            dve.tensor_tensor(sg[:, t, :], bank[t][:, :], sg[:, t, :], ALU.mult).then_inc(s_hid, 1)

                        def low_f(t):
                            dve.wait_ge(s_h2h, t + 1 + f * 4)
                            dve.tensor_tensor(h2l[:, t, :, :].rearrange("p j t -> p (j t)"), bank[4 + t % 2][:, :],
                                              h2h[:, t, :, :].bitcast(F32).rearrange("p j t -> p (j t)"),
                                              ALU.subtract).then_inc(s_h2l, 1)

                        for j in range(4):
                            split_f(j + 2)
                        gate_f(0)
                        gate_f(1)
                        low_f(0)
                        gate_f(2)
                        low_f(1)
                        gate_f(3)
                        split_f(6)
                        low_f(2)
                        for q in range(8):
                            if q == 4:
                                split_f(7)
                            dve.wait_ge(s_da, q + 1 + f * 8)
                            add_down(q, f, q // 4, q % 4, bank[6 + q % 2][:, :], (q // 4) * 512)
                            if q == 0:
                                low_f(3)
                    n = FN + 6 * FFULL
                    ahead(n)
                    ahead(n + 1)

                    def gate_r(t):
                        dve.wait_ge(s_mm, before[n + 1] + t + 1)
                        dve.wait_ge(s_si, 4 * FFULL + t + 1)
                        dve.tensor_tensor(sg[:, t, 0:FREM], bank[t][:, 0:FREM], sg[:, t, 0:FREM],
                                          ALU.mult).then_inc(s_hid, 1)

                    def low_r(t):
                        dve.wait_ge(s_h2h, 4 * FFULL + t + 1)
                        dve.tensor_tensor(h2l[:, t, 0:FREM // P, :].rearrange("p j t -> p (j t)"),
                                          bank[4 + t % 2][:, 0:FREM],
                                          h2h[:, t, 0:FREM // P, :].bitcast(F32).rearrange("p j t -> p (j t)"),
                                          ALU.subtract).then_inc(s_h2l, 1)

                    def add_r(q):
                        dve.wait_ge(s_mm, before[n + 2] + q + 1)
                        dve.wait_ge(s_da, 8 * FFULL + q + 1)
                        dve.tensor_tensor(A[:, q // 2, (q % 2) * 512:(q % 2 + 1) * 512],
                                          A[:, q // 2, (q % 2) * 512:(q % 2 + 1) * 512], bank[6 + q % 2][:, :],
                                          ALU.add).then_inc(s_da, 1)

                    gate_r(0)
                    low_r(0)
                    gate_r(1)
                    low_r(1)
                    gate_r(2)
                    gate_r(3)
                    for q in range(8):
                        add_r(q)
                        if q in (1, 3):
                            low_r(q // 2 + 2)
                        if q == 3:
                            ahead(n + 2)
                    add_normed(3, lambda t: A[:, t, :])
                    mod(MODS_GAP[3][0])
                    dve.wait_ge(s_xu, xu_at[4])
                    normalised(4)

            def split_x(E, j, f):
                dve.wait_ge(s_hi, SN + j + 1 + E * XU + f * 6)
                dve.tensor_tensor(wlo[j % 3][:, :], rawm[j][:, :], whi[j % 3][:, :].bitcast(F32),
                                  ALU.subtract).then_inc(s_lo, 1)

            step = [0]

            def R(c, w=LB * NE):
                return route[:, c:c + w]

            def R3(c):
                return route[:, c:c + LB * NE].rearrange("p (b e) -> p b e", b=LB)

            def did(ins):
                step[0] += 1
                ins.then_inc(s_rt, 1)
                dve.wait_ge(s_rt, step[0])

            def columns_of(src, e, out):
                v = src.rearrange("p (b e) -> p b e", b=LB)
                return dve.tensor_copy(out, v[:, :, e:e + 1] if isinstance(e, int) else v[:, :, bass.ds(e, 1)])

            def gather_matrix(b, e, E):
                columns_of(R(POSM), e, route[:, CURG:CURG + LB, None]).then_inc(s_cur, 1)
                dve.wait_ge(s_cur, E * 3 + 1)
                for t in range(LB):
                    dve.tensor_scalar(Gat[:, t, :], K[:, K_IO:K_IO + P], float(b * P), route[:, CURG + t:CURG + t + 1],
                                      ALU.add, ALU.is_equal).then_inc(s_gat, 1)

            dve.memset(yacc[:, :, :], 0.0).then_inc(s_sca, 1)
            split_x(0, 0, 0)
            split_x(0, 1, 0)
            dve.wait_ge(s_lg, 1)
            halves = bank[0][:, 0:2 * LB * NE].rearrange("p (b h e) -> p b h e", b=LB, h=2)
            did(dve.tensor_tensor(R3(LG), halves[:, :, 0, :], brB[:, None, :].to_broadcast([P, LB, NE]), ALU.add))
            did(dve.tensor_tensor(R3(LG), halves[:, :, 1, :], R3(LG), ALU.add))
            for b in range(LB):
                did(dve.max(route[:, M8 + 8 * b:M8 + 8 * b + 8], route[:, LG + NE * b:LG + NE * (b + 1)]))
            did(dve.tensor_tensor(R(DIF, LB), route[:, M8 + 1:M8 + 10:8], route[:, M8:M8 + 9:8], ALU.subtract))
            assert step[0] == R_DIF
            lj = R3(LG)[:, :, None, :].to_broadcast([P, LB, NE, NE])
            li = R3(LG)[:, :, :, None].to_broadcast([P, LB, NE, NE])
            t1, t2 = (route[:, c:c + LB * NE * NE].rearrange("p (b e j) -> p b e j", b=LB, e=NE) for c in (T1, T2))
            lower = K[:, K_JLT:K_JLT + NE * NE].rearrange("p (e j) -> p e j", e=NE)
            did(dve.tensor_tensor(t1, lj, li, ALU.is_gt))
            did(dve.tensor_tensor(t2, lj, li, ALU.is_equal))
            did(dve.tensor_tensor(t2, t2, lower[:, None, :, :].to_broadcast([P, LB, NE, NE]), ALU.mult))
            did(dve.tensor_tensor(t1, t1, t2, ALU.add))
            did(dve.tensor_reduce(R3(RK), t1, AX_X, ALU.add))
            did(dve.tensor_scalar(R(F1), R(RK), 0.0, None, ALU.is_equal))
            did(dve.tensor_scalar(R(F2), R(RK), 1.0, None, ALU.is_equal))
            did(dve.tensor_tensor(R(SEL), R(F1), R(F2), ALU.add))
            assert step[0] == R_SEL
            dve.wait_ge(s_rx, 1)
            did(dve.tensor_scalar(R(DNR, LB), R(EXD, LB), 1.0, None, ALU.add))
            did(dve.reciprocal(R(W1, LB), R(DNR, LB)))
            did(dve.tensor_tensor(R(W2, LB), R(EXD, LB), R(W1, LB), ALU.mult))
            for f, w in ((F1, W1), (F2, W2)):
                did(dve.tensor_tensor(R3(f), R3(f), route[:, w:w + LB, None].to_broadcast([P, LB, NE]), ALU.mult))
            did(dve.tensor_tensor(R(CW), R(F1), R(F2), ALU.add))
            dve.wait_ge(s_cnt, 1)
            did(dve.scalar_tensor_tensor(R(POS), bank[1][:, 0:LB * NE], 1.0, R(SEL), ALU.add, ALU.mult))
            did(dve.tensor_scalar(R(POSM), R(POS), -1.0, None, ALU.add))
            gather_matrix(0, 0, 0)
            did(dve.tensor_reduce(R(CNT, 1), bank[1][:, LB * NE:LB * NE + NE], AX_X, ALU.max))
            dve.tensor_scalar(R(FLAG, 1).bitcast(I32), R(CNT, 1), float(P), None, ALU.is_gt).then_inc(s_flag, 1)
            dve.wait_ge(s_flag, 1)

            def gathered_low(E):
                for half in range(2):
                    ks = slice(half * KT // 2, (half + 1) * KT // 2)
                    dve.wait_ge(s_xgh, 2 * E + half + 1)
                    dve.tensor_tensor(xgl[:, ks, :].rearrange("p k t -> p (k t)"),
                                      xgm[:, ks, :].rearrange("p k t -> p (k t)"),
                                      xgh[:, ks, :].bitcast(F32).rearrange("p k t -> p (k t)"),
                                      ALU.subtract).then_inc(s_xgl, 1)

            def gate_x(E, f, up):
                dve.wait_ge(s_mm, up)
                dve.wait_ge(s_si, H0 + 1 + E * XS + f)
                dve.tensor_tensor(sgm[:, :], bank[1][:, :], sgm[:, :], ALU.mult).then_inc(s_hid, 1)

            def low_x(E, f):
                dve.wait_ge(s_h2h, H0 + 1 + E * XS + f)
                dve.tensor_tensor(h2lm[:, :, :].rearrange("p j t -> p (j t)"), bank[4][:, :],
                                  h2hm[:, :, :].bitcast(F32).rearrange("p j t -> p (j t)"),
                                  ALU.subtract).then_inc(s_h2l, 1)

            def scatter_matrix(b, e, E):
                columns_of(R(POSM), e, route[:, CURS:CURS + LB, None]).then_inc(s_cur, 1)
                columns_of(R(CW), e, route[:, CURW:CURW + LB, None]).then_inc(s_cur, 1)
                dve.wait_ge(s_cur, 3 + E * 3)
                for t in range(LB):
                    dve.tensor_scalar(Gsc[:, t, :], K[:, K_IO:K_IO + P], float(b * P), route[:, CURS + t:CURS + t + 1],
                                      ALU.add, ALU.is_equal).then_inc(s_gsc, 1)
                    dve.wait_ge(s_gsc, 2 * t + 1 + E * 4)
                    dve.tensor_scalar(Gsc[:, t, :], Gsc[:, t, :], route[:, CURW + t:CURW + t + 1], None,
                                      ALU.mult).then_inc(s_gsc, 1)

            def add_output(E, q):
                dve.wait_ge(s_sc, q + 1 + E * 4)
                t, h = q // 2, q % 2
                dve.tensor_tensor(yacc[:, t, h * 512:(h + 1) * 512], yacc[:, t, h * 512:(h + 1) * 512],
                                  bank[2 + q % 2][:, :], ALU.add).then_inc(s_sca, 1)
                if q == 2 * LB - 1:
                    dve.wait_ge(s_sca, 5 + E * 4)

            def slice_(E, f, low=None, out=None, last=False):
                for j in range(6):
                    split_x(E, j, f)
                    if out is not None and j == 1:
                        add_output(out, 0)
                        add_output(out, 1)
                    if j == 3:
                        gate_x(E, f, GM + 2 + E * XU + f * 6)
                        if low is not None:
                            gathered_low(low)
                        if out is not None:
                            add_output(out, 2)
                            add_output(out, 3)
                    if j == 4 and last:
                        low_x(E, f)
                if not last:
                    low_x(E, f)

            def expert(b, e, last):
                E = e + b * NE
                scatter_matrix(b, e, E)
                if not last:
                    gather_matrix(b, e + 1, E + 1)
                slice_(E, 2)
                with dve.Fori(3, XS - 1) as f:
                    slice_(E, f)
                slice_(E, XS - 1, None if last else E + 1, last=last)
                if last:
                    for q in range(2 * LB):
                        add_output(E, q)
                else:
                    slice_(E, XS)
                    slice_(E, XS + 1, out=E)

            def expert_pass(b):
                E = b * NE
                if b:
                    gather_matrix(b, 0, E)
                gathered_low(E)
                for j in range(2, 6):
                    split_x(E, j, 0)
                gate_x(E, 0, GM + 4 + E * XU)
                low_x(E, 0)
                slice_(E, 1)
                with dve.Fori(0, NE - 1) as e:
                    expert(b, e, False)
                expert(b, NE - 1, True)

            expert_pass(0)
            with dve.If(dve.value_load(route[0:1, FLAG:FLAG + 1].bitcast(I32), min_val=0, max_val=1) > 0):
                split_x(NE, 0, 0)
                split_x(NE, 1, 0)
                expert_pass(1)
            dve.memset(den[:, :], 0.0).then_inc(s_moe, 1)
            add_normed(7, lambda t: yacc[:, t, :])

        @block.tensor
        def _(pe):
            def product(out, hi, lo, wh, wl, start, stop):
                pe.matmul(out, hi, wh, start=start, stop=False)
                pe.matmul(out, hi, wl, start=False, stop=False)
                return pe.matmul(out, lo, wh, start=False, stop=stop)

            def group(slot, rows, width, out, hi, lo, start, stop, col=0, w=None, part=None):
                w = w or width
                for j in range(rows) if part is None else range(part * rows // 2, (part + 1) * rows // 2):
                    c = j * width + col
                    mm = product(out, hi(j), lo(j), whi[slot][:, c:c + w], wlo[slot][:, c:c + w],
                                 start and j == 0, stop and j == rows - 1)
                if part != 0:
                    mm.then_inc(s_mm, 1)

            def hT(k0, t):
                return ((lambda j: hTh[:, k0 + j, t * P:(t + 1) * P]), (lambda j: hTl[:, k0 + j, t * P:(t + 1) * P]))

            def project(n, nb, free=None, tiles=None):
                rows = plan[n][2]
                npieces = KT // rows
                for i in range(npieces):
                    s = split_of[n + i]
                    pe.wait_ge(s_lo, s + 1)
                    if tiles:
                        tiles(rows * (i + 1))
                    for t in range(nb):
                        if i == 0 and free:
                            free(t)
                        hi, lo = hT(rows * i, t)
                        group(s % 3, rows, plan[n][3], bank[t][:, 0:plan[n][3]], hi, lo, i == 0, i == npieces - 1)

            def mod_piece(chunk, i):
                l, m = chunk
                n, M = first[f"m{m}.{l}"] + i, MCH * l + m
                if i == 0 and M >= 2:
                    pe.wait_ge(s_md, M - 1)
                if chunk in MODS_SPLIT:
                    w = split_of[n]
                    pe.wait_ge(s_cs, 4)
                    pe.wait_ge(s_lo, w + 1)
                    for j in range(4):
                        c = slice(j * 512, (j + 1) * 512)
                        pe.matmul(mod_bank(M)[0:4, :], cst[:, 4 * i + j, :], whi[w % 3][:, c], start=i + j == 0, stop=False)
                        mm = pe.matmul(mod_bank(M)[0:4, :], csz[:, 4 * i + j, :], wlo[w % 3][:, c],
                                       start=False, stop=4 * i + j == KT - 1)
                    mm.then_inc(s_mm, 1)
                    return
                r = load_of[n]
                pe.wait_ge(s_raw[r % 3], 16 * (r // 3 + 1))
                for j in range(4):
                    mm = pe.matmul(mod_bank(M)[0:2, :], csil[:, 4 * i + j, :], raw[r % 3][:, j * 512:(j + 1) * 512],
                                   start=i + j == 0, stop=4 * i + j == KT - 1)
                mm.then_inc(s_mm, 1)

            def mod_rows(chunk):
                mod_piece(chunk, 0)
                mod_piece(chunk, 1)

            def mod_t(chunk):
                M = MCH * chunk[0] + chunk[1]
                pe.wait_ge(s_mrow, M + 1)
                for j in range(4):
                    if chunk in MODS_SPLIT:
                        mm = pe.matmul(mod_bank(M)[:, 2 * j:2 * j + 2], modrow[0:4, M % 2, j * P:(j + 1) * P], sel4[:, :],
                                       start=True, stop=True)
                    else:
                        mm = pe.transpose(mod_bank(M)[:, 2 * j:2 * j + 2], modrow[0:2, M % 2, j * P:(j + 1) * P],
                                          ident[0:2, 0:2])
                mm.then_inc(s_mt, 1)

            def mod_run(chunks):
                for j, chunk in enumerate(chunks):
                    mod_piece(chunk, 0)
                    if j:
                        mod_t(chunks[j - 1])
                    mod_piece(chunk, 1)

            def build(i, bi):
                gap, inside = MODS_GAP.get(i - 1, []), MODS_BUILD[bi]
                for k in range(KT):
                    if k >= 2:
                        pe.wait_ge(s_hm, hm_at[bi] + (norm_nb[i] // LB) * (k - 1))
                    for t in range(norm_nb[i]):
                        if k == 0:
                            pe.wait_ge(s_xn, xn_at[i] + t + 1)
                        mm = pe.transpose(bank[4 + k % 2][:, t * P:(t + 1) * P], A[:, t, k * P:(k + 1) * P], ident)
                    mm.then_inc(s_tr, 1)
                    if inside and k % 2:
                        if k == 1 and gap:
                            mod_t(gap[-1])
                        if k == 5:
                            mod_t(inside[0])
                        mod_piece(inside[k // 4], k // 2 % 2)
                if gap and not inside:
                    mod_t(gap[-1])

            def gain_rows(i, streams):
                for s in range(streams):
                    pe.wait_ge(s_dg, gb_at[i] + s + 1)
                    for k in range(KT):
                        mm = pe.matmul(bank[4 + 2 * s + k // 4][:, (k % 4) * P:(k % 4 + 1) * P], ones[:, :],
                                       diag[:, s, k, :], start=True, stop=True)
                    mm.then_inc(s_gb, 1)

            pe.wait_ge(s_const, 16)
            pe.wait_ge(s_small, 80)
            pe.transpose(bank[4][:, 0:V_BM], vst[0:V_BM, 0, :], ident[0:V_BM, 0:V_BM]).then_inc(s_vt, 1)
            pe.transpose(bank[5][:, 0:V_ALL - V_BM], vst[0:V_ALL - V_BM, 1, :],
                         ident[0:V_ALL - V_BM, 0:V_ALL - V_BM]).then_inc(s_vt, 1)
            pe.wait_ge(s_csil, 1)
            pe.wait_ge(s_ini, 5)
            mod_run(MODS_FIRST)
            mod_t(MODS_FIRST[-1])
            for l in range(DEPTH):
                nb, streams = blocks(l), blocks(l) // LB
                a0 = att0[l]
                build(4 * l, 2 * l)
                if l:
                    pe.wait_ge(s_md, MCH + 8)
                project(first[f"q.{l}"], nb, tiles=lambda k: pe.wait_ge(s_h, KT * 2 * l + k))
                mod_t(MODS_BUILD[2 * l][1])
                project(first[f"kv.{l}"], 2 * LB,
                        lambda t: pe.wait_ge(s_qr, qb0[l] + min(t, nb - 1) + 1))
                for t in range(nb):
                    pe.wait_ge(s_qr, qb0[l] + t + 1)
                    if t >= 2:
                        pe.wait_ge(s_qk, qb0[l] + l + t - 1)
                    for c in range(QC):
                        mm = pe.transpose(bank[4 + t % 2][:, c * P:(c + 1) * P], qrot[:, t, c * P:(c + 1) * P], ident)
                    mm.then_inc(s_qt, 1)
                pe.wait_ge(s_kr, 4 * (l + 1))
                pe.wait_ge(s_qk, qb0[l] + l + nb)
                for t in range(2 * LB):
                    mm = pe.transpose(bank[4][:, t * P:(t + 1) * P], krot[:, t, :], ident)
                mm.then_inc(s_kt, 1)
                project(first[f"p.{l}"], nb, lambda t: pe.wait_ge(s_v, 4 * l + t + 1))

                units = units_of(l)
                n0 = first[f"g0n0.{l}"]

                def scores(a):
                    (s, b, h), u = units[a], a0 + a
                    if a == 0:
                        pe.wait_ge(s_qk, qb0[l] + l + nb + 1)
                        last = MODS_BUILD[2 * l][1]
                        pe.wait_ge(s_md, MCH * last[0] + last[1] + 1)
                    if u >= 2:
                        pe.wait_ge(s_e, u - 1)
                    g, cc = h // QC, h % QC
                    k0, kw = (0, 2 * L) if s == 0 else (L, L)
                    mm = pe.matmul(bank[4 + u % 2][:, 0:kw],
                                   qT[g * HD:(g + 1) * HD, cc, (s * LB + b) * P:(s * LB + b + 1) * P],
                                   kT[g * HD:(g + 1) * HD, k0:k0 + kw], start=True, stop=s == 1)
                    if s == 0:
                        mm = pe.matmul(bank[4 + u % 2][:, 0:L], identb[:, :], maskb[:, b * L:(b + 1) * L],
                                       start=False, stop=True)
                    mm.then_inc(s_s, 1)

                def probs_t(a):
                    (s, _, _), u = units[a], a0 + a
                    pe.wait_ge(s_e, u + 1)
                    if u:
                        pe.wait_ge(s_ptc, u)
                    for kb in range(4 if s == 0 else 2):
                        mm = pe.transpose(bank[6][:, kb * P:(kb + 1) * P], Pb[:, u % 2, kb * P:(kb + 1) * P], ident)
                    mm.then_inc(s_pt, 1)

                def values(a):
                    (s, b, h), u = units[a], a0 + a
                    pe.wait_ge(s_ptc, u + 1)
                    if u:
                        pe.wait_ge(s_oc, u)
                    if h == 0 and u:
                        pe.wait_ge(s_al, u // NH)
                    g = h // QC
                    kbs = range(4) if s == 0 else range(2)
                    for kb in kbs:
                        mm = pe.matmul(bank[7][:, h * HD:(h + 1) * HD], PT[:, a % 2, kb, :],
                                       V[:, (0 if s == 0 else LB) + kb, g * HD:(g + 1) * HD],
                                       start=kb == 0, stop=kb == kbs[-1])
                    mm.then_inc(s_pv, 1)

                def att_t(j):
                    T = qb0[l] + j
                    pe.wait_ge(s_oc, NH * (T + 1))
                    for cc in range(QC):
                        mm = pe.transpose(bank[7][:, cc * P:(cc + 1) * P], att[:, cc * P:(cc + 1) * P], ident)
                    mm.then_inc(s_at, 1)

                def filler(g, part):
                    n, t = n0 + g // nb, g % nb
                    if t == 0 and part == 0:
                        pe.wait_ge(s_lo, split_of[n] + 1)
                    half, i = g // (2 * nb), (g // nb) % 2
                    if i == 0 and half == 0 and part == 0:
                        pe.wait_ge(s_pin, qb0[l] + t + 1)
                    if i == 0 and half == 1 and part == 0:
                        pe.wait_ge(s_g0, (0 if l == 0 else 8) + t + 1)
                    hi, lo = hT(4 * i, t)
                    group(split_of[n] % 3, 4, 512, bank[t][:, :], hi, lo, i == 0, i == 1, part=part)

                for a in range(len(units) + 1):
                    if a < len(units):
                        scores(a)
                    if a:
                        probs_t(a - 1)
                    if a % NH == 1 and a > NH:
                        att_t(a // NH - 1)
                    if a < len(units):
                        filler(a // 2, a % 2)
                    if a:
                        values(a - 1)
                att_t(nb - 1)

                def br(j, t):
                    return brh[:, j, t * P:(t + 1) * P], brl[:, j, t * P:(t + 1) * P]

                g0 = 0 if l == 0 else 8

                def branch(n, free):
                    pe.wait_ge(s_lo, split_of[n] + 1)
                    for t in range(nb):
                        free(t)
                        group(split_of[n] % 3, 4, 512, bank[t][:, :], lambda j: br(j, t)[0], lambda j: br(j, t)[1], True, True)

                mid = MODS_MID[l]
                if mid[0]:
                    mod_rows(mid[0])
                pe.wait_ge(s_al, qb0[l] + nb)
                branch(first[f"ao0.{l}"], lambda t: pe.wait_ge(s_g0, g0 + nb + t + 1))
                branch(first[f"ao1.{l}"], lambda t: pe.wait_ge(s_ao, g0 + t + 1))
                if mid[0]:
                    mod_t(mid[0])

                def pooled(g):
                    if g >= 2:
                        pe.wait_ge(s_plc, NG * l + g - 1)
                    for s in range(streams):
                        for b in range(LB):
                            mm = pe.matmul(bank[4 + g % 2][:, s * L:(s + 1) * L], pin[:, s * LB + b, g * P:(g + 1) * P],
                                           poolM[:, b, g, :], start=b == 0, stop=b == LB - 1)
                    mm.then_inc(s_pl, 1)

                def mixed(g):
                    pe.wait_ge(s_plc, NG * l + g + 1)
                    if g < 2:
                        if mid[0]:
                            pe.wait_ge(s_md, mid[0][1] + 1)
                    else:
                        pe.wait_ge(s_mxl, NG * l + g - 1)
                    pe.matmul(bank[6 + g % 2][:, 0:nb * P], poolW[:, g, :], pooledT[:, 0:nb * P],
                              start=True, stop=True).then_inc(s_mx, 1)

                pe.wait_ge(s_pin, qb0[l] + nb)
                pe.wait_ge(s_poolw, 16 * (l + 1))
                pe.wait_ge(s_poolm, 16)
                pooled(0)
                for g in range(NG):
                    if g + 1 < NG:
                        pooled(g + 1)
                    mixed(g)
                for h in range(2):
                    free = ((lambda t: pe.wait_ge(s_ao, g0 + nb + t + 1)) if h == 0 else
                            (lambda t: pe.wait_ge(s_po, g0 + t + 1)))
                    project(first[f"g1n{h}.{l}"], nb, free)
                    if h == 0:
                        pe.wait_ge(s_mxl, NG * (l + 1))
                    if h and mid[2]:
                        mod_t(mid[2])
                    if h == 0 and mid[1]:
                        mod_rows(mid[1])
                    branch(first[f"po{h}.{l}"], lambda t: pe.wait_ge(s_g1, g0 + h * nb + t + 1))
                    if h == 0 and mid[1]:
                        mod_t(mid[1])
                    if h == 0 and mid[2]:
                        mod_rows(mid[2])
                for k in range(KT):
                    if k >= 2:
                        pe.wait_ge(s_mgl, KT * l + k - 1)
                    for t in range(nb):
                        if k in (0, 4):
                            pe.wait_ge(s_mg, g0 + (k // 4) * nb + t + 1)
                        mm = pe.transpose(bank[4 + k % 2][:, t * P:(t + 1) * P], A[:, t, k * P:(k + 1) * P], ident)
                    mm.then_inc(s_mgt, 1)
                    if mid[3] and k in (1, 3):
                        mod_piece(mid[3], k // 2)
                    if mid[3] and k == 5:
                        mod_t(mid[3])
                project(first[f"o0.{l}"], nb, tiles=lambda k: pe.wait_ge(s_mgl, KT * l + k))
                project(first[f"o1.{l}"], nb, lambda t: pe.wait_ge(s_y, g0 + t + 1))
                if mid[3]:
                    pe.wait_ge(s_md, mid[3][1] + 1)
                gain_rows(4 * l + 1, streams)
                pe.wait_ge(s_y, g0 + 2 * nb)
                mod_run(MODS_GAP[4 * l + 1])
                pe.wait_ge(s_ys, 2 * xu_at[4 * l + 2])
                build(4 * l + 2, 2 * l + 1)
                if l == 0:
                    mod_t(MODS_BUILD[1][1])
                    pe.wait_ge(s_md, MCH + 4)

                    def hidden_t(t, f, tiles):
                        pe.wait_ge(s_hid, t + 1 + f * 4)
                        if t >= 2:
                            pe.wait_ge(s_h2l, t - 1 + f * 4)
                        for j in range(tiles):
                            mm = pe.transpose(bank[4 + t % 2][:, j * P:(j + 1) * P], sg[:, t, j * P:(j + 1) * P], ident)
                        mm.then_inc(s_ht, 1)

                    def h2(t):
                        return (lambda j: h2h[:, t, j, :]), (lambda j: h2l[:, t, j, :])

                    with pe.Fori(0, FFULL) as f:
                        for j in range(4):
                            pe.wait_ge(s_lo, SF + j + 1 + f * 6)
                            if j < 2:
                                pe.wait_ge(s_h, KT + 4 * (j + 1))
                            for t in range(4):
                                if j == 2:
                                    pe.wait_ge(s_si, t + 1 + f * 4)
                                if j == 3 and t == 2:
                                    hidden_t(0, f, 4)
                                if j == 3 and t == 3:
                                    hidden_t(1, f, 4)
                                hi, lo = hT(4 * (j % 2), t)
                                group((SF + j) % 3, 4, 512, bank[t][:, :], hi, lo, j % 2 == 0, j % 2 == 1)
                        for h in range(2):
                            pe.wait_ge(s_lo, SF + 4 + h + 1 + f * 6)
                            for t in range(4):
                                q = 4 * h + t
                                if h == 0:
                                    pe.wait_ge(s_h2l, t + 1 + f * 4)
                                pe.wait_ge(s_da, (q if q >= 2 else 1) + f * 8)
                                hi, lo = h2(t)
                                group((SF + 4 + h) % 3, 4, 512, bank[6 + q % 2][:, :], hi, lo, True, True)
                                if h == 0 and t < 2:
                                    hidden_t(2 + t, f, 4)
                    n = FN + 6 * FFULL
                    project(n, 4)

                    def free(t):
                        pe.wait_ge(s_si, 4 * FFULL + t + 1)
                        if t >= 2:
                            hidden_t(t - 2, FFULL, FREM // P)

                    project(n + 1, 4, free)
                    pe.wait_ge(s_lo, split_of[n + 2] + 1)
                    for q in range(8):
                        t, h = q // 2, q % 2
                        if q in (2, 4):
                            hidden_t(q // 2 + 1, FFULL, FREM // P)
                        pe.wait_ge(s_h2l, 4 * FFULL + t + 1)
                        pe.wait_ge(s_da, 8 * FFULL + max(q, 1))
                        hi, lo = h2(t)
                        group(split_of[n + 2] % 3, FREM // P, D, bank[6 + q % 2][:, :], hi, lo, True, True, col=h * 512, w=512)
                    pe.wait_ge(s_h2l, H0)
                    pe.wait_ge(s_da, 8 * FFULL + 9)
                    gain_rows(3, streams)
                    mod_run(MODS_GAP[3])
                    pe.wait_ge(s_ys, 16)

            pe.wait_ge(s_wrl, 1)
            pe.wait_ge(s_h, KT * 2 * DEPTH)
            pe.wait_ge(s_md, MCH * DEPTH)
            for b in range(LB):
                for k in range(KT):
                    for x in (hTh, hTl):
                        mm = pe.matmul(bank[0][:, 2 * b * NE:2 * (b + 1) * NE], x[:, k, b * P:(b + 1) * P],
                                       wrs[:, k, :, :].rearrange("p h e -> p (h e)"),
                                       start=k == 0 and x is hTh, stop=k == KT - 1 and x is hTl)
            mm.then_inc(s_lg, 1)
            pe.wait_ge(s_rt, R_SEL)
            tri = K[:, K_TRI:K_TRI + P]
            s0, s1 = route[:, SEL:SEL + NE], route[:, SEL + NE:SEL + 2 * NE]
            pe.matmul(bank[1][:, 0:NE], tri, s0, start=True, stop=True)
            pe.matmul(bank[1][:, NE:2 * NE], tri, s1, start=True, stop=False)
            pe.matmul(bank[1][:, NE:2 * NE], ones[:, :], s0, start=False, stop=True)
            pe.matmul(bank[1][:, 2 * NE:3 * NE], ones[:, :], s0, start=True, stop=False)
            pe.matmul(bank[1][:, 2 * NE:3 * NE], ones[:, :], s1, start=False, stop=True).then_inc(s_cnt, 1)

            def gather(E, added):
                pe.wait_ge(s_gat, 2 + E * 2)
                pe.wait_ge(s_sca, added)
                for k in range(KT):
                    for t in range(LB):
                        mm = pe.matmul(bank[2 + k // 4][:, (k % 4) * P:(k % 4 + 1) * P], A[:, t, k * P:(k + 1) * P],
                                       Gat[:, t, :], start=t == 0, stop=t == LB - 1)
                    if k % 4 == 3:
                        mm.then_inc(s_xg, 1)

            def gate_up(E, f, p0, between=None, tokens=None):
                for j in range(4):
                    pe.wait_ge(s_lo, SN + p0 + j + 1 + E * XU + f * 6)
                    k0 = 4 * (j % 2)
                    if tokens is not None and j < 2:
                        pe.wait_ge(s_xgl, 2 * tokens + j + 1)
                    group((p0 + j) % 3, 4, 512, bank[j // 2][:, :], lambda i: xgh[:, k0 + i, :],
                          lambda i: xgl[:, k0 + i, :], j % 2 == 0, j % 2 == 1)
                    if between:
                        between(j)

            def hidden_t(E, f):
                pe.wait_ge(s_hid, H0 + 1 + E * XS + f)
                for j in range(4):
                    mm = pe.transpose(bank[4][:, j * P:(j + 1) * P], sgm[:, j * P:(j + 1) * P], ident)
                mm.then_inc(s_ht, 1)

            def down(E, f, p0, start, stop):
                for h in range(2):
                    pe.wait_ge(s_lo, SN + p0 + h + 1 + E * XU + f * 6)
                    if h == 0:
                        pe.wait_ge(s_h2l, H0 + E * XS + f)
                    group((p0 + h) % 3, 4, 512, bank[6 + h][:, :],
                          lambda i: h2hm[:, i, :], lambda i: h2lm[:, i, :], start, stop)

            def slice_(E, f):
                gate_up(E, f, -2)
                down(E, f, 2, False, False)
                hidden_t(E, f)

            def scatter(E, q):
                t, h = q // 2, q % 2
                pe.wait_ge(s_sca, (q if q >= 2 else 1) + E * 4)
                pe.matmul(bank[2 + q % 2][:, :], Sct[:, t * P:(t + 1) * P], yslot[:, h * 512:(h + 1) * 512],
                          start=True, stop=True).then_inc(s_sc, 1)

            def expert(b, e, last):
                E = e + b * NE
                slice_(E, 2)
                pe.wait_ge(s_gsc, 4 + E * 4)
                for t in range(LB):
                    mm = pe.transpose(bank[5][:, t * P:(t + 1) * P], Gsc[:, t, :], ident)
                mm.then_inc(s_gst, 1)
                if not last:
                    gather(E + 1, 1 + E * 4)
                with pe.Fori(3, XS) as f:
                    slice_(E, f)
                if last:
                    down(E, XS, -2, False, True)
                    pe.wait_ge(s_gsc2, E + 1)
                    pe.wait_ge(s_ysl, 2 + E * 2)
                    for q in range(2 * LB):
                        scatter(E, q)
                else:
                    gate_up(E, XS, -2, tokens=E + 1)
                    down(E, XS, 2, False, True)
                    hidden_t(E, XS)

                    def between(j):
                        if j == 1:
                            pe.wait_ge(s_gsc2, E + 1)
                            pe.wait_ge(s_ysl, 2 + E * 2)
                            pe.wait_ge(s_xgm, KT * 2 + E * KT)
                            scatter(E, 0)
                            scatter(E, 1)
                        if j == 3:
                            scatter(E, 2)
                            scatter(E, 3)

                    gate_up(E, XS + 1, -2, between)
                    down(E, XS + 1, 2, True, False)
                    hidden_t(E, XS + 1)

            def expert_pass(b):
                E = b * NE
                gather(E, 1 + b * NE * 4)
                gate_up(E, 0, 0, tokens=E)
                hidden_t(E, 0)
                gate_up(E, 1, -2)
                down(E, 1, 2, True, False)
                hidden_t(E, 1)
                with pe.Fori(0, NE - 1) as e:
                    expert(b, e, False)
                expert(b, NE - 1, True)

            expert_pass(0)
            pe.wait_ge(s_flag, 1)
            with pe.If(pe.value_load(route[0:1, FLAG:FLAG + 1].bitcast(I32), min_val=0, max_val=1) > 0):
                expert_pass(1)
            pe.wait_ge(s_h2l, H0 + XS * NE)
            gain_rows(7, 1)


_INS = ["x", "c", "ctx", "c_ctx", "w_mod", "b_mod", "norm_g", "w_in", "sinks", "w_att_o", "pool_w", "pool_scale",
        "w_pool_o", "w_out", "w_ffn_gate", "w_ffn_up", "w_ffn_down", "w_router", "b_router",
        "w_exp_gate", "w_exp_up", "w_exp_down"]


def kernel(**inputs):
    import numpy as _np
    import concourse.bacc as _bacc
    from concourse import mybir as _mybir
    from concourse.bass_utils import run_bass_kernel_spmd as _run

    nc = _bacc.Bacc("TRN2", target_bir_lowering=False, num_devices=1)
    k_const, k_pool = constants()
    given = {name: inputs[name] for name in _INS}
    given.update(k_const=k_const, k_pool=k_pool)
    arrays, args = {}, []
    for name, a in given.items():
        a = _np.ascontiguousarray(a)
        arrays[f"in_{name}_dram"] = a
        args.append(nc.dram_tensor(f"in_{name}_dram", a.shape, _mybir.dt.from_np(a.dtype), kind="ExternalInput").ap())
    args.append(nc.dram_tensor("out_0_dram", (1, L, D), _mybir.dt.float32, kind="ExternalOutput").ap())
    backbone(nc, *args)
    r = _run(nc, [arrays], core_ids=[0])
    return r.results[0]["out_0_dram"]
```
